# Optimizing a Trainium2 kernel written in Bass

```python
import math
import jax, jax.numpy as jnp
from jax import lax
import numpy as np

D_MODEL = 1024
BATCH = 1
SEQ = 512
DEPTH = 1

MIX_WIDTH = D_MODEL
ATTN_WIDTH = D_MODEL // 2
GDN_WIDTH = MIX_WIDTH - ATTN_WIDTH
DIFF_HEAD_DIM = 128
DIFF_QK_DIM = DIFF_HEAD_DIM // 2
DIFF_HEADS = ATTN_WIDTH // DIFF_HEAD_DIM
ATTN_BLOCK = 128
GDN_HEAD_DIM = 128
GDN_HEADS = GDN_WIDTH // GDN_HEAD_DIM
CONV_WIDTH = 4
GDN_CHUNK = 64
IN_COLS = 3 * ATTN_WIDTH + 4 * GDN_WIDTH + 2 * GDN_HEADS
N_KEYS = 128
N_EXPERTS = N_KEYS * N_KEYS
PEER_HEADS = 8
PEER_TOPK = 16
PEER_KEY_DIM = 256
PEER_HALF = PEER_KEY_DIM // 2
PEER_BLOCK = 128
MOD_CHUNKS = 6
NORM_EPS = 1e-6
NEG_INF = -1e30

kernel_name = "hymba_diffattn_gdn_peer_layer"

def rms_norm(x, gain):
    xf = x.astype(jnp.float32)
    y = xf * lax.rsqrt(jnp.mean(xf * xf, axis=-1, keepdims=True) + NORM_EPS)
    return (y * gain.astype(jnp.float32)).astype(x.dtype)

def l2_norm(x):
    xf = x.astype(jnp.float32)
    return (xf * lax.rsqrt(jnp.sum(xf * xf, axis=-1, keepdims=True) + NORM_EPS)).astype(x.dtype)

def causal_depthwise_conv(x, w):
    C = x.shape[-1]
    return lax.conv_general_dilated(
        x, w[:, None, :].astype(x.dtype), window_strides=(1,),
        padding=[(CONV_WIDTH - 1, 0)], dimension_numbers=("NWC", "WIO", "NWC"),
        feature_group_count=C)

def diff_attention(q, k, v, lam):
    S = q.shape[1]
    H = DIFF_HEADS
    scale = DIFF_QK_DIM ** -0.5
    slopes = 2.0 ** (-8.0 * jnp.arange(1, H + 1, dtype=jnp.float32) / H)
    outs = []
    for blk in range(S // ATTN_BLOCK):
        q0 = blk * ATTN_BLOCK
        kv_len = q0 + ATTN_BLOCK
        qb = q[:, q0:kv_len]
        kb = k[:, :kv_len]
        vb = v[:, :kv_len]
        s = jnp.einsum("bqhmd,bkhmd->bhmqk", qb, kb).astype(jnp.float32) * scale
        rel = (q0 + jnp.arange(ATTN_BLOCK))[:, None] - jnp.arange(kv_len)[None, :]
        bias = jnp.where(rel >= 0, -slopes[:, None, None] * rel, NEG_INF)
        p = jax.nn.softmax(s + bias[None, :, None], axis=-1)
        pd = p[:, :, 0] - lam * p[:, :, 1]
        outs.append(jnp.einsum("bhqk,bkhd->bqhd", pd.astype(v.dtype), vb))
    return jnp.concatenate(outs, axis=1)

def gated_delta_rule_chunked(q, k, v, g, beta):
    out_dtype = v.dtype
    q, k, v, g, beta = (t.astype(jnp.float32) for t in (q, k, v, g, beta))
    B, H, S, dk = k.shape
    dv = v.shape[-1]
    C = GDN_CHUNK
    N = S // C
    q = q * (dk ** -0.5)

    def chunks(t):
        return t.reshape(B, H, N, C, *t.shape[3:])

    q, k, v, g, beta = (chunks(t) for t in (q, k, v, g, beta))
    g = jnp.cumsum(g, axis=-1)
    k_beta = k * beta[..., None]
    v_beta = v * beta[..., None]
    incl = jnp.tril(jnp.ones((C, C), dtype=bool))
    strict = jnp.tril(jnp.ones((C, C), dtype=bool), k=-1)
    gdiff = g[..., :, None] - g[..., None, :]
    decay = jnp.where(incl, jnp.exp(jnp.where(incl, gdiff, 0.0)), 0.0)
    L = jnp.where(strict, jnp.einsum("bhnid,bhnjd->bhnij", k_beta, k) * decay, 0.0)
    rhs = jnp.concatenate([v_beta, k_beta * jnp.exp(g)[..., None]], axis=-1)
    sol = lax.linalg.triangular_solve(L, rhs, left_side=True, lower=True, unit_diagonal=True)
    u, w = sol[..., :dv], sol[..., dv:]
    qk = jnp.einsum("bhnid,bhnjd->bhnij", q, k) * decay
    g_last = g[..., -1]

    def step(state, xs):
        q_c, k_c, u_c, w_c, g_c, gl_c, qk_c = xs
        v_new = u_c - jnp.einsum("bhik,bhkv->bhiv", w_c, state)
        o = (jnp.einsum("bhik,bhkv->bhiv", q_c * jnp.exp(g_c)[..., None], state)
             + jnp.einsum("bhij,bhjv->bhiv", qk_c, v_new))
        k_dec = k_c * jnp.exp(gl_c[..., None] - g_c)[..., None]
        state = state * jnp.exp(gl_c)[..., None, None] + jnp.einsum("bhik,bhiv->bhkv", k_dec, v_new)
        return state, o

    xs = tuple(jnp.moveaxis(t, 2, 0) for t in (q, k, u, w, g, g_last, qk))
    state0 = jnp.zeros((B, H, dk, dv), jnp.float32)
    _, o = lax.scan(step, state0, xs)
    o = jnp.moveaxis(o, 0, 2).reshape(B, H, S, dv)
    return o.astype(out_dtype)

def hybrid_mixer(h, w_in, conv_w, a_log, dt_bias, lambda_q1, lambda_k1, lambda_q2, lambda_k2,
                 attn_norm_gain, gdn_norm_gain, w_out, lambda_init):
    B, S, _ = h.shape
    A, G = ATTN_WIDTH, GDN_WIDTH
    proj = h @ w_in
    qa = proj[..., 0:A].reshape(B, S, DIFF_HEADS, 2, DIFF_QK_DIM)
    ka = proj[..., A:2 * A].reshape(B, S, DIFF_HEADS, 2, DIFF_QK_DIM)
    va = proj[..., 2 * A:3 * A].reshape(B, S, DIFF_HEADS, DIFF_HEAD_DIM)
    lam = (jnp.exp(jnp.sum(lambda_q1.astype(jnp.float32) * lambda_k1.astype(jnp.float32)))
           - jnp.exp(jnp.sum(lambda_q2.astype(jnp.float32) * lambda_k2.astype(jnp.float32)))
           + lambda_init)
    oa = diff_attention(qa, ka, va, lam)
    oa = rms_norm(oa, attn_norm_gain) * (1.0 - lambda_init)
    qkv = jax.nn.silu(causal_depthwise_conv(proj[..., 3 * A:3 * A + 3 * G], conv_w))
    qg = l2_norm(qkv[..., 0:G].reshape(B, S, GDN_HEADS, GDN_HEAD_DIM))
    kg = l2_norm(qkv[..., G:2 * G].reshape(B, S, GDN_HEADS, GDN_HEAD_DIM))
    vg = qkv[..., 2 * G:3 * G].reshape(B, S, GDN_HEADS, GDN_HEAD_DIM)
    z = proj[..., 3 * A + 3 * G:3 * A + 4 * G].reshape(B, S, GDN_HEADS, GDN_HEAD_DIM)
    b_lin = proj[..., 3 * A + 4 * G:3 * A + 4 * G + GDN_HEADS].astype(jnp.float32)
    a_lin = proj[..., 3 * A + 4 * G + GDN_HEADS:].astype(jnp.float32)
    beta = jax.nn.sigmoid(b_lin)
    g = -jnp.exp(a_log.astype(jnp.float32)) * jax.nn.softplus(a_lin + dt_bias.astype(jnp.float32))
    og = gated_delta_rule_chunked(
        qg.transpose(0, 2, 1, 3), kg.transpose(0, 2, 1, 3), vg.transpose(0, 2, 1, 3),
        g.transpose(0, 2, 1), beta.transpose(0, 2, 1))
    og = og.transpose(0, 2, 1, 3)
    og = rms_norm(og, gdn_norm_gain) * jax.nn.silu(z)
    y = jnp.concatenate([oa.reshape(B, S, A), og.reshape(B, S, G)], axis=-1)
    return y @ w_out

def peer_ffn(h, w_query, sub_keys, expert_down, expert_up):
    B, S, D = h.shape
    P = PEER_BLOCK
    K = PEER_TOPK
    blocks = h.reshape((B * S) // P, P, D)

    def block_fn(xb):
        q = (xb @ w_query).reshape(P, PEER_HEADS, 2, PEER_HALF)
        s = jnp.einsum("phcd,hcnd->phcn", q, sub_keys)
        s_top, i_top = lax.top_k(s, K)
        cand = s_top[:, :, 0, :, None] + s_top[:, :, 1, None, :]
        cand_idx = i_top[:, :, 0, :, None] * N_KEYS + i_top[:, :, 1, None, :]
        best, pos = lax.top_k(cand.reshape(P, PEER_HEADS, K * K), K)
        idx = jnp.take_along_axis(cand_idx.reshape(P, PEER_HEADS, K * K), pos, axis=-1)
        gates = jax.nn.softmax(best.astype(jnp.float32), axis=-1).astype(xb.dtype)
        idx = idx.reshape(P, PEER_HEADS * K)
        u = expert_down[idx]
        act = jax.nn.gelu(jnp.einsum("pd,ped->pe", xb, u), approximate=False)
        coef = gates.reshape(P, PEER_HEADS * K) * act
        return jnp.einsum("pe,ped->pd", coef, expert_up[idx])

    return lax.map(block_fn, blocks).reshape(B, S, D)

def setup_inputs(seed: int = 0) -> dict:
    key = jax.random.key(seed)
    ks = jax.random.split(key, 24)
    D = D_MODEL

    def nrm(k, shape, scale):
        return jax.random.normal(k, shape, jnp.float32) * scale

    dt = jnp.exp(jax.random.uniform(ks[10], (DEPTH, GDN_HEADS), jnp.float32,
                                    minval=math.log(1e-3), maxval=math.log(1e-1)))
    return {
        "x": nrm(ks[0], (BATCH, SEQ, D), 1.0),
        "c": nrm(ks[1], (BATCH, D), 1.0),
        "w_mod": nrm(ks[2], (DEPTH, D, MOD_CHUNKS * D), 0.5 * D ** -0.5),
        "b_mod": nrm(ks[3], (DEPTH, MOD_CHUNKS * D), 0.01),
        "pre_mix_gain": 1.0 + nrm(ks[4], (DEPTH, D), 0.02),
        "post_mix_gain": 1.0 + nrm(ks[5], (DEPTH, D), 0.02),
        "pre_ffn_gain": 1.0 + nrm(ks[6], (DEPTH, D), 0.02),
        "post_ffn_gain": 1.0 + nrm(ks[7], (DEPTH, D), 0.02),
        "w_in": nrm(ks[8], (DEPTH, D, IN_COLS), D ** -0.5),
        "conv_w": nrm(ks[9], (DEPTH, CONV_WIDTH, 3 * GDN_WIDTH), CONV_WIDTH ** -0.5),
        "a_log": jnp.log(jax.random.uniform(ks[11], (DEPTH, GDN_HEADS), jnp.float32,
                                             minval=1.0, maxval=16.0)),
        "dt_bias": dt + jnp.log(-jnp.expm1(-dt)),
        "lambda_q1": nrm(ks[12], (DEPTH, DIFF_QK_DIM), 0.1),
        "lambda_k1": nrm(ks[13], (DEPTH, DIFF_QK_DIM), 0.1),
        "lambda_q2": nrm(ks[14], (DEPTH, DIFF_QK_DIM), 0.1),
        "lambda_k2": nrm(ks[15], (DEPTH, DIFF_QK_DIM), 0.1),
        "attn_norm_gain": 1.0 + nrm(ks[16], (DEPTH, DIFF_HEAD_DIM), 0.02),
        "gdn_norm_gain": 1.0 + nrm(ks[17], (DEPTH, GDN_HEAD_DIM), 0.02),
        "w_out": nrm(ks[18], (DEPTH, MIX_WIDTH, D), MIX_WIDTH ** -0.5),
        "w_query": nrm(ks[19], (DEPTH, D, PEER_HEADS * PEER_KEY_DIM), D ** -0.5),
        "sub_keys": nrm(ks[20], (DEPTH, PEER_HEADS, 2, N_KEYS, PEER_HALF), PEER_HALF ** -0.5),
        "expert_down": nrm(ks[21], (DEPTH, N_EXPERTS, D), D ** -0.5),
        "expert_up": nrm(ks[22], (DEPTH, N_EXPERTS, D), D ** -0.5),
    }

def reference(x, c, w_mod, b_mod, pre_mix_gain, post_mix_gain, pre_ffn_gain, post_ffn_gain,
              w_in, conv_w, a_log, dt_bias, lambda_q1, lambda_k1, lambda_q2, lambda_k2,
              attn_norm_gain, gdn_norm_gain, w_out, w_query, sub_keys, expert_down, expert_up):
    for layer in range(DEPTH):
        mod = jax.nn.silu(c) @ w_mod[layer] + b_mod[layer]
        shift_m, scale_m, gate_m, shift_f, scale_f, gate_f = (
            m[:, None, :] for m in jnp.split(mod, MOD_CHUNKS, axis=-1))
        lambda_init = 0.8 - 0.6 * math.exp(-0.3 * layer)
        h = rms_norm(x, pre_mix_gain[layer]) * (1.0 + scale_m) + shift_m
        y = hybrid_mixer(h, w_in[layer], conv_w[layer], a_log[layer], dt_bias[layer],
                         lambda_q1[layer], lambda_k1[layer], lambda_q2[layer], lambda_k2[layer],
                         attn_norm_gain[layer], gdn_norm_gain[layer], w_out[layer], lambda_init)
        x = x + gate_m * rms_norm(y, post_mix_gain[layer])
        h = rms_norm(x, pre_ffn_gain[layer]) * (1.0 + scale_f) + shift_f
        y = peer_ffn(h, w_query[layer], sub_keys[layer], expert_down[layer], expert_up[layer])
        x = x + gate_f * rms_norm(y, post_ffn_gain[layer])
    return x


_drawn_inputs = setup_inputs


def setup_inputs(seed=0):
    import zlib

    import numpy as np

    out = dict(_drawn_inputs(seed))
    spreads = {}
    factors = {'post_ffn_gain': 8.0, 'lambda_q2': 4.591, 'gdn_norm_gain': 3.018}
    for name, (base, spread) in spreads.items():
        noise = np.random.default_rng([zlib.crc32(name.encode()), seed]).standard_normal(out[name].shape)
        drawn = base * np.exp(spread * noise) if base else spread * noise
        out[name] = __import__('jax').numpy.asarray(drawn.astype(out[name].dtype))
    for name, factor in factors.items():
        out[name] = (out[name] * factor).astype(out[name].dtype)
    return out
```

```python
import math
from contextlib import ExitStack

import concourse.bass as bass
from concourse import mybir

F32 = mybir.dt.float32
F32R = mybir.dt.float32r
BF16 = mybir.dt.bfloat16
I32 = mybir.dt.int32
U32 = mybir.dt.uint32
ALU = mybir.AluOpType
ACT = mybir.ActivationFunctionType
AX_X = mybir.AxisListType.X

P = 128
D = 1024
SEQ = 512
KD = D // P
NB = SEQ // P
H = 4
HD = 128
QK = 64
CH = 64
NCH = SEQ // CH
EPS = 1e-6
NEG = -1e30
LOWEST = -3.4e38
LAMBDA_INIT = 0.8 - 0.6 * math.exp(0.0)
PH = 8
TOPK = 16
N_TILES = 128

T_GDN, T_KA, T_QA = 0, 12, 16
T_VA, T_Z, T_OUT, T_QUERY = 20, 24, 28, 36
T_DOWN = 52
T_UP = T_DOWN + N_TILES
T_ALL = T_UP + N_TILES
RAW = 4
SPLIT = 2
AHEAD = RAW + 1

LEAD, BUILD, REST = 12, 16, 12
RING = 4
TOK4 = 4


def build(nc, x, c_col, mod_tiles, mod_bias_col, gate_bias_rows, gain_cols, gain_rows, in_tiles,
          ba_w, conv_col, a_log, dt_bias, lambdas, head_gains, out_tiles, query_tiles, keys_t,
          expert_tiles, out):
    act_dram = nc.dram_tensor("act_scratch", (N_TILES, P, SEQ), F32).ap()
    gate_dram = nc.dram_tensor("gate_scratch", (N_TILES, P, SEQ), F32).ap()
    x1_dram = nc.dram_tensor("x1_scratch", (NB, P, D), F32).ap()
    with ExitStack() as ctx:
        def sem(name):
            return ctx.enter_context(nc.semaphore(name))

        cursor = [17408]

        def at(name, shape, dt, offset=None):
            size = 2 if dt == BF16 else 4
            for n in shape[1:]:
                size *= n
            offset = cursor[0] if offset is None else offset
            cursor[0] = offset + (size + 31) // 32 * 32
            assert cursor[0] <= 229344, (name, cursor[0])
            return nc.alloc_sbuf_tensor_at(name, shape, dt, offset=offset)

        ident = at("ident", [P, P], F32)
        acol = at("acol", [P, 2, KD], F32)
        bcol = at("bcol", [P, 2, KD], F32)
        gaincol = at("gaincol", [P, 2, KD], F32)
        modbcol = at("modbcol", [P, 4, KD], F32)
        small = at("small", [P, 64], F32)
        iota16 = at("iota16", [P, TOPK], F32)
        iotaN = at("iotaN", [P, P], F32)
        gate_m = at("gate_m", [P, D], F32)
        gate_f = at("gate_f", [P, D], F32)
        raw = at("raw", [P, RAW, D], F32)
        whi = at("whi", [P, SPLIT, D], F32R)
        wlo = at("wlo", [P, SPLIT, D], F32R)
        acts = cursor[0]
        act_hi = at("act_hi", [P, KD, SEQ], F32R)
        act_lo = at("act_lo", [P, KD, SEQ], F32R)
        phase = cursor[0]

        xn = at("xn", [P, NB, D], F32)
        kbeg = at("kbeg", [P, NB, 512], F32, phase)
        kdec = at("kdec", [P, NB, 512], F32)
        modr = at("modr", [P, 4, D], F32)
        onat = at("onat", [P, NB, D], F32, cursor[0] - 4 * D * 4)
        xs2 = at("xs2", [P, NB, D], F32, cursor[0] - 4 * D * 4)
        kq = cursor[0]
        kaT = at("kaT", [P, H, SEQ], F32)
        qaT = at("qaT", [P, H, SEQ], F32)
        osq = at("osq", [P, NB * D], F32, kq)
        va = at("va", [P, NB, 512], F32)
        zs = at("zs", [P, NB, 512], F32)
        qkvT = at("qkvT", [P, 12, SEQ], F32)
        u = at("u", [P, NB, 512], F32, cursor[0] - 4 * SEQ * 4)
        t_base = cursor[0]
        Tm = at("Tm", [P, NB, 512], F32)
        TT = at("TT", [P, NB, 512], F32)
        PM = at("PM", [P, NB, 512], F32)
        after_t = cursor[0]
        bias = at("bias", [P, 2, 512], F32, t_base)
        pr = at("pr", [P, 2, 2, 512], F32)
        pT = at("pT", [P, 2, 512], F32)
        rel = at("rel", [P, 512], F32)
        negm = at("negm", [P, 512], F32)
        wk = at("wk", [P, 4, 512], F32, t_base + 2 * 512 * 4)
        vbeta = at("vbeta", [P, NB, 512], F32, after_t)
        gainrow = at("gainrow", [P, 2, D], F32, after_t)
        masks = at("masks", [P, 10, P], F32)
        state = at("state", [P, 512], F32)
        vnew = at("vnew", [P, 512], F32)
        ones = at("ones", [P, P], F32, cursor[0] - 512 * 4)
        mrow = at("mrow", [P, 576], F32, cursor[0] + 3 * P * 4)
        gsm = at("gsm", [P, 288], F32)
        baw = at("baw", [P, KD, 8], F32)
        xij = at("xij", [P, 2, P], I32, after_t)
        LT = at("LT", [P, NB, 512], F32, acts)
        LM = at("LM", [P, NB, 512], F32)
        QKT = at("QKT", [P, NB, 512], F32)
        wT = at("wT", [P, NB, 512], F32)
        gB = at("gB", [P, 16, P], F32, cursor[0] - NB * 512 * 4)

        M_INCL, M_STRICT, M_U, M_FIRST, MT = 0, 1, 2, 3, 4

        def mask4(m):
            return masks[:, m, :].unsqueeze(1).to_broadcast([P, H, P])

        def by_head(ap):
            return ap.rearrange("p (h n) -> p h n", h=H)

        conv_w = mrow[:, 0:48].rearrange("p (n j) -> p n j", n=12)
        again = mrow[:, 48:176]
        ggain = mrow[:, 176:304]
        lam_in = mrow[:, 304:560]
        lam = mrow[:, 560:564]
        eps_t = small[:, 0:1]
        ssq = small[:, 4:8]
        rstd = small[:, 8:12]
        c_raw = small[:, 16:24]
        c_silu = small[:, 24:32]
        ssq2 = small[:, 32:40]
        asm = small[:, 40:52].rearrange("p (s v) -> p s v", s=2)
        mark = small[:, 56:57]
        G_BETA, G_Y, G_AY, G_SP, G_CUM, G_EXP, G_DEC, G_BEXP, G_LOG = range(9)

        def g16(i):
            return gsm[:, 16 * i:16 * i + 16]

        g_last = gsm[:, 144:176]
        o_ms = gsm[:, 176:208]
        alog4 = gsm[:, 208:212]
        dt4 = gsm[:, 212:216]

        bank = [ctx.enter_context(nc.psum_tensor(f"bank{i}", [P, 512], F32)) for i in range(8)]

        cursor[0] = phase
        S = at("S", [P, NB, 2 * PH, P], F32)
        stage = at("stage", [P, P, P], F32)
        keys = at("keys", [P, 2 * PH, P], F32, cursor[0] - P * P * 4)
        qTs = at("qTs", [P, 2, SEQ], F32)
        hfl2 = at("hfl2", [P, 2, SEQ], F32)
        cursor[0] = phase + (32 + 64) * 1024
        aout = at("aout", [P, 2, SEQ], F32)
        cand = at("cand", [P, PH, 256], F32)
        top = at("top", [P, 2 * PH, TOPK], F32)
        topi = at("topi", [P, 2 * PH, TOPK], U32)
        topf = at("topf", [P, 2 * PH, TOPK], F32)
        tmp = at("tmp", [P, 256], F32)
        best = at("best", [P, PH, TOPK], F32)
        pos = at("pos", [P, P], U32)
        posi = at("posi", [P, P], U32)
        posf = at("posf", [P, P], F32)
        pick = at("pick", [P, 3, P], F32)
        gsum = at("gsum", [P, 2 * PH], F32)
        pickT = at("pickT", [P, 4, P], F32)
        gTh = at("gTh", [P, P], F32R)
        ohJ = at("ohJ", [P, 2, TOK4 * P], F32R)
        ohE = at("ohE", [P, TOK4 * P], F32)
        ohIh = at("ohIh", [P, 2, TOK4 * P], F32R)
        ohIl = at("ohIl", [P, 2, TOK4 * P], F32R)
        cursor[0] = phase
        a_in = at("a_in", [P, RAW, SEQ], F32)
        g_in = at("g_in", [P, RAW, SEQ], F32)
        coef = at("coef", [P, 2, SEQ], F32)
        chi = at("chi", [P, 2, SEQ], F32R)
        clo = at("clo", [P, 2, SEQ], F32R)
        x1 = at("x1", [P, NB, D], F32)
        yo = at("yo", [P, NB, D], F32)

        s_raw = [sem(f"raw_landed{i}") for i in range(RAW)]
        s_hi = sem("split_hi_ready")
        s_lo = sem("split_lo_ready")
        s_used = sem("split_used")
        s_x = sem("x_landed")
        s_c = sem("consts_landed")
        s_gr = sem("gain_rows_landed")
        s_modl = [sem(f"mod_landed{i}") for i in range(4)]
        s_modu = sem("mod_used")
        s_pool = sem("pool_consts")
        s_xij = sem("masks_made")
        s_cc = sem("c_silu")
        s_cols = sem("mod_columns_read")
        s_ssq = sem("sum_of_squares")
        s_msq = sem("mean_square")
        s_rt = sem("root")
        s_xs = sem("x_scaled")
        s_xT = sem("x_transposed")
        s_hf = sem("h_float")
        s_hhi = sem("h_hi")
        s_hlo = sem("h_lo")
        s_conv = sem("conv_done")
        s_silu = sem("silu_done")
        s_kq = sem("attn_kq_copied")
        s_nat = sem("natural_tiles_copied")
        s_ba = sem("ba_done")
        s_gate = sem("gate_group_read")
        s_sq = sem("qk_squares")
        s_l2 = sem("qk_norm_sums")
        s_l2r = sem("qk_norm_roots")
        s_l2n = sem("qk_normed")
        s_lam = sem("lambda_sums")
        s_lame = sem("lambda_exp")
        s_sc = sem("attn_scores")
        s_mx = sem("attn_max")
        s_ex = sem("attn_exp")
        s_pd = sem("attn_diff")
        s_pt = sem("attn_transposed")
        s_ptc = sem("attn_transposed_copied")
        s_av = sem("attn_values")
        s_oa = sem("attn_out_copied")
        s_g1 = sem("gdn_rows")
        s_g1e = sem("gdn_rows_exp")
        s_gl = sem("gdn_log_decay")
        s_gB = sem("gdn_decay_spread")
        s_gc = sem("gdn_cumsum")
        s_gcc = sem("gdn_cumsum_copied")
        s_row = sem("gdn_decay_rows")
        s_du = sem("gdn_decay_args")
        s_de = sem("gdn_decay_exp")
        s_kg = sem("gdn_grams")
        s_L = sem("gdn_L")
        s_LT = sem("gdn_L_transposed")
        s_LTc = sem("gdn_LT_copied")
        s_t0 = sem("inv_first_T")
        s_vt = sem("gdn_vk_transposed")
        s_vtd = sem("gdn_vk_scaled")
        s_lm = sem("inv_masked")
        s_pp = sem("inv_P")
        s_pc = sem("inv_P_copied")
        s_tt = sem("inv_update")
        s_td = sem("inv_T_ready")
        s_uw = sem("gdn_uw")
        s_uwc = sem("gdn_uw_copied")
        s_st0 = sem("scan_state_cleared")
        s_wS = sem("scan_wS")
        s_qS = sem("scan_qS")
        s_vn = sem("scan_vnew")
        s_kv = sem("scan_kv")
        s_qkv = sem("scan_qkv")
        s_st = sem("scan_state")
        s_oc = sem("scan_out_copied")
        s_oms = sem("head_mean_squares")
        s_omr = sem("head_roots")
        s_on = sem("heads_normed")
        s_oT = sem("o_transposed")
        s_ohi = sem("o_hi")
        s_olo = sem("o_lo")
        s_xr = sem("x_again_landed")
        s_x1 = sem("x1_ready")
        s_x1o = sem("x1_stored")
        s_key = sem("keys_landed")
        s_qT = sem("query_copied")
        s_qs = sem("key_scores")
        s_S = sem("key_scores_copied")
        s_act = sem("gelu_done")
        s_ast = [sem(f"act_stored{i}") for i in range(2)]
        s_best = sem("topk_best")
        s_gexp = sem("topk_exp")
        s_pick = sem("picks_ready")
        s_pkT = sem("picks_transposed")
        s_pkc = sem("picks_copied")
        s_oh = sem("onehots_ready")
        s_gp = sem("gate_products")
        s_gev = sem("gates_staged")
        s_gst = sem("gates_stored")
        s_ain = [sem(f"act_landed{i}") for i in range(RAW)]
        s_gin = [sem(f"gates_landed{i}") for i in range(RAW)]
        s_cf = sem("coef_ready")
        s_chi = sem("coef_hi")
        s_clo = sem("coef_lo")
        s_x1l = sem("x1_landed")
        s_yq = sem("y_squares")
        s_ym = sem("y_mean_square")
        s_yr = sem("y_root")
        s_yo = sem("out_ready")
        s_out = sem("out_stored")

        def raw_wait(eng, n):
            eng.wait_ge(s_raw[n % RAW], 16 * (n // RAW + 1))

        block = ctx.enter_context(nc.Block())

        @block.sync
        def _(sp):
            dq = sp.dma_start
            for b in range(NB):
                dq(xn[:, b, :], x[b]).then_inc(s_x, 16)
            for dst, src in [(gaincol[:], gain_cols), (modbcol[:], mod_bias_col),
                             (mrow[:, 0:48], conv_col), (c_raw, c_col), (baw[:], ba_w),
                             (mrow[:, 48:304], head_gains.partition_broadcast(P)),
                             (alog4, a_log.partition_broadcast(P)),
                             (dt4, dt_bias.partition_broadcast(P)),
                             (lam_in, lambdas.partition_broadcast(P)),
                             (gate_m[:], gate_bias_rows[0].partition_broadcast(P)),
                             (gate_f[:], gate_bias_rows[1].partition_broadcast(P))]:
                dq(dst, src).then_inc(s_c, 16)

            def load_mod(m):
                if m >= 4:
                    sp.wait_ge(s_modu, m - 3)
                dq(modr[:, m % 4, :], mod_tiles[m]).then_inc(s_modl[m % 4], 16)

            def load_raw(n, src):
                if n >= RAW:
                    sp.wait_ge(s_lo, n - RAW + 1)
                dq(raw[:, n % RAW, :], src).then_inc(s_raw[n % RAW], 16)

            for m in range(16):
                load_mod(m)
                if m >= 12:
                    load_raw(m - 12, in_tiles[m - 12])
            sp.wait_ge(s_xij, 1)
            for r in range(2):
                dq(gainrow[:, r, :], gain_rows[r].partition_broadcast(P)).then_inc(s_gr, 16)
            for n in range(4, 28):
                load_mod(n + 12)
                load_raw(n, in_tiles[n])
            for m in range(40, 48):
                load_mod(m)
            for n in range(8):
                load_raw(T_OUT + n, out_tiles[n])
            sp.wait_ge(s_on, 1)
            for b in range(NB):
                dq(xn[:, b, :], x[b]).then_inc(s_xr, 16)
            for n in range(4):
                load_raw(T_QUERY + n, query_tiles[n])
            sp.wait_ge(s_x1, NB)
            for b in range(NB):
                dq(x1_dram[b], xn[:, b, :]).then_inc(s_x1o, 16)
            sp.wait_ge(s_hlo, 2 * KD)
            sp.wait_ge(s_x1o, 16 * NB)
            dq(keys[:], keys_t).then_inc(s_key, 16)
            for n in range(4, 16):
                load_raw(T_QUERY + n, query_tiles[n])

            for n in range(AHEAD):
                load_raw(T_DOWN + n, expert_tiles[n])

            def down_tiles(t0, count, gates_of=None):
                with sp.Fori(0, count // 4) as i:
                    for j in range(4):
                        t = i * 4 + (t0 + j)
                        sp.wait_ge(s_act, t + 1)
                        dq(act_dram[t], aout[:, j % 2, :]).then_inc(s_ast[j % 2], 16)
                        sp.wait_ge(s_lo, t + (T_DOWN + AHEAD - RAW + 1))
                        slot = (T_DOWN + AHEAD + j) % RAW
                        dq(raw[:, slot, :], expert_tiles[t + AHEAD]).then_inc(s_raw[slot], 16)

            down_tiles(0, LEAD)
            for b in range(NB):
                down_tiles(LEAD + b * (BUILD + REST), BUILD)
                sp.wait_ge(s_gev, RING + 32 * (b + 1))
                dq(gate_dram[:, :, b * P:(b + 1) * P].rearrange("i j t -> j i t"),
                   stage[:]).then_inc(s_gst, 16)
                down_tiles(LEAD + b * (BUILD + REST) + BUILD, REST)
            down_tiles(LEAD + NB * (BUILD + REST), N_TILES - LEAD - NB * (BUILD + REST))

            sp.wait_ge(s_gst, 16 * NB)
            for r in range(2):
                sp.wait_ge(s_ast[r], 16 * (N_TILES // 2))
            for r in range(RAW):
                dq(a_in[:, r, :], act_dram[r]).then_inc(s_ain[r], 16)
                dq(g_in[:, r, :], gate_dram[r]).then_inc(s_gin[r], 16)
            for b in range(NB):
                dq(x1[:, b, :], x1_dram[b]).then_inc(s_x1l, 16)

            def up_tile(t, j, more):
                slot = (T_UP + AHEAD + j) % RAW
                if more:
                    sp.wait_ge(s_lo, t + (T_UP + AHEAD - RAW + 1))
                    dq(raw[:, slot, :], expert_tiles[t + (N_TILES + AHEAD)]).then_inc(s_raw[slot], 16)
                sp.wait_ge(s_cf, t + 1)
                dq(a_in[:, j, :], act_dram[t + RAW]).then_inc(s_ain[j], 16)
                dq(g_in[:, j, :], gate_dram[t + RAW]).then_inc(s_gin[j], 16)

            with sp.Fori(0, N_TILES // 4 - 2) as i:
                for j in range(4):
                    up_tile(i * 4 + j, j, True)
            for t in range(N_TILES - 8, N_TILES - 4):
                up_tile(t, t % 4, t + AHEAD < N_TILES)
            for b in range(NB):
                sp.wait_ge(s_yo, b + 1)
                dq(out[b], yo[:, b, :]).then_inc(s_out, 16)
            sp.wait_ge(s_out, 16 * NB)

        @block.gpsimd
        def _(pool):
            g = nc.gpsimd
            g.memset(ident[:], 0.0)
            g.memset(ones[:], 1.0)
            g.memset(small[:, 0:1], EPS)
            g.iota(xij[:, 0, :], pattern=[[0, P]], base=0, channel_multiplier=1)
            g.iota(xij[:, 1, :], pattern=[[1, P]], base=0, channel_multiplier=0)
            g.iota(rel[:], pattern=[[-1, 512]], base=384, channel_multiplier=1,
                   allow_small_or_imprecise_dtypes=True)
            g.iota(iota16[:], pattern=[[1, TOPK]], base=0, channel_multiplier=0,
                   allow_small_or_imprecise_dtypes=True)
            g.iota(iotaN[:], pattern=[[1, P]], base=0, channel_multiplier=0,
                   allow_small_or_imprecise_dtypes=True)
            g.drain()
            g.affine_select(out=ident[:], in_=ident[:], compare_op=ALU.not_equal, fill=1.0, base=0,
                            pattern=[[-1, P]], channel_multiplier=1).then_inc(s_pool, 1)
            with pool.Fori(0, T_ALL // RAW) as i:
                for j in range(RAW):
                    pool.wait_ge(s_hi, i * RAW + (j + 1))
                    g.tensor_tensor(wlo[:, j % SPLIT, :], raw[:, j, :],
                                    whi[:, j % SPLIT, :].bitcast(F32), ALU.subtract).then_inc(s_lo, 1)

        @block.scalar
        def _(act):
            sc = nc.scalar

            def hi(n):
                raw_wait(act, n)
                if n >= SPLIT:
                    act.wait_ge(s_used, n - SPLIT + 1)
                sc.copy(whi[:, n % SPLIT, :], raw[:, n % RAW, :]).then_inc(s_hi, 1)

            act.wait_ge(s_c, 16 * 11)
            sc.activation(c_silu, c_raw, ACT.Silu).then_inc(s_cc, 1)
            act.wait_ge(s_x, 16 * NB)
            for b in range(NB):
                sc.activation(qkvT[:, 0:2, :], xn[:, b, :].rearrange("p (a n) -> p a n", a=2),
                              ACT.Square, accum_out=ssq[:, b:b + 1]).then_inc(s_ssq, 1)
                act.wait_ge(s_ssq, b + 1)
            act.wait_ge(s_msq, 1)
            sc.activation(rstd, rstd, ACT.Sqrt).then_inc(s_rt, 1)
            hi(0)
            hi(1)
            for k in range(KD):
                act.wait_ge(s_hf, k + 1)
                sc.copy(act_hi[:, k, :], wk[:, k % 2, :]).then_inc(s_hhi, 1)
            for n in range(T_KA):
                hi(n + 2)
                act.wait_ge(s_conv, n + 1)
                sc.activation(qkvT[:, n, :], qkvT[:, n, :], ACT.Silu).then_inc(s_silu, 1)
            for n in range(T_KA, T_VA):
                hi(n + 2)
                act.wait_ge(s_used, n + 1)
                dst = kaT[:, n - T_KA, :] if n < T_QA else qaT[:, n - T_QA, :]
                sc.mul(dst, bank[n % 4][:], 1.0 if n < T_QA else QK ** -0.5).then_inc(s_kq, 1)
            hi(T_VA + 2)
            hi(T_VA + 3)
            act.wait_ge(s_used, T_Z)
            for b in range(NB):
                sc.copy(va[:, b, :], bank[b][:]).then_inc(s_nat, 1)
            for n in range(T_Z, T_OUT):
                hi(n)
            act.wait_ge(s_used, T_OUT)
            for b in range(NB):
                sc.activation(zs[:, b, :], bank[b][:], ACT.Silu).then_inc(s_nat, 1)
            hi(T_OUT)
            hi(T_OUT + 1)
            for n in range(8):
                act.wait_ge(s_l2, n + 1)
                if n >= 2:
                    act.wait_ge(s_l2n, n - 1)
                sc.activation(wk[:, 2 + n % 2, :], bank[n % 2][:], ACT.Sqrt, bias=eps_t).then_inc(s_l2r, 1)
            act.wait_ge(s_lam, 1)
            sc.activation(lam[:, 0:2], lam[:, 0:2], ACT.Exp).then_inc(s_lame, 1)
            act.wait_ge(s_g1, 1)
            sc.activation(g16(G_BETA), g16(G_BETA), ACT.Exp, scale=-1.0)
            sc.activation(g16(G_SP), g16(G_AY), ACT.Exp, scale=-1.0)
            sc.activation(alog4, alog4, ACT.Exp)
            sc.drain()
            sc.activation(g16(G_SP), g16(G_SP), ACT.Ln, bias=1.0).then_inc(s_g1e, 1)

            def exps(i):
                act.wait_ge(s_mx, i + 1)
                n = (i % NB + 1) * P
                for m in range(2):
                    last = sc.activation(pr[:, i % 2, m, 0:n], pr[:, i % 2, m, 0:n], ACT.Exp,
                                         bias=asm[:, i % 2, 2 + m:3 + m],
                                         accum_out=asm[:, i % 2, 4 + m:5 + m])
                last.then_inc(s_ex, 1)

            def copy_t(i):
                act.wait_ge(s_pt, i + 1)
                if i >= 2:
                    act.wait_ge(s_av, i - 1)
                n = (i % NB + 1) * P
                sc.copy(pT[:, i % 2, 0:n], bank[4 + i % 2][:, 0:n]).then_inc(s_ptc, 1)

            for i in range(H * NB + 1):
                if i < H * NB:
                    exps(i)
                if i >= 1:
                    copy_t(i - 1)

            for t in range(NB):
                act.wait_ge(s_du, t + 1)
                sc.activation(QKT[:, t, :], QKT[:, t, :], ACT.Exp)
                last = sc.activation(LM[:, t, :], LM[:, t, :], ACT.Exp, scale=-1.0)
                if t == NB - 1:
                    sc.activation(g16(G_EXP), g16(G_CUM), ACT.Exp)
                    sc.activation(g16(G_DEC), g16(G_DEC), ACT.Exp)
                    last = sc.activation(g_last, g_last, ACT.Exp)
                last.then_inc(s_de, 1)
            for t in range(NB):
                act.wait_ge(s_LT, t + 1)
                sc.copy(LT[:, t, :], bank[4 + t % 2][:]).then_inc(s_LTc, 1)
            for k in range(1, 6):
                for t in range(NB):
                    n = (k - 1) * NB + t
                    act.wait_ge(s_pp, n + 1)
                    if k > 1:
                        act.wait_ge(s_tt, n - NB + 1)
                    sc.copy(PM[:, t, :], bank[t % 2][:]).then_inc(s_pc, 1)
            for t in range(NB):
                act.wait_ge(s_uw, t + 1)
                sc.copy(u[:, t, :], bank[2 * (t % 2)][:])
                sc.copy(wT[:, t, :], bank[2 * (t % 2) + 1][:]).then_inc(s_uwc, 1)
            act.wait_ge(s_oms, 1)
            sc.activation(o_ms, o_ms, ACT.Sqrt).then_inc(s_omr, 1)
            for k in range(KD):
                act.wait_ge(s_oT, k + 1)
                sc.copy(act_hi[:, k, :], bank[6 + k % 2][:]).then_inc(s_ohi, 1)
            for n in range(T_OUT + 2, T_QUERY):
                hi(n)
            act.wait_ge(s_used, T_QUERY)
            for b in range(NB):
                for half in range(2):
                    last = sc.activation(osq[:, (2 * b + half) * 512:(2 * b + half + 1) * 512],
                                         bank[4 * half + b][:], ACT.Square,
                                         accum_out=ssq2[:, 2 * b + half:2 * b + half + 1])
            last.then_inc(s_ssq, 1)
            sc.drain()
            act.wait_ge(s_msq, 2)
            sc.activation(rstd, rstd, ACT.Sqrt).then_inc(s_rt, 1)
            hi(T_QUERY)
            hi(T_QUERY + 1)
            for b in range(NB):
                act.wait_ge(s_x1, b + 1)
                last = sc.activation(osq[:, b * D:(b + 1) * D], xn[:, b, :], ACT.Square,
                                     accum_out=ssq[:, b:b + 1])
            last.then_inc(s_ssq, 1)
            act.wait_ge(s_msq, 3)
            sc.activation(rstd, rstd, ACT.Sqrt).then_inc(s_rt, 1)
            for k in range(KD):
                act.wait_ge(s_hf, KD + k + 1)
                sc.copy(act_hi[:, k, :], hfl2[:, k % 2, :]).then_inc(s_hhi, 1)
            for n in range(16):
                act.wait_ge(s_used, T_QUERY + n + 1)
                if n >= 2:
                    act.wait_ge(s_qs, n - 1)
                sc.copy(qTs[:, n % 2, :], bank[n % 4][:]).then_inc(s_qT, 1)
                hi(T_QUERY + n + 2)

            act.sem_inc(s_gev, RING)

            def down_tiles(t0, count, b=None, first=0):
                def one(i, j, unguarded=False):
                    t = i * 4 + (t0 + j)
                    act.wait_ge(s_used, t + (T_DOWN + 1))
                    slot = (T_DOWN + 2 + j) % RAW
                    act.wait_ge(s_raw[slot], i * 16 + 16 * ((T_DOWN + 2 + t0 + j) // RAW + 1))
                    sc.copy(whi[:, j % SPLIT, :], raw[:, slot, :]).then_inc(s_hi, 1)
                    if j >= 2 or not unguarded:
                        act.wait_ge(s_ast[j % 2], i * 32 + 16 * ((t0 + j) // 2))
                    sc.activation(aout[:, j % 2, :], bank[j][:], ACT.Gelu).then_inc(s_act, 1)
                    if b is not None:
                        for r in range(2):
                            q = i * 8 + (32 * b + 2 * j + r)
                            act.wait_ge(s_gp, q + 1)
                            sc.copy(stage[:, :, bass.ds(i * 32 + (2 * j + r) * TOK4, TOK4)]
                                    .rearrange("p i t -> p t i"),
                                    bank[4 + (2 * j + r) % 4][:].rearrange("p (t i) -> p t i", t=TOK4)
                                    ).then_inc(s_gev, 1)
                if first:
                    for j in range(4):
                        one(0, j, True)
                with act.Fori(first, count // 4) as i:
                    for j in range(4):
                        one(i, j)

            down_tiles(0, LEAD, first=1)
            for b in range(NB):
                act.wait_ge(s_best, b + 1)
                sc.activation(pick[:, 2, :], best[:].rearrange("p h k -> p (h k)"),
                              ACT.Exp).then_inc(s_gexp, 1)
                if b > 0:
                    act.wait_ge(s_gst, 16 * b)
                down_tiles(LEAD + b * (BUILD + REST), BUILD, b)
                down_tiles(LEAD + b * (BUILD + REST) + BUILD, REST)
            down_tiles(LEAD + NB * (BUILD + REST), N_TILES - LEAD - NB * (BUILD + REST))

            def round_coef(t, j, reused):
                act.wait_ge(s_cf, t + 1)
                if reused:
                    act.wait_ge(s_used, t + (T_UP - 1))
                sc.copy(chi[:, j % 2, :], coef[:, j % 2, :]).then_inc(s_chi, 1)

            def up_tile(t, j, more):
                if more:
                    slot = (T_UP + 2 + j) % RAW
                    act.wait_ge(s_raw[slot], (t - j) * 4 + 16 * ((T_UP + 2 + j) // RAW + 1))
                    act.wait_ge(s_used, t + (T_UP + 1))
                    sc.copy(whi[:, j % SPLIT, :], raw[:, slot, :]).then_inc(s_hi, 1)

            round_coef(0, 0, False)
            round_coef(1, 1, False)
            up_tile(0, 0, True)
            for t in range(1, 4):
                round_coef(t + 1, t + 1, True)
                up_tile(t, t, True)
            with act.Fori(1, N_TILES // 4 - 1) as i:
                for j in range(4):
                    round_coef(i * 4 + (j + 1), j + 1, True)
                    up_tile(i * 4 + j, j, True)
            for t in range(N_TILES - 4, N_TILES):
                if t + 1 < N_TILES:
                    round_coef(t + 1, t + 1, True)
                up_tile(t, t % 4, t + 2 < N_TILES)
            act.wait_ge(s_used, T_ALL)
            for b in range(NB):
                for half in range(2):
                    last = sc.activation(yo[:, b, half * 512:(half + 1) * 512], bank[2 * b + half][:],
                                         ACT.Square, accum_out=ssq2[:, 2 * b + half:2 * b + half + 1])
            last.then_inc(s_yq, 1)
            act.wait_ge(s_ym, 1)
            sc.activation(rstd, rstd, ACT.Sqrt).then_inc(s_yr, 1)

        @block.tensor
        def _(pe):
            mm = nc.tensor.matmul

            def mod_column(m, col):
                pe.wait_ge(s_modl[m % 4], 16 * (m // 4 + 1))
                for k in range(KD):
                    last = mm(bank[7][:, col:col + 1], modr[:, m % 4, k * P:(k + 1) * P],
                              c_silu[:, k:k + 1], start=(k == 0), stop=(k == KD - 1))
                last.then_inc(s_modu, 1)

            def mod_gate(m):
                q = (m - 32) % 4
                pe.wait_ge(s_modl[m % 4], 16 * (m // 4 + 1))
                for kk in range(2):
                    k = 2 * q + kk
                    last = mm(bank[5 + (m - 32) // 4 % 2][:], c_silu[:, k:k + 1].to_broadcast([P, P]),
                              modr[:, m % 4, kk * 512:(kk + 1) * 512], start=(k == 0), stop=(k == KD - 1))
                last.then_inc(s_modu, 1)

            def split_wait(n):
                pe.wait_ge(s_lo, n + 1)

            def column_tile(slot, out_bank):
                for k in range(KD):
                    w = slice(k * P, (k + 1) * P)
                    mm(out_bank[:], whi[:, slot, w], act_hi[:, k, :], start=(k == 0), stop=False)
                    mm(out_bank[:], whi[:, slot, w], act_lo[:, k, :], start=False, stop=False)
                    last = mm(out_bank[:], wlo[:, slot, w], act_hi[:, k, :], start=False,
                              stop=(k == KD - 1))
                last.then_inc(s_used, 1)

            def natural_tile(slot, q, banks):
                for b in range(NB):
                    for kk in range(2):
                        k = 2 * q + kk
                        w = slice(kk * 512, (kk + 1) * 512)
                        a = slice(b * P, (b + 1) * P)
                        mm(banks[b][:], act_hi[:, k, a], whi[:, slot, w], start=(k == 0), stop=False)
                        mm(banks[b][:], act_hi[:, k, a], wlo[:, slot, w], start=False, stop=False)
                        last = mm(banks[b][:], act_lo[:, k, a], whi[:, slot, w], start=False,
                                  stop=(k == KD - 1))
                last.then_inc(s_used, 1)

            pe.wait_ge(s_cc, 1)
            for m in range(16):
                mod_column(m, m)
            pe.wait_ge(s_pool, 1)
            pe.wait_ge(s_xs, 1)
            for k in range(KD):
                if k >= 2:
                    pe.wait_ge(s_hf, k - 1)
                for b in range(NB):
                    last = nc.tensor.transpose(bank[k % 2][:, b * P:(b + 1) * P],
                                               xn[:, b, k * P:(k + 1) * P], ident[:])
                last.then_inc(s_xT, 1)
            pe.wait_ge(s_hlo, KD)
            for n in range(T_VA):
                split_wait(n)
                if 4 <= n < T_QA:
                    pe.wait_ge(s_conv, n - 3)
                if n >= T_QA:
                    pe.wait_ge(s_kq, n - T_QA + 1)
                column_tile(n % SPLIT, bank[n % 4])
                if n < 16:
                    mod_column(16 + n, 16 + n)
                else:
                    mod_gate(16 + n)
            for n in range(T_VA, T_OUT):
                split_wait(n)
                if n == T_VA:
                    pe.wait_ge(s_kq, 8)
                if n == T_Z:
                    pe.wait_ge(s_nat, NB)
                natural_tile(n % SPLIT, n % 4, bank[0:4])
                if n == T_Z:
                    pe.wait_ge(s_gate, 1)
                mod_gate(16 + n)
            for b in range(NB):
                for k in range(KD):
                    mm(bank[4][:, b * 8:b * 8 + 8], act_hi[:, k, b * P:(b + 1) * P].bitcast(F32),
                       baw[:, k, :], start=(k == 0), stop=False)
                    last = mm(bank[4][:, b * 8:b * 8 + 8], act_lo[:, k, b * P:(b + 1) * P].bitcast(F32),
                              baw[:, k, :], start=False, stop=(k == KD - 1))
            last.then_inc(s_ba, 1)
            pe.wait_ge(s_gate, 2)
            for m in range(44, 48):
                mod_gate(m)
            pe.wait_ge(s_nat, 2 * NB)
            for n in range(8):
                pe.wait_ge(s_sq, n + 1)
                if n >= 2:
                    pe.wait_ge(s_l2r, n - 1)
                mm(bank[n % 2][:], ones[:], wk[:, n % 2, :], start=True, stop=True).then_inc(s_l2, 1)

            pe.wait_ge(s_l2r, 8)
            pe.wait_ge(s_gate, 4)
            pe.wait_ge(s_cols, 2)
            pe.wait_ge(s_g1, 1)

            def scores(i):
                h, b = divmod(i, NB)
                if i >= 2:
                    pe.wait_ge(s_mx, i - 1)
                for m in range(2):
                    r = slice(m * QK, (m + 1) * QK)
                    last = mm(bank[2 * (i % 2) + m][:, 0:(b + 1) * P], qaT[r, h, b * P:(b + 1) * P],
                              kaT[r, h, 0:(b + 1) * P], start=True, stop=True)
                last.then_inc(s_sc, 1)

            def transposes(i):
                pe.wait_ge(s_pd, i + 1)
                if i >= 2:
                    pe.wait_ge(s_ptc, i - 1)
                for j in range(i % NB + 1):
                    last = nc.tensor.transpose(bank[4 + i % 2][:, j * P:(j + 1) * P],
                                               pr[:, i % 2, 0, j * P:(j + 1) * P], ident[:])
                last.then_inc(s_pt, 1)

            def values(i):
                h, b = divmod(i, NB)
                pe.wait_ge(s_ptc, i + 1)
                if i >= 2:
                    pe.wait_ge(s_oa, i - 1)
                for j in range(b + 1):
                    last = mm(bank[6 + i % 2][:, 0:HD], pT[:, i % 2, j * P:(j + 1) * P],
                              va[:, j, h * HD:(h + 1) * HD], start=(j == 0), stop=(j == b))
                last.then_inc(s_av, 1)

            for i in range(H * NB + 2):
                if i < H * NB:
                    scores(i)
                if 1 <= i <= H * NB:
                    transposes(i - 1)
                if i >= 2:
                    values(i - 2)

            def blk(t):
                return slice(t * P, (t + 1) * P)

            def hs(h):
                return slice(h * HD, (h + 1) * HD)

            pe.wait_ge(s_oa, H * NB)
            pe.wait_ge(s_gB, 1)
            mm(bank[7][:, 0:16], masks[:, M_U, :], g16(G_LOG), start=True, stop=True).then_inc(s_gc, 1)
            for t in range(NB):
                for h in range(H):
                    last = mm(bank[t][:, hs(h)], gB[:, 4 * t + h, :], masks[:, M_U, :], start=True, stop=True)
                last.then_inc(s_row, 1)
            pe.wait_ge(s_gcc, 1)
            for t in range(NB):
                if t >= 2:
                    pe.wait_ge(s_L, t - 1)
                for h in range(H):
                    mm(bank[4 + t % 2][:, hs(h)], qkvT[:, 4 + h, blk(t)], qkvT[:, 4 + h, blk(t)],
                       start=True, stop=True)
                for h in range(H):
                    last = mm(bank[6 + t % 2][:, hs(h)], qkvT[:, 4 + h, blk(t)], qkvT[:, h, blk(t)],
                              start=True, stop=True)
                last.then_inc(s_kg, 1)
            for t in range(NB):
                if t == 0:
                    pe.wait_ge(s_L, NB)
                if t >= 2:
                    pe.wait_ge(s_LTc, t - 1)
                for h in range(H):
                    last = nc.tensor.transpose(bank[4 + t % 2][:, hs(h)], LM[:, t, hs(h)], ident[:])
                last.then_inc(s_LT, 1)
            for t in range(NB):
                if t >= 1:
                    pe.wait_ge(s_vtd, t)
                for h in range(H):
                    nc.tensor.transpose(bank[6][:, hs(h)], qkvT[:, 8 + h, blk(t)], ident[:])
                for h in range(H):
                    last = nc.tensor.transpose(bank[7][:, hs(h)], qkvT[:, 4 + h, blk(t)], ident[:])
                last.then_inc(s_vt, 1)

            def level_p(n):
                t = n % NB
                pe.wait_ge(s_lm, n + 1)
                pe.wait_ge(s_td, n + 1)
                if n >= 2:
                    pe.wait_ge(s_pc, n - 1)
                for h in range(H):
                    last = mm(bank[t % 2][:, hs(h)], LM[:, t, hs(h)], Tm[:, t, hs(h)], start=True, stop=True)
                last.then_inc(s_pp, 1)

            def level_t(n):
                k, t = divmod(n, NB)
                pe.wait_ge(s_pc, n + 1)
                if n >= 2:
                    pe.wait_ge(s_td, NB + n - 1)
                if n == 0:
                    pe.wait_ge(s_LTc, NB)
                for h in range(H):
                    if k < 4:
                        mm(bank[2 + t % 2][:, hs(h)], TT[:, t, hs(h)], PM[:, t, hs(h)], start=True, stop=True)
                for h in range(H):
                    last = mm(bank[4 + t % 2][:, hs(h)], PM[:, t, hs(h)], TT[:, t, hs(h)], start=True, stop=True)
                last.then_inc(s_tt, 1)

            for n in range(5 * NB + 1):
                if n < 5 * NB:
                    level_p(n)
                if n >= 1:
                    level_t(n - 1)
            for t in range(NB):
                pe.wait_ge(s_td, 5 * NB + t + 1)
                if t == 0:
                    pe.wait_ge(s_td, 6 * NB)
                    pe.wait_ge(s_vtd, NB)
                if t >= 2:
                    pe.wait_ge(s_uwc, t - 1)
                for h in range(H):
                    mm(bank[2 * (t % 2)][:, hs(h)], TT[:, t, hs(h)], vbeta[:, t, hs(h)], start=True, stop=True)
                for h in range(H):
                    last = mm(bank[2 * (t % 2) + 1][:, hs(h)], kbeg[:, t, hs(h)], TT[:, t, hs(h)],
                              start=True, stop=True)
                last.then_inc(s_uw, 1)
            pe.wait_ge(s_uwc, NB)
            for c in range(NCH):
                t = c // 2
                r = slice(CH * (c % 2), CH * (c % 2) + CH)
                tok = slice(c * CH, (c + 1) * CH)
                pe.wait_ge(s_st, c + 1)
                for h in range(H):
                    off = h * HD + CH * (c % 2)
                    last = mm(bank[0][r, hs(h)], wT[:, t, off:off + CH], state[:, hs(h)], start=True, stop=True)
                last.then_inc(s_wS, 1)
                if c >= 2:
                    pe.wait_ge(s_oc, c - 1)
                for h in range(H):
                    last = mm(bank[2 + c % 2][r, hs(h)], qkvT[:, h, tok], state[:, hs(h)], start=True, stop=True)
                last.then_inc(s_qS, 1)
                pe.wait_ge(s_vn, c + 1)
                for h in range(H):
                    last = mm(bank[1][:, hs(h)], kdec[r, t, hs(h)], vnew[r, hs(h)], start=True, stop=True)
                last.then_inc(s_kv, 1)
                for h in range(H):
                    off = h * HD + CH * (c % 2)
                    last = mm(bank[4 + c % 2][r, hs(h)], QKT[r, t, off:off + CH], vnew[r, hs(h)],
                              start=True, stop=True)
                last.then_inc(s_qkv, 1)
            pe.wait_ge(s_on, 1)
            for k in range(KD):
                if k >= 2:
                    pe.wait_ge(s_olo, k - 1)
                for b in range(NB):
                    last = nc.tensor.transpose(bank[6 + k % 2][:, blk(b)], onat[:, b, blk(k)], ident[:])
                last.then_inc(s_oT, 1)
            pe.wait_ge(s_olo, KD)
            for n in range(T_OUT, T_QUERY):
                split_wait(n)
                natural_tile(n % SPLIT, n % 4, bank[0:4] if n < T_OUT + 4 else bank[4:8])
            pe.wait_ge(s_xs, 2)
            for k in range(KD):
                if k >= 2:
                    pe.wait_ge(s_hf, KD + k - 1)
                for b in range(NB):
                    last = nc.tensor.transpose(bank[k % 2][:, blk(b)], xs2[:, b, blk(k)], ident[:])
                last.then_inc(s_xT, 1)
            pe.wait_ge(s_hlo, 2 * KD)

            def key_scores(n):
                pe.wait_ge(s_qT, n + 1)
                if n == 0:
                    pe.wait_ge(s_key, 16)
                if n >= 2:
                    pe.wait_ge(s_S, n - 1)
                for b in range(NB):
                    last = mm(bank[4 + n % 2][:, blk(b)], qTs[:, n % 2, blk(b)], keys[:, n, :],
                              start=True, stop=True)
                last.then_inc(s_qs, 1)

            for n in range(17):
                if n < 16:
                    split_wait(T_QUERY + n)
                    if n >= 4:
                        pe.wait_ge(s_qT, n - 3)
                    column_tile(n % SPLIT, bank[n % 4])
                if n >= 1:
                    key_scores(n - 1)

            pe.wait_ge(s_qT, 16)
            pe.wait_ge(s_S, 16)

            def gate_group(q, slot, ring_free, tok0):
                pe.wait_ge(s_oh, q + 1)
                if ring_free:
                    pe.wait_ge(s_gev, q + 1)
                for tk in range(TOK4):
                    c = slice(tk * P, (tk + 1) * P)
                    mm(bank[4 + slot % 4][:, c], ohJ[:, slot % 2, c], ohIh[:, slot % 2, c],
                       start=True, stop=False)
                    last = mm(bank[4 + slot % 4][:, c], ohJ[:, slot % 2, c], ohIl[:, slot % 2, c],
                              start=False, stop=True)
                last.then_inc(s_gp, 1)

            def down_tiles(t0, count, b=None, first=0):
                def one(i, j, free):
                    t = i * 4 + (t0 + j)
                    pe.wait_ge(s_lo, t + (T_DOWN + 1))
                    if free:
                        pe.wait_ge(s_act, t - 3)
                    column_tile(j % SPLIT, bank[j])
                    if b is not None:
                        for r in range(2):
                            gate_group(i * 8 + (32 * b + 2 * j + r), 2 * j + r, True, None)
                if first:
                    for j in range(4):
                        one(0, j, False)
                with pe.Fori(first, count // 4) as i:
                    for j in range(4):
                        one(i, j, True)

            down_tiles(0, LEAD, first=1)
            for b in range(NB):
                pe.wait_ge(s_pick, b + 1)
                pe.wait_ge(s_gev, RING + 32 * b)
                for v in range(3):
                    last = nc.tensor.transpose(bank[7][:, v * P:(v + 1) * P], pick[:, v, :], ident[:])
                last.then_inc(s_pkT, 1)
                down_tiles(LEAD + b * (BUILD + REST), BUILD, b)
                down_tiles(LEAD + b * (BUILD + REST) + BUILD, REST)
            down_tiles(LEAD + NB * (BUILD + REST), N_TILES - LEAD - NB * (BUILD + REST))

            def up_tile(t, j, start, stop):
                pe.wait_ge(s_lo, t + (T_UP + 1))
                pe.wait_ge(s_clo, t + 1)
                for b in range(NB):
                    a = blk(b)
                    for half in range(2):
                        w = slice(half * 512, (half + 1) * 512)
                        o = bank[2 * b + half][:]
                        mm(o, chi[:, j % 2, a], whi[:, j % SPLIT, w], start=start, stop=False,
                           skip_group_check=True)
                        mm(o, chi[:, j % 2, a], wlo[:, j % SPLIT, w], start=False, stop=False,
                           skip_group_check=True)
                        last = mm(o, clo[:, j % 2, a], whi[:, j % SPLIT, w], start=False, stop=stop,
                                  skip_group_check=True)
                last.then_inc(s_used, 1)

            pe.wait_ge(s_act, N_TILES)
            pe.wait_ge(s_gev, RING + 32 * NB)
            for t in range(4):
                up_tile(t, t, t == 0, False)
            with pe.Fori(1, N_TILES // 4 - 1) as i:
                for j in range(4):
                    up_tile(i * 4 + j, j, False, False)
            for t in range(N_TILES - 4, N_TILES):
                up_tile(t, t % 4, False, t == N_TILES - 1)

        @block.vector
        def _(dve):
            v = nc.vector
            tt, ts, stt = v.tensor_tensor, v.tensor_scalar, v.scalar_tensor_tensor

            def bc(ap16, t):
                return ap16[:, 4 * t:4 * t + 4].unsqueeze(2).to_broadcast([P, H, P])

            dve.wait_ge(s_pool, 1)
            ge = wk[:, 0, 0:P]
            lt = wk[:, 0, P:2 * P]
            same = wk[:, 0, 2 * P:3 * P]
            xo = wk[:, 1, 0:P].bitcast(I32)
            xk = wk[:, 1, P:2 * P].bitcast(I32)
            tt(ge, xij[:, 0, :], xij[:, 1, :], ALU.is_ge)
            tt(lt, xij[:, 0, :], xij[:, 1, :], ALU.is_lt)
            tt(masks[:, M_STRICT, :], xij[:, 0, :], xij[:, 1, :], ALU.is_gt)
            tt(xo, xij[:, 0, :], xij[:, 1, :], ALU.bitwise_xor)
            v.drain()
            ts(same, xo, CH, None, ALU.is_lt)
            v.drain()
            tt(masks[:, M_INCL, :], ge, same, ALU.mult)
            tt(masks[:, M_U, :], lt, same, ALU.mult)
            tt(masks[:, M_STRICT, :], masks[:, M_STRICT, :], same, ALU.mult)
            v.drain()
            tt(masks[:, M_U, :], masks[:, M_U, :], ident[:], ALU.add)
            for k in range(6):
                v.drain()
                ts(xk, xo, k, None, ALU.logical_shift_right)
                v.drain()
                ts(masks[:, MT + k, :], xk, 1, None, ALU.is_equal)
                if k == 0:
                    ts(masks[:, M_FIRST, :], xk, 1, None, ALU.is_equal)
                v.drain()
                tt(masks[:, MT + k, :], masks[:, MT + k, :], lt, ALU.mult)
            tt(masks[:, M_FIRST, :], masks[:, M_FIRST, :], masks[:, M_STRICT, :], ALU.mult)
            v.drain()
            ts(negm[:], rel[:], 0.0, NEG, ALU.is_lt, ALU.mult).then_inc(s_xij, 1)
            dve.wait_ge(s_ssq, NB)

            def inverse_root(wait_root):
                dve.wait_ge(s_rt, wait_root)
                v.reciprocal(rstd, rstd)
                v.drain()

            ts(rstd, ssq, 1.0 / D, EPS, ALU.mult, ALU.add).then_inc(s_msq, 1)
            inverse_root(1)
            for b in range(NB):
                last = ts(xn[:, b, :], xn[:, b, :], rstd[:, b:b + 1], None, ALU.mult)
            last.then_inc(s_xs, 1)

            def mod_columns(half):
                dve.wait_ge(s_modu, 16 * (half + 1))
                ps = bank[7][:, 16 * half:16 * half + 16].rearrange("p (a k) -> p a k", a=2)
                tt(bcol[:, half, :], ps[:, 0, :], modbcol[:, 2 * half, :], ALU.add)
                tt(acol[:, half, :], ps[:, 1, :], modbcol[:, 2 * half + 1, :], ALU.add)
                v.drain()
                stt(out=acol[:, half, :], in0=acol[:, half, :], scalar=1.0, in1=gaincol[:, half, :],
                    op0=ALU.add, op1=ALU.mult).then_inc(s_cols, 1)
                v.drain()

            def shifted(half, buf):
                def low(k):
                    dve.wait_ge(s_hhi, KD * half + k + 1)
                    tt(act_lo[:, k, :], buf[:, k % 2, :], act_hi[:, k, :].bitcast(F32),
                       ALU.subtract).then_inc(s_hlo, 1)
                for k in range(KD):
                    v.drain()
                    dve.wait_ge(s_xT, KD * half + k + 1)
                    ts(buf[:, k % 2, :], bank[k % 2][:], acol[:, half, k:k + 1], bcol[:, half, k:k + 1],
                       ALU.mult, ALU.add).then_inc(s_hf, 1)
                    if k >= 1:
                        v.drain()
                        low(k - 1)
                v.drain()
                low(KD - 1)

            dve.wait_ge(s_c, 16 * 11)
            mod_columns(0)
            shifted(0, wk)

            def gate_group(g):
                buf = (gate_m, gate_f)[g // 2][:, (g % 2) * 512:(g % 2 + 1) * 512]
                gr = gainrow[:, g // 2, (g % 2) * 512:(g % 2 + 1) * 512]
                dve.wait_ge(s_modu, 36 + 4 * g)
                tt(buf, buf, bank[5 + g % 2][:], ALU.add).then_inc(s_gate, 1)
                v.drain()
                tt(buf, buf, gr, ALU.mult)

            for n in range(T_KA):
                dve.wait_ge(s_used, n + 1)
                o = qkvT[:, n, :]
                ts(o, bank[n % 4][:], conv_w[:, n, 3:4], None, ALU.mult)
                for j in (2, 1, 0):
                    s = 3 - j
                    v.drain()
                    last = stt(out=o[:, s:], in0=bank[n % 4][:, 0:SEQ - s], scalar=conv_w[:, n, j:j + 1],
                               in1=o[:, s:], op0=ALU.mult, op1=ALU.add)
                last.then_inc(s_conv, 1)

            def normed(n):
                dve.wait_ge(s_l2r, n + 1)
                r = wk[:, 2 + n % 2, :]
                v.reciprocal(r, r)
                v.drain()
                stt(out=qkvT[:, n, :], in0=qkvT[:, n, :], scalar=HD ** -0.5 if n < 4 else 1.0, in1=r,
                    op0=ALU.mult, op1=ALU.mult).then_inc(s_l2n, 1)

            dve.wait_ge(s_gr, 32)
            gate_group(0)
            gate_group(1)
            mod_columns(1)
            dve.wait_ge(s_hlo, KD)
            for n in range(8):
                dve.wait_ge(s_silu, n + 1)
                if n >= 2:
                    dve.wait_ge(s_l2, n - 1)
                tt(wk[:, n % 2, :], qkvT[:, n, :], qkvT[:, n, :], ALU.mult).then_inc(s_sq, 1)
                if n == 1:
                    gate_group(2)
                    gate_group(3)
                if n >= 1:
                    normed(n - 1)
            normed(7)

            l64 = lam_in.rearrange("p (a n) -> p a n", a=4)
            for m in range(2):
                tt(l64[:, m, :], l64[:, m, :], l64[:, 2 + m, :], ALU.mult)
            v.drain()
            v.tensor_reduce(lam[:, 0:2], l64[:, 0:2, :], AX_X, ALU.add).then_inc(s_lam, 1)
            ts(again, again, 1.0 - LAMBDA_INIT, None, ALU.mult)
            dve.wait_ge(s_lame, 1)
            tt(lam[:, 2:3], lam[:, 0:1], lam[:, 1:2], ALU.subtract)
            v.drain()
            ts(lam[:, 2:3], lam[:, 2:3], LAMBDA_INIT, -1.0, ALU.add, ALU.mult)

            dve.wait_ge(s_ba, 1)
            ba = bank[4][:, 0:32].rearrange("p (t c) -> p t c", t=NB)
            def th(ap):
                return ap.rearrange("p (t h) -> p t h", t=NB)
            v.tensor_copy(th(g16(G_BETA)), ba[:, :, 0:4])
            tt(th(g16(G_Y)), ba[:, :, 4:8], dt4.unsqueeze(1).to_broadcast([P, NB, H]), ALU.add)
            v.drain()
            stt(out=g16(G_AY), in0=g16(G_Y), scalar=-1.0, in1=g16(G_Y), op0=ALU.mult,
                op1=ALU.max).then_inc(s_g1, 1)
            dve.wait_ge(s_g1e, 1)
            ts(g16(G_BETA), g16(G_BETA), 1.0, None, ALU.add)
            stt(out=g16(G_SP), in0=g16(G_Y), scalar=0.0, in1=g16(G_SP), op0=ALU.max, op1=ALU.add)
            v.drain()
            v.reciprocal(g16(G_BETA), g16(G_BETA))
            stt(out=th(g16(G_LOG)), in0=th(g16(G_SP)), scalar=-1.0,
                in1=alog4.unsqueeze(1).to_broadcast([P, NB, H]), op0=ALU.mult, op1=ALU.mult)
            v.drain()
            v.tensor_copy(gB[:], g16(G_LOG).unsqueeze(2).to_broadcast([P, 16, P])).then_inc(s_gB, 1)

            def biased(i):
                h, b = divmod(i, NB)
                n = (b + 1) * P
                if b == 0:
                    stt(out=bias[:, h % 2, :], in0=rel[:], scalar=-(2.0 ** (-8.0 * (h + 1) / H)),
                        in1=negm[:], op0=ALU.mult, op1=ALU.add)
                    v.drain()
                dve.wait_ge(s_sc, i + 1)
                if i >= 2:
                    dve.wait_ge(s_pt, i - 1)
                for m in range(2):
                    v.tensor_tensor_reduce(out=pr[:, i % 2, m, 0:n], in0=bank[2 * (i % 2) + m][:, 0:n],
                                           in1=bias[:, h % 2, 512 - n:512], scale=1.0, scalar=-3e38,
                                           op0=ALU.add, op1=ALU.max, accum_out=asm[:, i % 2, m:m + 1])
                v.drain()
                ts(asm[:, i % 2, 2:4], asm[:, i % 2, 0:2], -1.0, None, ALU.mult).then_inc(s_mx, 1)

            def difference(i):
                n = (i % NB + 1) * P
                dve.wait_ge(s_ex, i + 1)
                a = asm[:, i % 2, 4:6]
                v.reciprocal(a, a)
                v.drain()
                tt(a[:, 1:2], a[:, 1:2], lam[:, 2:3], ALU.mult)
                ts(pr[:, i % 2, 0, 0:n], pr[:, i % 2, 0, 0:n], a[:, 0:1], None, ALU.mult)
                v.drain()
                stt(out=pr[:, i % 2, 0, 0:n], in0=pr[:, i % 2, 1, 0:n], scalar=a[:, 1:2],
                    in1=pr[:, i % 2, 0, 0:n], op0=ALU.mult, op1=ALU.add).then_inc(s_pd, 1)

            def attn_out(i):
                h, b = divmod(i, NB)
                dve.wait_ge(s_av, i + 1)
                v.tensor_copy(onat[:, b, h * HD:(h + 1) * HD], bank[6 + i % 2][:, 0:HD]).then_inc(s_oa, 1)

            v.drain()
            for i in range(H * NB + 3):
                if i < H * NB:
                    biased(i)
                if 1 <= i <= H * NB:
                    difference(i - 1)
                if i >= 3:
                    attn_out(i - 3)

            dve.wait_ge(s_gc, 1)
            v.tensor_copy(g16(G_CUM), bank[7][:, 0:16]).then_inc(s_gcc, 1)
            v.memset(state[:], 0.0).then_inc(s_st, 1)
            v.drain()
            for t in range(NB):
                dve.wait_ge(s_row, t + 1)
                row = by_head(bank[t][:])
                tt(by_head(QKT[:, t, :]), row, bc(g16(G_CUM), t), ALU.subtract)
                for s in range(2):
                    r = slice(CH * s, CH * (s + 1))
                    tt(g16(G_DEC)[r, 4 * t:4 * t + 4], row[r, :, CH * s + CH - 1],
                       g16(G_CUM)[r, 4 * t:4 * t + 4], ALU.subtract)
                    c = 2 * t + s
                    v.tensor_copy(g_last[:, 4 * c:4 * c + 4], row[:, :, CH * s + CH - 1])
                v.drain()
                tt(by_head(LM[:, t, :]), by_head(QKT[:, t, :]), mask4(M_INCL), ALU.mult)
                v.drain()
                tt(by_head(QKT[:, t, :]), by_head(QKT[:, t, :]), mask4(M_U), ALU.mult).then_inc(s_du, 1)
            for t in range(NB):
                dve.wait_ge(s_de, t + 1)
                tt(by_head(LM[:, t, :]), by_head(LM[:, t, :]), mask4(M_STRICT), ALU.mult)
                tt(by_head(QKT[:, t, :]), by_head(QKT[:, t, :]), mask4(M_U), ALU.mult)
                v.drain()
                dve.wait_ge(s_kg, t + 1)
                tt(LM[:, t, :], LM[:, t, :], bank[4 + t % 2][:], ALU.mult)
                tt(QKT[:, t, :], QKT[:, t, :], bank[6 + t % 2][:], ALU.mult)
                v.drain()
                tt(by_head(LM[:, t, :]), by_head(LM[:, t, :]), bc(g16(G_BETA), t),
                   ALU.mult).then_inc(s_L, 1)
                v.drain()
                tt(by_head(PM[:, t, :]), by_head(LM[:, t, :]), mask4(M_FIRST), ALU.mult)
                v.drain()
                tt(by_head(Tm[:, t, :]), ident[:].unsqueeze(1).to_broadcast([P, H, P]),
                   by_head(PM[:, t, :]), ALU.subtract)
            tt(g16(G_BEXP), g16(G_BETA), g16(G_EXP), ALU.mult)
            v.drain()
            for t in range(NB):
                dve.wait_ge(s_LTc, t + 1)
                tt(by_head(PM[:, t, :]), by_head(LT[:, t, :]), mask4(MT), ALU.mult)
                v.drain()
                tt(by_head(TT[:, t, :]), ident[:].unsqueeze(1).to_broadcast([P, H, P]),
                   by_head(PM[:, t, :]), ALU.subtract).then_inc(s_td, 1)
            def scaled_vk(t):
                dve.wait_ge(s_vt, t + 1)
                tt(by_head(vbeta[:, t, :]), by_head(bank[6][:]), bc(g16(G_BETA), t), ALU.mult)
                tt(by_head(kbeg[:, t, :]), by_head(bank[7][:]), bc(g16(G_BEXP), t), ALU.mult)
                tt(by_head(kdec[:, t, :]), by_head(bank[7][:]), bc(g16(G_DEC), t),
                   ALU.mult).then_inc(s_vtd, 1)

            def masked(n):
                k, t = divmod(n, NB)
                if k >= 1:
                    dve.wait_ge(s_pp, n - NB + 1)
                tt(by_head(LM[:, t, :]), by_head(LT[:, t, :]), mask4(MT + 1 + k), ALU.mult).then_inc(s_lm, 1)

            def updated(n):
                k, t = divmod(n, NB)
                dve.wait_ge(s_tt, n + 1)
                if k < 4:
                    tt(Tm[:, t, :], Tm[:, t, :], bank[2 + t % 2][:], ALU.subtract)
                tt(TT[:, t, :], TT[:, t, :], bank[4 + t % 2][:], ALU.subtract).then_inc(s_td, 1)

            for n in range(NB):
                masked(n)
            for t in range(NB):
                scaled_vk(t)
            for n in range(5 * NB):
                updated(n)
                if n + NB < 5 * NB:
                    v.drain()
                    masked(n + NB)

            def chunk_out(c):
                t = c // 2
                r = slice(CH * (c % 2), CH * (c % 2) + CH)
                o = onat[r, t, 512:1024]
                dve.wait_ge(s_qkv, c + 1)
                tt(by_head(o), by_head(bank[2 + c % 2][r, :]),
                   g16(G_EXP)[r, 4 * t:4 * t + 4].unsqueeze(2).to_broadcast([CH, H, P]), ALU.mult)
                v.drain()
                tt(o, o, bank[4 + c % 2][r, :], ALU.add).then_inc(s_oc, 1)

            dve.wait_ge(s_uwc, NB)
            for c in range(NCH):
                t = c // 2
                r = slice(CH * (c % 2), CH * (c % 2) + CH)
                dve.wait_ge(s_wS, c + 1)
                tt(vnew[r, :], u[r, t, :], bank[0][r, :], ALU.subtract).then_inc(s_vn, 1)
                dve.wait_ge(s_qS, c + 1)
                tt(by_head(state[:]), by_head(state[:]),
                   g_last[:, 4 * c:4 * c + 4].unsqueeze(2).to_broadcast([P, H, P]), ALU.mult)
                v.drain()
                dve.wait_ge(s_kv, c + 1)
                tt(state[:], state[:], bank[1][:], ALU.add).then_inc(s_st, 1)
                chunk_out(c)
            v.drain()
            of = onat[:].rearrange("p b n -> p (b n)")
            o32 = of.rearrange("p (m n) -> p m n", n=HD)
            tt(osq[:], of, of, ALU.mult)
            v.drain()
            v.tensor_reduce(o_ms, osq[:].rearrange("p (m n) -> p m n", n=HD), AX_X, ALU.add)
            v.drain()
            ts(o_ms, o_ms, 1.0 / HD, EPS, ALU.mult, ALU.add).then_inc(s_oms, 1)
            dve.wait_ge(s_omr, 1)
            v.reciprocal(o_ms, o_ms)
            v.drain()
            tt(o32, o32, o_ms.unsqueeze(2).to_broadcast([P, 32, HD]), ALU.mult)
            v.drain()
            o4 = onat[:].rearrange("p b (m n) -> p b m n", n=HD)
            for b in range(NB):
                tt(o4[:, b, 0:4, :], o4[:, b, 0:4, :], again.unsqueeze(1).to_broadcast([P, 4, HD]), ALU.mult)
                tt(o4[:, b, 4:8, :], o4[:, b, 4:8, :], ggain.unsqueeze(1).to_broadcast([P, 4, HD]), ALU.mult)
            v.drain()
            tt(onat[:, :, 512:1024], onat[:, :, 512:1024], zs[:], ALU.mult).then_inc(s_on, 1)
            for k in range(KD):
                dve.wait_ge(s_ohi, k + 1)
                tt(act_lo[:, k, :], bank[6 + k % 2][:], act_hi[:, k, :].bitcast(F32),
                   ALU.subtract).then_inc(s_olo, 1)
            dve.wait_ge(s_ssq, NB + 1)
            v.tensor_reduce(rstd, ssq2.rearrange("p (b a) -> p b a", a=2), AX_X, ALU.add)
            v.drain()
            ts(rstd, rstd, 1.0 / D, EPS, ALU.mult, ALU.add).then_inc(s_msq, 1)
            inverse_root(2)
            dve.wait_ge(s_xr, 16 * NB)
            for b in range(NB):
                for half in range(2):
                    w = slice(half * 512, (half + 1) * 512)
                    stt(out=xs2[:, b, w], in0=bank[4 * half + b][:], scalar=rstd[:, b:b + 1],
                        in1=gate_m[:, w], op0=ALU.mult, op1=ALU.mult)
                v.drain()
                tt(xn[:, b, :], xn[:, b, :], xs2[:, b, :], ALU.add).then_inc(s_x1, 1)
            dve.wait_ge(s_ssq, NB + 2)
            ts(rstd, ssq, 1.0 / D, EPS, ALU.mult, ALU.add).then_inc(s_msq, 1)
            inverse_root(3)
            for b in range(NB):
                last = ts(xs2[:, b, :], xn[:, b, :], rstd[:, b:b + 1], None, ALU.mult)
            last.then_inc(s_xs, 1)
            shifted(1, hfl2)
            dve.wait_ge(s_x1o, 16 * NB)
            for n in range(16):
                dve.wait_ge(s_qs, n + 1)
                v.tensor_copy(S[:, :, n, :], bank[4 + n % 2][:].rearrange("p (b n) -> p b n", b=NB)
                              ).then_inc(s_S, 1)

            def top16(vals, idx, src, scratch):
                v.max(vals[:, 0:8], src)
                v.drain()
                v.max_index(idx[:, 0:8], vals[:, 0:8], src)
                v.match_replace(out=scratch, in_to_replace=vals[:, 0:8], in_values=src, imm_value=LOWEST)
                v.drain()
                v.max(vals[:, 8:16], scratch)
                v.drain()
                v.max_index(idx[:, 8:16], vals[:, 8:16], scratch)

            def retrieve(b):
                for n in range(2 * PH):
                    top16(top[:, n, :], topi[:, n, :], S[:, b, n, :], tmp[:, 0:P])
                v.drain()
                v.tensor_copy(topf[:], topi[:])
                for h in range(PH):
                    tt(cand[:, h, :].rearrange("p (a c) -> p a c", a=TOPK),
                       top[:, 2 * h, :].unsqueeze(2).to_broadcast([P, TOPK, TOPK]),
                       top[:, 2 * h + 1, :].unsqueeze(1).to_broadcast([P, TOPK, TOPK]), ALU.add)
                v.drain()
                if b >= 1:
                    dve.wait_ge(s_gexp, b)
                for h in range(PH):
                    top16(best[:, h, :], pos[:, h * TOPK:(h + 1) * TOPK], cand[:, h, :], tmp[:])
                v.drain()
                v.tensor_copy(gsum[:, 0:PH], best[:, :, 0])
                if b >= 1:
                    dve.wait_ge(s_pkT, b)
                v.drain()
                tt(best[:], best[:], gsum[:, 0:PH].unsqueeze(2).to_broadcast([P, PH, TOPK]),
                   ALU.subtract).then_inc(s_best, 1)
                c3 = cand[:].rearrange("p h (k a) -> p h k a", k=TOPK)
                for m, (op, arg) in enumerate([(ALU.logical_shift_right, 4), (ALU.bitwise_and, 15)]):
                    ts(posi[:], pos[:], arg, None, op)
                    v.drain()
                    v.tensor_copy(posf[:], posi[:])
                    v.drain()
                    flat = cand[:].rearrange("p h (k a) -> p (h k) a", k=TOPK)
                    tt(flat, posf[:].unsqueeze(2).to_broadcast([P, P, TOPK]),
                       iota16[:].unsqueeze(1).to_broadcast([P, P, TOPK]), ALU.is_equal)
                    v.drain()
                    half = topf[:].rearrange("p (h c) k -> p h c k", c=2)[:, :, m, :]
                    tt(c3, c3, half.unsqueeze(2).to_broadcast([P, PH, TOPK, TOPK]), ALU.mult)
                    v.drain()
                    v.tensor_reduce(pick[:, m, :], flat, AX_X, ALU.add)
                dve.wait_ge(s_gexp, b + 1)
                g3 = pick[:, 2, :].rearrange("p (h k) -> p h k", h=PH)
                v.tensor_reduce(gsum[:, PH:2 * PH], g3, AX_X, ALU.add)
                v.drain()
                v.reciprocal(gsum[:, PH:2 * PH], gsum[:, PH:2 * PH])
                v.drain()
                tt(g3, g3, gsum[:, PH:2 * PH].unsqueeze(2).to_broadcast([P, PH, TOPK]),
                   ALU.mult).then_inc(s_pick, 1)
                dve.wait_ge(s_pkT, b + 1)
                v.tensor_copy(pickT[:, 0:2, :], bank[7][:, 0:2 * P].rearrange("p (a n) -> p a n", a=2))
                v.tensor_copy(gTh[:], bank[7][:, 2 * P:3 * P])
                v.drain()
                tt(pickT[:, 3, :], bank[7][:, 2 * P:3 * P], gTh[:].bitcast(F32), ALU.subtract)
                v.tensor_copy(pickT[:, 2, :], gTh[:].bitcast(F32)).then_inc(s_pkc, 1)
                v.drain()

            def onehots(b):
                def one(i, r, free):
                    q = i * 2 + (32 * b + r)
                    tok = bass.ds(i * 8 + r * TOK4, TOK4)

                    def spread(row):
                        return pickT[:, row, tok].unsqueeze(2).to_broadcast([P, TOK4, P])
                    lane = iotaN[:].unsqueeze(1).to_broadcast([P, TOK4, P])

                    def by_tok(ap):
                        return ap.rearrange("p (t n) -> p t n", t=TOK4)
                    v.drain()
                    if free:
                        dve.wait_ge(s_gp, q - 1)
                    tt(by_tok(ohE[:]), lane, spread(0), ALU.is_equal)
                    tt(by_tok(ohJ[:, r, :]), lane, spread(1), ALU.is_equal)
                    v.drain()
                    tt(by_tok(ohIh[:, r, :]), by_tok(ohE[:]), spread(2), ALU.mult)
                    tt(by_tok(ohIl[:, r, :]), by_tok(ohE[:]), spread(3), ALU.mult).then_inc(s_oh, 1)
                if b == 0:
                    for r in range(2):
                        one(0, r, False)
                with dve.Fori(1 if b == 0 else 0, 16) as i:
                    for r in range(2):
                        one(i, r, True)

            for b in range(NB):
                retrieve(b)
                onehots(b)

            def up_tile(t, j, free):
                def low():
                    dve.wait_ge(s_chi, t + 1)
                    tt(clo[:, j % 2, :], coef[:, j % 2, :], chi[:, j % 2, :].bitcast(F32),
                       ALU.subtract).then_inc(s_clo, 1)
                dve.wait_ge(s_ain[j], (t - j) * 4 + 16)
                dve.wait_ge(s_gin[j], (t - j) * 4 + 16)
                tt(coef[:, j % 2, :], a_in[:, j, :], g_in[:, j, :], ALU.mult).then_inc(s_cf, 1)
                v.drain()
                low()

            for t in range(4):
                up_tile(t, t, t >= 2)
            with dve.Fori(1, N_TILES // 4) as i:
                for j in range(4):
                    up_tile(i * 4 + j, j, True)
            dve.wait_ge(s_yq, 1)
            v.tensor_reduce(rstd, ssq2.rearrange("p (b a) -> p b a", a=2), AX_X, ALU.add)
            v.drain()
            ts(rstd, rstd, 1.0 / D, EPS, ALU.mult, ALU.add).then_inc(s_ym, 1)
            dve.wait_ge(s_yr, 1)
            v.reciprocal(rstd, rstd)
            v.drain()
            dve.wait_ge(s_x1l, 16 * NB)
            for b in range(NB):
                for half in range(2):
                    w = slice(half * 512, (half + 1) * 512)
                    stt(out=yo[:, b, w], in0=bank[2 * b + half][:], scalar=rstd[:, b:b + 1],
                        in1=gate_f[:, w], op0=ALU.mult, op1=ALU.mult)
                v.drain()
                tt(yo[:, b, :], yo[:, b, :], x1[:, b, :], ALU.add).then_inc(s_yo, 1)


def kernel(**inputs):
    import numpy as np
    import concourse.bacc as bacc
    from concourse import mybir as mb
    from concourse.bass_utils import run_bass_kernel_spmd

    a = {k: np.asarray(v) for k, v in inputs.items()}
    w_mod = a["w_mod"][0].reshape(KD, P, 6, D)
    b_mod = a["b_mod"][0].reshape(6, KD, P)

    def column_tiles(w):
        n = w.shape[1] // P
        return w.reshape(KD, P, n, P).transpose(2, 1, 0, 3).reshape(n, P, D)

    def natural_tiles(w):
        n = w.shape[1] // 512
        return w.reshape(4, 2, P, n, 512).transpose(3, 0, 2, 1, 4).reshape(4 * n, P, D)

    w_in = a["w_in"][0]
    A = 512
    qa, ka, va = w_in[:, 0:A], w_in[:, A:2 * A], w_in[:, 2 * A:3 * A]
    qkv, z = w_in[:, 3 * A:6 * A], w_in[:, 6 * A:7 * A]
    ba = w_in[:, 7 * A:7 * A + 2 * H]
    down = a["expert_down"][0].reshape(N_TILES, P, KD, P).transpose(0, 3, 2, 1).reshape(N_TILES, P, D)
    up = a["expert_up"][0].reshape(N_TILES, P, D)
    arrays = {
        "x": a["x"].reshape(NB, P, D),
        "c_col": a["c"].reshape(KD, P).T,
        "mod_tiles": np.concatenate([column_tiles(w_mod[:, :, m].reshape(D, D)) for m in (0, 1, 3, 4)]
                                    + [natural_tiles(w_mod[:, :, m].reshape(D, D)) for m in (2, 5)]),
        "mod_bias_col": b_mod[[0, 1, 3, 4]].transpose(2, 0, 1),
        "gate_bias_rows": b_mod[[2, 5]].reshape(2, D),
        "gain_cols": np.stack([a["pre_mix_gain"][0], a["pre_ffn_gain"][0]]).reshape(2, KD, P).transpose(2, 0, 1),
        "gain_rows": np.concatenate([a["post_mix_gain"], a["post_ffn_gain"]]),
        "in_tiles": np.concatenate([column_tiles(qkv), column_tiles(ka), column_tiles(qa),
                                    natural_tiles(va), natural_tiles(z)]),
        "ba_w": ba.reshape(KD, P, 2 * H).transpose(1, 0, 2),
        "conv_col": a["conv_w"][0].reshape(4, 12, P).transpose(2, 1, 0).reshape(P, 48),
        "a_log": a["a_log"][0],
        "dt_bias": a["dt_bias"][0],
        "lambdas": np.concatenate([a[f"lambda_{n}"][0] for n in ("q1", "q2", "k1", "k2")]),
        "head_gains": np.concatenate([a["attn_norm_gain"][0], a["gdn_norm_gain"][0]]),
        "out_tiles": natural_tiles(a["w_out"][0]),
        "query_tiles": column_tiles(a["w_query"][0]),
        "keys_t": a["sub_keys"][0].reshape(2 * PH, P, P).transpose(2, 0, 1),
        "expert_tiles": np.concatenate([down, up]),
    }
    nc = bacc.Bacc("TRN2", target_bir_lowering=False, num_devices=1)
    feed, args = {}, []
    for name, v in arrays.items():
        v = np.ascontiguousarray(v)
        feed[f"in_{name}"] = v
        args.append(nc.dram_tensor(f"in_{name}", v.shape, mb.dt.from_np(v.dtype), kind="ExternalInput").ap())
    out = nc.dram_tensor("out", (NB, P, D), mb.dt.from_np(np.dtype("float32")), kind="ExternalOutput").ap()
    build(nc, *args, out)
    r = run_bass_kernel_spmd(nc, [feed], core_ids=[0])
    return r.results[0]["out"].reshape(1, SEQ, D)
```

```python
import math
from contextlib import ExitStack

import concourse.bass as bass
from concourse import mybir

F32 = mybir.dt.float32
F32R = mybir.dt.float32r
BF16 = mybir.dt.bfloat16
I32 = mybir.dt.int32
U32 = mybir.dt.uint32
ALU = mybir.AluOpType
ACT = mybir.ActivationFunctionType
AX_X = mybir.AxisListType.X

P = 128
D = 1024
SEQ = 512
KD = D // P
NB = SEQ // P
H = 4
HD = 128
QK = 64
CH = 64
NCH = SEQ // CH
EPS = 1e-6
NEG = -1e30
LOWEST = -3.4e38
LAMBDA_INIT = 0.8 - 0.6 * math.exp(0.0)
PH = 8
TOPK = 16
N_TILES = 128

T_VA, T_Z, T_KQ, T_GDN, T_OUT, T_QUERY = 0, 4, 8, 16, 28, 36
SLOT0 = T_KQ + 2
N_MOD = 48
T_DOWN = 52
T_UP = T_DOWN + N_TILES
T_ALL = T_UP + N_TILES
RAW = 4
SPLIT = 2
AHEAD = RAW + 1

LEAD, BUILD, REST = 12, 16, 12
STORE = 8
RING = 4
OH = 4
TOK4 = 4


def mod_order(m):
    half, r = divmod(m, 24)
    return (3 * half + r % 2, r // 2) if r < 16 else (3 * half + 2, r - 16)


def build(nc, x, c, mod_tiles, mod_bias_col, gain_cols, in_tiles,
          ba_w, conv_col, a_log, dt_bias, lambdas, head_gains, out_tiles, query_tiles, keys_t,
          expert_tiles, out):
    act_dram = nc.dram_tensor("act_scratch", (N_TILES, P, SEQ), F32).ap()
    gate_dram = nc.dram_tensor("gate_scratch", (N_TILES, P, SEQ), F32).ap()
    x1_dram = nc.dram_tensor("x1_scratch", (NB, P, D), F32).ap()
    with ExitStack() as ctx:
        def sem(name):
            return ctx.enter_context(nc.semaphore(name))

        cursor = [17408]

        def at(name, shape, dt, offset=None):
            size = 2 if dt == BF16 else 4
            for n in shape[1:]:
                size *= n
            offset = cursor[0] if offset is None else offset
            cursor[0] = offset + (size + 31) // 32 * 32
            assert cursor[0] <= 229344, (name, cursor[0])
            return nc.alloc_sbuf_tensor_at(name, shape, dt, offset=offset)

        ident = at("ident", [P, P], F32)
        acol = at("acol", [P, 2, KD], F32)
        bcol = at("bcol", [P, 2, KD], F32)
        gaincol = at("gaincol", [P, 4, KD], F32)
        modbcol = at("modbcol", [P, 6, KD], F32)
        small = at("small", [P, 64], F32)
        iota16 = at("iota16", [P, TOPK], F32)
        iotaN = at("iotaN", [P, P], F32)
        gate_m = at("gate_m", [P, D], F32)
        gate_f = at("gate_f", [P, D], F32)
        raw = at("raw", [P, RAW, D], F32)
        whi = at("whi", [P, SPLIT, D], F32R)
        wlo = at("wlo", [P, SPLIT, D], F32R)
        acts = cursor[0]
        act_hi = at("act_hi", [P, KD, SEQ], F32R)
        act_lo = at("act_lo", [P, KD, SEQ], F32R)
        phase = cursor[0]

        xn = at("xn", [P, NB, D], F32)
        kbeg = at("kbeg", [P, NB, 512], F32, phase)
        kdec = at("kdec", [P, NB, 512], F32)
        modx = at("modx", [P, 4, D], F32, phase)
        l2r = at("l2r", [P, 8, SEQ], F32, phase)
        modr = at("modr", [P, 4, D], F32)
        onat = at("onat", [P, NB, D], F32, cursor[0] - 4 * D * 4)
        xs2 = at("xs2", [P, NB, D], F32, cursor[0] - 4 * D * 4)
        kq = cursor[0]
        kaT = at("kaT", [P, H, SEQ], F32)
        qaT = at("qaT", [P, H, SEQ], F32)
        osq = at("osq", [P, NB * D], F32, kq)
        va = at("va", [P, NB, 512], F32)
        zs = at("zs", [P, NB, 512], F32)
        qkvT = at("qkvT", [P, 12, SEQ], F32)
        u = at("u", [P, NB, 512], F32, cursor[0] - 4 * SEQ * 4)
        t_base = cursor[0]
        Tm = at("Tm", [P, NB, 512], F32)
        TT = at("TT", [P, NB, 512], F32)
        PM = at("PM", [P, NB, 512], F32)
        after_t = cursor[0]
        bias = at("bias", [P, 2, 512], F32, t_base)
        pr = at("pr", [P, 2, 2, 512], F32)
        pT = at("pT", [P, 2, 512], F32)
        rel = at("rel", [P, 512], F32)
        negm = at("negm", [P, 512], F32)
        wk = at("wk", [P, 4, 512], F32, t_base + 2 * 512 * 4)
        vbeta = at("vbeta", [P, NB, 512], F32, after_t)
        c_row = at("c_row", [P, D], F32, after_t + D * 4)
        masks = at("masks", [P, 10, P], F32)
        state = at("state", [P, 512], F32)
        vnew = at("vnew", [P, 512], F32)
        ones = at("ones", [P, P], F32, cursor[0] - 512 * 4)
        mrow = at("mrow", [P, 576], F32, cursor[0] + 3 * P * 4)
        gsm = at("gsm", [P, 288], F32)
        baw = at("baw", [P, KD, 8], F32)
        modcol = at("modcol", [P, 6, KD], F32)
        gcol = at("gcol", [P, 2, KD], F32)
        baT = at("baT", [8, SEQ], F32, kq + 2 * H * SEQ * 4 - SEQ * 4)
        baw_hi = at("baw_hi", [P, KD, 8], F32R, after_t + 2048)
        baw_lo = at("baw_lo", [P, KD, 8], F32R)
        xij = at("xij", [P, 2, P], I32, after_t)
        LT = at("LT", [P, NB, 512], F32, acts)
        LM = at("LM", [P, NB, 512], F32)
        QKT = at("QKT", [P, NB, 512], F32)
        wT = at("wT", [P, NB, 512], F32)
        gB = at("gB", [P, 16, P], F32, cursor[0] - NB * 512 * 4)

        M_INCL, M_STRICT, M_U, M_FIRST, MT = 0, 1, 2, 3, 4

        def mask4(m):
            return masks[:, m, :].unsqueeze(1).to_broadcast([P, H, P])

        def by_head(ap):
            return ap.rearrange("p (h n) -> p h n", h=H)

        conv_w = mrow[:, 0:48].rearrange("p (n j) -> p n j", n=12)
        again = mrow[:, 48:176]
        ggain = mrow[:, 176:304]
        lam_in = mrow[:, 304:560]
        lam = mrow[:, 560:564]
        eps_t = small[:, 0:1]
        ssq = small[:, 4:8]
        rstd = small[:, 8:12]
        ssq2 = small[:, 32:40]
        asm = small[:, 40:52].rearrange("p (s v) -> p s v", s=2)
        mark = small[:, 56:57]
        G_BETA, G_Y, G_AY, G_SP, G_CUM, G_EXP, G_DEC, G_BEXP, G_LOG = range(9)

        def g16(i):
            return gsm[:, 16 * i:16 * i + 16]

        g_last = gsm[:, 144:176]
        o_ms = gsm[:, 176:208]
        alog4 = gsm[:, 208:212]
        dt4 = gsm[:, 212:216]

        bank = [ctx.enter_context(nc.psum_tensor(f"bank{i}", [P, 512], F32)) for i in range(8)]

        cursor[0] = phase
        S = at("S", [P, NB, 2 * PH, P], F32)
        stage = at("stage", [P, P, P], F32)
        keys = at("keys", [P, 2 * PH, P], F32, cursor[0] - P * P * 4)
        qTs = at("qTs", [P, 2, SEQ], F32)
        hfl2 = at("hfl2", [P, 2, SEQ], F32)
        cursor[0] = phase + (32 + 64) * 1024
        aout = at("aout", [P, 2, SEQ], F32)
        cand_at = cursor[0]
        cand = at("cand", [P, PH, 256], F32)
        top = at("top", [P, 2 * PH, TOPK], F32)
        topi = at("topi", [P, 2 * PH, TOPK], U32)
        topf = at("topf", [P, 2 * PH, TOPK], F32)
        best = at("best", [P, PH, TOPK], F32)
        pos = at("pos", [P, P], U32)
        posi = at("posi", [P, P], U32)
        posf = at("posf", [P, P], F32)
        pick = at("pick", [P, 3, P], F32)
        gsum = at("gsum", [P, 2 * PH], F32)
        pickT = at("pickT", [P, 4, P], F32)
        gTh = at("gTh", [P, P], F32R)
        ohJ = at("ohJ", [P, OH, TOK4 * P], F32R)
        ohIh = at("ohIh", [P, OH, TOK4 * P], F32R)
        ohIl = at("ohIl", [P, OH, TOK4 * P], F32R, cand_at)

        def ohE(b, slot):
            return S[:, b, slot * TOK4:(slot + 1) * TOK4, :]
        cursor[0] = phase
        a_in = at("a_in", [P, RAW, SEQ], F32)
        g_in = at("g_in", [P, RAW, SEQ], F32)
        coef = at("coef", [P, 2, SEQ], F32)
        chi = at("chi", [P, 2, SEQ], F32R)
        clo = at("clo", [P, 2, SEQ], F32R)
        x1 = at("x1", [P, NB, D], F32)
        yo = at("yo", [P, NB, D], F32)

        s_raw = [sem(f"raw_landed{i}") for i in range(RAW)]
        s_hi = sem("split_hi_ready")
        s_lo = sem("split_lo_ready")
        s_used = sem("split_used")
        s_x = sem("x_landed")
        s_crow = sem("c_landed")
        s_c = sem("consts_landed")
        s_hc = sem("head_consts_landed")
        s_modl = [sem(f"mod_landed{i}") for i in range(4)]
        s_modu = sem("mod_used")
        s_pool = sem("pool_consts")
        s_xij = sem("masks_made")
        s_cc = sem("c_silu")
        s_cols = sem("mod_columns_read")
        s_ssq = sem("sum_of_squares")
        s_msq = sem("mean_square")
        s_rt = sem("root")
        s_xs = sem("x_scaled")
        s_xT = sem("x_transposed")
        s_hf = sem("h_float")
        s_hhi = sem("h_hi")
        s_hlo = sem("h_lo")
        s_conv = sem("conv_done")
        s_silu = sem("silu_done")
        s_kq = sem("attn_kq_copied")
        s_nat = sem("natural_tiles_copied")
        s_ba = sem("ba_done")
        s_gcol = sem("gate_columns")
        s_gsp = sem("gate_rows")
        s_gate = sem("gate_rows_copied")
        s_bas = sem("ba_weights_split")
        s_baT = sem("ba_columns")
        s_bac = sem("ba_columns_copied")
        s_sq = sem("qk_squares")
        s_l2 = sem("qk_norm_sums")
        s_l2r = sem("qk_norm_roots")
        s_l2e = sem("qk_inverse_norms")
        s_l2n = sem("qk_normed")
        s_lam = sem("lambda_sums")
        s_lame = sem("lambda_exp")
        s_sc = sem("attn_scores")
        s_mx = sem("attn_max")
        s_ex = sem("attn_exp")
        s_pd = sem("attn_diff")
        s_pt = sem("attn_transposed")
        s_ptc = sem("attn_transposed_copied")
        s_av = sem("attn_values")
        s_oa = sem("attn_out_copied")
        s_g1 = sem("gdn_rows")
        s_g1e = sem("gdn_rows_exp")
        s_gl = sem("gdn_log_decay")
        s_gB = sem("gdn_decay_spread")
        s_gc = sem("gdn_cumsum")
        s_gcc = sem("gdn_cumsum_copied")
        s_row = sem("gdn_decay_rows")
        s_du = sem("gdn_decay_args")
        s_de = sem("gdn_decay_exp")
        s_kg = sem("gdn_grams")
        s_L = sem("gdn_L")
        s_LT = sem("gdn_L_transposed")
        s_LTc = sem("gdn_LT_copied")
        s_t0 = sem("inv_first_T")
        s_vt = sem("gdn_vk_transposed")
        s_vtd = sem("gdn_vk_scaled")
        s_lm = sem("inv_masked")
        s_pp = sem("inv_P")
        s_pc = sem("inv_P_copied")
        s_tt = sem("inv_update")
        s_td = sem("inv_T_ready")
        s_uw = sem("gdn_uw")
        s_uwc = sem("gdn_uw_copied")
        s_st0 = sem("scan_state_cleared")
        s_wS = sem("scan_wS")
        s_qS = sem("scan_qS")
        s_vn = sem("scan_vnew")
        s_kv = sem("scan_kv")
        s_qkv = sem("scan_qkv")
        s_st = sem("scan_state")
        s_oc = sem("scan_out_copied")
        s_oms = sem("head_mean_squares")
        s_omr = sem("head_roots")
        s_on = sem("heads_normed")
        s_oT = sem("o_transposed")
        s_ohi = sem("o_hi")
        s_olo = sem("o_lo")
        s_xr = sem("x_again_landed")
        s_x1 = sem("x1_ready")
        s_x1o = sem("x1_stored")
        s_key = sem("keys_landed")
        s_qT = sem("query_copied")
        s_qs = sem("key_scores")
        s_S = sem("key_scores_copied")
        s_act = sem("gelu_done")
        s_ast = [sem(f"act_stored{i}") for i in range(2)]
        s_best = sem("topk_best")
        s_gexp = sem("topk_exp")
        s_pick = sem("picks_ready")
        s_pkT = sem("picks_transposed")
        s_pkc = sem("picks_copied")
        s_oh = sem("onehots_ready")
        s_ohl = sem("onehots_low_ready")
        s_gp = sem("gate_products")
        s_gev = sem("gates_staged")
        s_gst = sem("gates_stored")
        s_ain = [sem(f"act_landed{i}") for i in range(RAW)]
        s_gin = [sem(f"gates_landed{i}") for i in range(RAW)]
        s_cf = sem("coef_ready")
        s_chi = sem("coef_hi")
        s_clo = sem("coef_lo")
        s_x1l = sem("x1_landed")
        s_yq = sem("y_squares")
        s_ym = sem("y_mean_square")
        s_yr = sem("y_root")
        s_yo = sem("out_ready")
        s_out = sem("out_stored")

        def raw_wait(eng, n):
            eng.wait_ge(s_raw[n % RAW], 16 * (n // RAW + 1))

        block = ctx.enter_context(nc.Block())

        @block.sync
        def _(sp):
            dq = sp.dma_start
            dq(c_row[:], c.partition_broadcast(P)).then_inc(s_crow, 16)
            for b in range(NB):
                dq(xn[:, b, :], x[b]).then_inc(s_x, 16)
            for dst, src in [(gaincol[:], gain_cols), (modbcol[:], mod_bias_col), (baw[:], ba_w)]:
                dq(dst, src).then_inc(s_c, 16)

            def load_mod(m):
                if m >= 4:
                    sp.wait_ge(s_modu, m - 3)
                if m == 16:
                    sp.wait_ge(s_xT, KD)
                ring = modr if m < 16 else modx
                dq(ring[:, m % 4, :], mod_tiles[m]).then_inc(s_modl[m % 4], 16)

            def load_raw(n, src):
                if n >= RAW:
                    sp.wait_ge(s_lo, n - RAW + 1)
                dq(raw[:, n % RAW, :], src).then_inc(s_raw[n % RAW], 16)

            for m in range(16):
                load_mod(m)
                if m in (5, 7, 9, 11):
                    load_raw((m - 5) // 2, in_tiles[(m - 5) // 2])
            for dst, src in [(mrow[:, 0:48], conv_col),
                             (mrow[:, 48:304], head_gains.partition_broadcast(P)),
                             (alog4, a_log.partition_broadcast(P)),
                             (dt4, dt_bias.partition_broadcast(P)),
                             (lam_in, lambdas.partition_broadcast(P))]:
                dq(dst, src).then_inc(s_hc, 16)
            for n in range(4, T_OUT):
                load_raw(n, in_tiles[n])
                for m in range(2 * n + 8, min(2 * n + 10, N_MOD)):
                    load_mod(m)
            for n in range(8):
                load_raw(T_OUT + n, out_tiles[n])
            sp.wait_ge(s_on, 1)
            for b in range(NB):
                dq(xn[:, b, :], x[b]).then_inc(s_xr, 16)
            for n in range(4):
                load_raw(T_QUERY + n, query_tiles[n])
            sp.wait_ge(s_x1, NB)
            for b in range(NB):
                dq(x1_dram[b], xn[:, b, :]).then_inc(s_x1o, 16)
            sp.wait_ge(s_hlo, 2 * KD)
            sp.wait_ge(s_x1o, 16 * NB)
            dq(keys[:], keys_t).then_inc(s_key, 16)
            for n in range(4, 16):
                load_raw(T_QUERY + n, query_tiles[n])

            for n in range(AHEAD):
                load_raw(T_DOWN + n, expert_tiles[n])

            def down_tiles(t0, count, gates_of=None):
                with sp.Fori(0, count // 4) as i:
                    for j in range(4):
                        t = i * 4 + (t0 + j)
                        sp.wait_ge(s_act, t + 1)
                        dq(act_dram[t], aout[:, j % 2, :]).then_inc(s_ast[j % 2], 16)
                        sp.wait_ge(s_lo, t + (T_DOWN + AHEAD - RAW + 1))
                        slot = (T_DOWN + AHEAD + j) % RAW
                        dq(raw[:, slot, :], expert_tiles[t + AHEAD]).then_inc(s_raw[slot], 16)
                        if gates_of is not None:
                            e = i * 64 + j * 16
                            dq(gate_dram[bass.ds(e, 16), :, gates_of * P:(gates_of + 1) * P]
                               .rearrange("i j t -> j i t"), stage[:, bass.ds(e, 16), :]).then_inc(s_gst, 16)

            down_tiles(0, LEAD)
            for b in range(NB):
                down_tiles(LEAD + b * (BUILD + REST), BUILD)
                sp.wait_ge(s_gev, RING + 32 * (b + 1))
                down_tiles(LEAD + b * (BUILD + REST) + BUILD, STORE, b)
                down_tiles(LEAD + b * (BUILD + REST) + BUILD + STORE, REST - STORE)
            down_tiles(LEAD + NB * (BUILD + REST), N_TILES - LEAD - NB * (BUILD + REST))

            sp.wait_ge(s_gst, 16 * STORE * NB)
            for r in range(2):
                sp.wait_ge(s_ast[r], 16 * (N_TILES // 2))
            for r in range(RAW):
                dq(a_in[:, r, :], act_dram[r]).then_inc(s_ain[r], 16)
                dq(g_in[:, r, :], gate_dram[r]).then_inc(s_gin[r], 16)
            for b in range(NB):
                dq(x1[:, b, :], x1_dram[b]).then_inc(s_x1l, 16)

            def up_tile(t, j, more):
                slot = (T_UP + AHEAD + j) % RAW
                if more:
                    sp.wait_ge(s_lo, t + (T_UP + AHEAD - RAW + 1))
                    dq(raw[:, slot, :], expert_tiles[t + (N_TILES + AHEAD)]).then_inc(s_raw[slot], 16)
                sp.wait_ge(s_cf, t + 1)
                dq(a_in[:, j, :], act_dram[t + RAW]).then_inc(s_ain[j], 16)
                dq(g_in[:, j, :], gate_dram[t + RAW]).then_inc(s_gin[j], 16)

            with sp.Fori(0, N_TILES // 4 - 2) as i:
                for j in range(4):
                    up_tile(i * 4 + j, j, True)
            for t in range(N_TILES - 8, N_TILES - 4):
                up_tile(t, t % 4, t + AHEAD < N_TILES)
            for b in range(NB):
                sp.wait_ge(s_yo, b + 1)
                dq(out[b], yo[:, b, :]).then_inc(s_out, 16)
            sp.wait_ge(s_out, 16 * NB)

        @block.gpsimd
        def _(pool):
            g = nc.gpsimd
            g.memset(ident[:], 0.0)
            g.memset(ones[:], 1.0)
            g.memset(small[:, 0:1], EPS)
            g.iota(xij[:, 0, :], pattern=[[0, P]], base=0, channel_multiplier=1)
            g.iota(xij[:, 1, :], pattern=[[1, P]], base=0, channel_multiplier=0)
            g.iota(rel[:], pattern=[[-1, 512]], base=384, channel_multiplier=1,
                   allow_small_or_imprecise_dtypes=True)
            g.iota(iota16[:], pattern=[[1, TOPK]], base=0, channel_multiplier=0,
                   allow_small_or_imprecise_dtypes=True)
            g.iota(iotaN[:], pattern=[[1, P]], base=0, channel_multiplier=0,
                   allow_small_or_imprecise_dtypes=True)
            g.drain()
            g.affine_select(out=ident[:], in_=ident[:], compare_op=ALU.not_equal, fill=1.0, base=0,
                            pattern=[[-1, P]], channel_multiplier=1).then_inc(s_pool, 1)
            def lo(n, j):
                pool.wait_ge(s_hi, n + 1)
                g.tensor_tensor(wlo[:, j % SPLIT, :], raw[:, j % RAW, :],
                                whi[:, j % SPLIT, :].bitcast(F32), ALU.subtract).then_inc(s_lo, 1)

            def lows(t0, t1):
                with pool.Fori(0, (t1 - t0) // RAW) as i:
                    for j in range(RAW):
                        lo(i * RAW + (t0 + j), t0 + j)

            def lows_and_onehots(t0, b):
                with pool.Fori(0, BUILD // RAW) as i:
                    for j in range(RAW):
                        lo(i * RAW + (t0 + j), t0 + j)
                        for r in range(2):
                            slot = 2 * j + r
                            pool.wait_ge(s_oh, i * 8 + (32 * b + slot + 1))
                            tok = bass.ds(i * 32 + slot * TOK4, TOK4)
                            g.tensor_tensor(ohIl[:, slot % OH, :].rearrange("p (t n) -> p t n", t=TOK4),
                                            ohE(b, slot % OH),
                                            pickT[:, 3, tok].unsqueeze(2).to_broadcast([P, TOK4, P]),
                                            ALU.mult).then_inc(s_ohl, 1)

            first = T_DOWN + LEAD
            lows(0, first)
            lo(first, first)
            for b in range(NB):
                t = first + 1 + b * (BUILD + REST)
                lows_and_onehots(t, b)
                lows(t + BUILD, t + BUILD + REST)
            t += BUILD + REST
            lows(t, T_ALL - 3)
            for n in range(T_ALL - 3, T_ALL):
                lo(n, n)

        @block.scalar
        def _(act):
            sc = nc.scalar

            def hi(n):
                raw_wait(act, n)
                if n >= SPLIT:
                    act.wait_ge(s_used, n - SPLIT + 1)
                sc.copy(whi[:, n % SPLIT, :], raw[:, n % RAW, :]).then_inc(s_hi, 1)

            act.wait_ge(s_crow, 16)
            sc.activation(c_row[:], c_row[:], ACT.Silu).then_inc(s_cc, 1)
            act.wait_ge(s_x, 16 * NB)
            for b in range(NB):
                sc.activation(qkvT[:, 0:2, :], xn[:, b, :].rearrange("p (a n) -> p a n", a=2),
                              ACT.Square, accum_out=ssq[:, b:b + 1]).then_inc(s_ssq, 1)
                act.wait_ge(s_ssq, b + 1)
            act.wait_ge(s_msq, 1)
            sc.activation(rstd, rstd, ACT.Sqrt).then_inc(s_rt, 1)
            act.wait_ge(s_c, 16 * 3)
            sc.copy(baw_hi[:], baw[:]).then_inc(s_bas, 1)
            act.wait_ge(s_xij, 1)

            def shifted(half, buf):
                for k in range(KD + 1):
                    if k < KD:
                        act.wait_ge(s_xT, KD * half + k + 1)
                        act.wait_ge(s_cols, k // 2 + 1 if half == 0 else 5)
                        if k >= 2:
                            act.wait_ge(s_hlo, KD * half + k - 1)
                        sc.activation(buf[:, k % 2, :], bank[(6, 0)[half] + k % 2][:], ACT.Identity,
                                      bias=bcol[:, half, k:k + 1],
                                      scale=acol[:, half, k:k + 1]).then_inc(s_hf, 1)
                    if k >= 1:
                        act.wait_ge(s_hf, KD * half + k)
                        sc.copy(act_hi[:, k - 1, :], buf[:, (k - 1) % 2, :]).then_inc(s_hhi, 1)
                    if half == 0 and k in (3, 5):
                        hi((k - 3) // 2)

            shifted(0, wk)
            for n in range(T_VA, T_Z):
                hi(n + 2)
            act.wait_ge(s_used, T_Z)
            for b in range(NB):
                sc.copy(va[:, b, :], bank[b][:]).then_inc(s_nat, 1)
            for n in range(T_Z, T_KQ):
                hi(n + 2)
            act.wait_ge(s_used, T_KQ)
            for b in range(NB):
                sc.activation(zs[:, b, :], bank[4 + b][:], ACT.Silu).then_inc(s_nat, 1)

            def kq_copy(n):
                act.wait_ge(s_used, n + 1)
                h = (n - T_KQ) // 2
                dst, scale = (qaT, QK ** -0.5) if (n - T_KQ) % 2 else (kaT, 1.0)
                sc.mul(dst[:, h, :], bank[n % 2][:], scale).then_inc(s_kq, 1)

            hi(T_KQ + 2)
            kq_copy(T_KQ)
            hi(T_KQ + 3)
            kq_copy(T_KQ + 1)
            act.wait_ge(s_lam, 1)
            sc.activation(lam[:, 0:2], lam[:, 0:2], ACT.Exp).then_inc(s_lame, 1)
            act.wait_ge(s_g1, 1)
            sc.activation(g16(G_BETA), g16(G_BETA), ACT.Exp, scale=-1.0)
            sc.activation(g16(G_SP), g16(G_AY), ACT.Exp, scale=-1.0)
            sc.activation(alog4, alog4, ACT.Exp)
            sc.drain()
            sc.activation(g16(G_SP), g16(G_SP), ACT.Ln, bias=1.0).then_inc(s_g1e, 1)

            def exps(i):
                act.wait_ge(s_mx, i + 1)
                n = (i % NB + 1) * P
                for m in range(2):
                    last = sc.activation(pr[:, i % 2, m, 0:n], pr[:, i % 2, m, 0:n], ACT.Exp,
                                         bias=asm[:, i % 2, 2 + m:3 + m],
                                         accum_out=asm[:, i % 2, 4 + m:5 + m])
                last.then_inc(s_ex, 1)

            def copy_t(i):
                act.wait_ge(s_pt, i + 1)
                if i >= 2:
                    act.wait_ge(s_av, i - 1)
                n = (i % NB + 1) * P
                sc.copy(pT[:, i % 2, 0:n], bank[6][:, 0:n]).then_inc(s_ptc, 1)

            for s in range(T_OUT - SLOT0):
                hi(SLOT0 + s + 2)
                if SLOT0 + s < T_GDN:
                    kq_copy(SLOT0 + s)
                if s < H * NB:
                    exps(s)
                if 1 <= s <= H * NB:
                    copy_t(s - 1)
                if s in (10, 14):
                    g = (s - 10) // 4
                    act.wait_ge(s_conv, 4 * g + 4)
                    sc.activation(qkvT[:, 4 * g:4 * g + 4, :], qkvT[:, 4 * g:4 * g + 4, :],
                                  ACT.Silu).then_inc(s_silu, 1)
            act.wait_ge(s_modu, N_MOD)
            act.wait_ge(s_silu, 2)
            for n in range(8):
                sc.activation(l2r[:, n, :], qkvT[:, n, :], ACT.Square).then_inc(s_sq, 1)
            for n in range(8):
                act.wait_ge(s_l2, n + 1)
                sc.activation(l2r[:, n, :], bank[4 + n % 3][:], ACT.Ln, bias=eps_t).then_inc(s_l2r, 1)
            for n in range(8):
                act.wait_ge(s_l2r, n + 1)
                sc.activation(l2r[:, n, :], l2r[:, n, :], ACT.Exp, scale=-0.5).then_inc(s_l2e, 1)

            for t in range(NB):
                act.wait_ge(s_du, t + 1)
                sc.activation(QKT[:, t, :], QKT[:, t, :], ACT.Exp)
                last = sc.activation(LM[:, t, :], LM[:, t, :], ACT.Exp, scale=-1.0)
                if t == NB - 1:
                    sc.activation(g16(G_EXP), g16(G_CUM), ACT.Exp)
                    sc.activation(g16(G_DEC), g16(G_DEC), ACT.Exp)
                    last = sc.activation(g_last, g_last, ACT.Exp)
                last.then_inc(s_de, 1)
            act.wait_ge(s_conv, 12)
            sc.activation(qkvT[:, 8:12, :], qkvT[:, 8:12, :], ACT.Silu).then_inc(s_silu, 1)
            for t in range(NB):
                act.wait_ge(s_LT, t + 1)
                sc.copy(LT[:, t, :], bank[4 + t % 2][:]).then_inc(s_LTc, 1)
            for k in range(1, 6):
                for t in range(NB):
                    n = (k - 1) * NB + t
                    act.wait_ge(s_pp, n + 1)
                    if k > 1:
                        act.wait_ge(s_tt, n - NB + 1)
                    sc.copy(PM[:, t, :], bank[t % 2][:]).then_inc(s_pc, 1)
            for t in range(NB):
                act.wait_ge(s_uw, t + 1)
                sc.copy(u[:, t, :], bank[2 * (t % 2)][:])
                sc.copy(wT[:, t, :], bank[2 * (t % 2) + 1][:]).then_inc(s_uwc, 1)
            for g, dst in enumerate((gate_m, gate_f)):
                act.wait_ge(s_gsp, g + 1)
                for half in range(2):
                    last = sc.copy(dst[:, half * 512:(half + 1) * 512], bank[6 + half][:])
                last.then_inc(s_gate, 1)
            act.wait_ge(s_oms, 1)
            sc.activation(o_ms, o_ms, ACT.Sqrt).then_inc(s_omr, 1)
            for k in range(KD):
                act.wait_ge(s_oT, k + 1)
                sc.copy(act_hi[:, k, :], bank[6 + k % 2][:]).then_inc(s_ohi, 1)
            for n in range(T_OUT + 2, T_QUERY):
                hi(n)
            act.wait_ge(s_used, T_QUERY)
            for b in range(NB):
                for half in range(2):
                    last = sc.activation(osq[:, (2 * b + half) * 512:(2 * b + half + 1) * 512],
                                         bank[4 * half + b][:], ACT.Square,
                                         accum_out=ssq2[:, 2 * b + half:2 * b + half + 1])
            last.then_inc(s_ssq, 1)
            sc.drain()
            act.wait_ge(s_msq, 2)
            sc.activation(rstd, rstd, ACT.Sqrt).then_inc(s_rt, 1)
            hi(T_QUERY)
            hi(T_QUERY + 1)
            for b in range(NB):
                act.wait_ge(s_x1, b + 1)
                last = sc.activation(osq[:, b * D:(b + 1) * D], xn[:, b, :], ACT.Square,
                                     accum_out=ssq[:, b:b + 1])
            last.then_inc(s_ssq, 1)
            act.wait_ge(s_msq, 3)
            sc.activation(rstd, rstd, ACT.Sqrt).then_inc(s_rt, 1)
            shifted(1, hfl2)
            for n in range(16):
                act.wait_ge(s_used, T_QUERY + n + 1)
                if n >= 2:
                    act.wait_ge(s_qs, n - 1)
                sc.copy(qTs[:, n % 2, :], bank[n % 4][:]).then_inc(s_qT, 1)
                hi(T_QUERY + n + 2)

            act.sem_inc(s_gev, RING)

            def down_tiles(t0, count, b=None, first=0):
                def one(i, j, unguarded=False):
                    t = i * 4 + (t0 + j)
                    act.wait_ge(s_used, t + (T_DOWN + 1))
                    slot = (T_DOWN + 2 + j) % RAW
                    act.wait_ge(s_raw[slot], i * 16 + 16 * ((T_DOWN + 2 + t0 + j) // RAW + 1))
                    sc.copy(whi[:, j % SPLIT, :], raw[:, slot, :]).then_inc(s_hi, 1)
                    if j >= 2 or not unguarded:
                        act.wait_ge(s_ast[j % 2], i * 32 + 16 * ((t0 + j) // 2))
                    sc.activation(aout[:, j % 2, :], bank[j][:], ACT.Gelu).then_inc(s_act, 1)
                    if b is not None:
                        for r in range(2):
                            q = i * 8 + (32 * b + 2 * j + r)
                            act.wait_ge(s_gp, q + 1)
                            sc.copy(stage[:, :, bass.ds(i * 32 + (2 * j + r) * TOK4, TOK4)]
                                    .rearrange("p i t -> p t i"),
                                    bank[4 + (2 * j + r) % 4][:].rearrange("p (t i) -> p t i", t=TOK4)
                                    ).then_inc(s_gev, 1)
                if first:
                    for j in range(4):
                        one(0, j, True)
                with act.Fori(first, count // 4) as i:
                    for j in range(4):
                        one(i, j)

            down_tiles(0, LEAD, first=1)
            for b in range(NB):
                act.wait_ge(s_best, b + 1)
                sc.activation(pick[:, 2, :], best[:].rearrange("p h k -> p (h k)"),
                              ACT.Exp).then_inc(s_gexp, 1)
                if b > 0:
                    act.wait_ge(s_gst, 16 * STORE * b)
                down_tiles(LEAD + b * (BUILD + REST), BUILD, b)
                down_tiles(LEAD + b * (BUILD + REST) + BUILD, REST)
            down_tiles(LEAD + NB * (BUILD + REST), N_TILES - LEAD - NB * (BUILD + REST))

            def round_coef(t, j, reused):
                act.wait_ge(s_cf, t + 1)
                if reused:
                    act.wait_ge(s_used, t + (T_UP - 1))
                sc.copy(chi[:, j % 2, :], coef[:, j % 2, :]).then_inc(s_chi, 1)

            def up_tile(t, j, more):
                if more:
                    slot = (T_UP + 2 + j) % RAW
                    act.wait_ge(s_raw[slot], (t - j) * 4 + 16 * ((T_UP + 2 + j) // RAW + 1))
                    act.wait_ge(s_used, t + (T_UP + 1))
                    sc.copy(whi[:, j % SPLIT, :], raw[:, slot, :]).then_inc(s_hi, 1)

            round_coef(0, 0, False)
            round_coef(1, 1, False)
            up_tile(0, 0, True)
            for t in range(1, 4):
                round_coef(t + 1, t + 1, True)
                up_tile(t, t, True)
            with act.Fori(1, N_TILES // 4 - 1) as i:
                for j in range(4):
                    round_coef(i * 4 + (j + 1), j + 1, True)
                    up_tile(i * 4 + j, j, True)
            for t in range(N_TILES - 4, N_TILES):
                if t + 1 < N_TILES:
                    round_coef(t + 1, t + 1, True)
                up_tile(t, t % 4, t + 2 < N_TILES)
            act.wait_ge(s_used, T_ALL)
            for b in range(NB):
                for half in range(2):
                    last = sc.activation(yo[:, b, half * 512:(half + 1) * 512], bank[2 * b + half][:],
                                         ACT.Square, accum_out=ssq2[:, 2 * b + half:2 * b + half + 1])
            last.then_inc(s_yq, 1)
            act.wait_ge(s_ym, 1)
            sc.activation(rstd, rstd, ACT.Sqrt).then_inc(s_yr, 1)

        @block.tensor
        def _(pe):
            mm = nc.tensor.matmul

            def split_wait(n):
                pe.wait_ge(s_lo, n + 1)

            def column_tile(slot, out_bank):
                for k in range(KD):
                    w = slice(k * P, (k + 1) * P)
                    mm(out_bank[:], whi[:, slot, w], act_hi[:, k, :], start=(k == 0), stop=False)
                    mm(out_bank[:], whi[:, slot, w], act_lo[:, k, :], start=False, stop=False)
                    last = mm(out_bank[:], wlo[:, slot, w], act_hi[:, k, :], start=False,
                              stop=(k == KD - 1))
                last.then_inc(s_used, 1)

            def natural_tile(slot, q, banks):
                for b in range(NB):
                    for kk in range(2):
                        k = 2 * q + kk
                        w = slice(kk * 512, (kk + 1) * 512)
                        a = slice(b * P, (b + 1) * P)
                        mm(banks[b][:], act_hi[:, k, a], whi[:, slot, w], start=(k == 0), stop=False)
                        mm(banks[b][:], act_hi[:, k, a], wlo[:, slot, w], start=False, stop=False)
                        last = mm(banks[b][:], act_lo[:, k, a], whi[:, slot, w], start=False,
                                  stop=(k == KD - 1))
                last.then_inc(s_used, 1)

            pe.wait_ge(s_pool, 1)
            pe.wait_ge(s_xs, 1)
            for k in range(KD):
                if k >= 2:
                    pe.wait_ge(s_hf, k - 1)
                for b in range(NB):
                    last = nc.tensor.transpose(bank[6 + k % 2][:, b * P:(b + 1) * P],
                                               xn[:, b, k * P:(k + 1) * P], ident[:])
                last.then_inc(s_xT, 1)
            for n in range(T_VA, T_KQ):
                split_wait(n)
                if n < T_Z:
                    pe.wait_ge(s_hlo, 2 * n + 2)
                natural_tile(n % SPLIT, n % 4, bank[0:4] if n < T_Z else bank[4:8])
            pe.wait_ge(s_nat, NB)
            pe.wait_ge(s_bas, 2)
            for k in range(KD):
                mm(bank[2][0:8, :], baw_hi[:, k, :], act_hi[:, k, :], start=(k == 0), stop=False)
                mm(bank[2][0:8, :], baw_hi[:, k, :], act_lo[:, k, :], start=False, stop=False)
                last = mm(bank[2][0:8, :], baw_lo[:, k, :], act_hi[:, k, :], start=False,
                          stop=(k == KD - 1))
            last.then_inc(s_baT, 1)
            for n in range(T_KQ, SLOT0):
                split_wait(n)
                column_tile(n % SPLIT, bank[n % 2])
            pe.wait_ge(s_bac, 1)
            for b in range(NB):
                last = nc.tensor.transpose(bank[3][:, b * 8:b * 8 + 8], baT[:, b * P:(b + 1) * P],
                                           ident[0:8, 0:8])
            last.then_inc(s_ba, 1)

            def scores(i):
                h, b = divmod(i, NB)
                if i == 0:
                    pe.wait_ge(s_g1, 1)
                if i == 1:
                    pe.wait_ge(s_nat, 2 * NB)
                if b == 0:
                    pe.wait_ge(s_kq, 2 * h + 2)
                if i >= 2:
                    pe.wait_ge(s_mx, i - 1)
                for m in range(2):
                    r = slice(m * QK, (m + 1) * QK)
                    last = mm(bank[2 + 2 * (i % 2) + m][:, 0:(b + 1) * P], qaT[r, h, b * P:(b + 1) * P],
                              kaT[r, h, 0:(b + 1) * P], start=True, stop=True)
                last.then_inc(s_sc, 1)

            def transposes(i):
                pe.wait_ge(s_pd, i + 1)
                if i >= 1:
                    pe.wait_ge(s_ptc, i)
                for j in range(i % NB + 1):
                    last = nc.tensor.transpose(bank[6][:, j * P:(j + 1) * P],
                                               pr[:, i % 2, 0, j * P:(j + 1) * P], ident[:])
                last.then_inc(s_pt, 1)

            def values(i):
                h, b = divmod(i, NB)
                pe.wait_ge(s_ptc, i + 1)
                if i >= 1:
                    pe.wait_ge(s_oa, i)
                for j in range(b + 1):
                    last = mm(bank[7][:, 0:HD], pT[:, i % 2, j * P:(j + 1) * P],
                              va[:, j, h * HD:(h + 1) * HD], start=(j == 0), stop=(j == b))
                last.then_inc(s_av, 1)

            for s in range(T_OUT - SLOT0):
                n = SLOT0 + s
                split_wait(n)
                if n - 2 < T_GDN:
                    pe.wait_ge(s_kq, n - 2 - T_KQ + 1)
                else:
                    pe.wait_ge(s_conv, n - 2 - T_GDN + 1)
                column_tile(n % SPLIT, bank[n % 2])
                if s < H * NB:
                    scores(s)
                if 1 <= s <= H * NB:
                    transposes(s - 1)
                if 2 <= s <= H * NB + 1:
                    values(s - 2)

            def blk(t):
                return slice(t * P, (t + 1) * P)

            def hs(h):
                return slice(h * HD, (h + 1) * HD)

            def norm_sums(n):
                pe.wait_ge(s_sq, n + 1)
                if n >= 3:
                    pe.wait_ge(s_l2r, n - 2)
                mm(bank[4 + n % 3][:], ones[:], l2r[:, n, :], start=True, stop=True).then_inc(s_l2, 1)

            for n in range(3):
                norm_sums(n)
            pe.wait_ge(s_oa, H * NB)
            pe.wait_ge(s_gB, 1)
            mm(bank[7][:, 0:16], masks[:, M_U, :], g16(G_LOG), start=True, stop=True).then_inc(s_gc, 1)
            pe.wait_ge(s_conv, 12)
            for t in range(NB):
                for h in range(H):
                    last = mm(bank[t][:, hs(h)], gB[:, 4 * t + h, :], masks[:, M_U, :], start=True, stop=True)
                last.then_inc(s_row, 1)
            for n in range(3, 8):
                norm_sums(n)
            pe.wait_ge(s_l2n, 8)
            pe.wait_ge(s_gcc, 1)
            for t in range(NB):
                if t >= 2:
                    pe.wait_ge(s_L, t - 1)
                for h in range(H):
                    mm(bank[4 + t % 2][:, hs(h)], qkvT[:, 4 + h, blk(t)], qkvT[:, 4 + h, blk(t)],
                       start=True, stop=True)
                for h in range(H):
                    last = mm(bank[6 + t % 2][:, hs(h)], qkvT[:, 4 + h, blk(t)], qkvT[:, h, blk(t)],
                              start=True, stop=True)
                last.then_inc(s_kg, 1)
            for t in range(NB):
                if t == 0:
                    pe.wait_ge(s_L, NB)
                if t >= 2:
                    pe.wait_ge(s_LTc, t - 1)
                for h in range(H):
                    last = nc.tensor.transpose(bank[4 + t % 2][:, hs(h)], LM[:, t, hs(h)], ident[:])
                last.then_inc(s_LT, 1)
            pe.wait_ge(s_silu, 3)
            for t in range(NB):
                if t >= 1:
                    pe.wait_ge(s_vtd, t)
                for h in range(H):
                    nc.tensor.transpose(bank[6][:, hs(h)], qkvT[:, 8 + h, blk(t)], ident[:])
                for h in range(H):
                    last = nc.tensor.transpose(bank[7][:, hs(h)], qkvT[:, 4 + h, blk(t)], ident[:])
                last.then_inc(s_vt, 1)

            def level_p(n):
                t = n % NB
                pe.wait_ge(s_lm, n + 1)
                pe.wait_ge(s_td, n + 1)
                if n >= 2:
                    pe.wait_ge(s_pc, n - 1)
                for h in range(H):
                    last = mm(bank[t % 2][:, hs(h)], LM[:, t, hs(h)], Tm[:, t, hs(h)], start=True, stop=True)
                last.then_inc(s_pp, 1)

            def level_t(n):
                k, t = divmod(n, NB)
                pe.wait_ge(s_pc, n + 1)
                if n >= 2:
                    pe.wait_ge(s_td, NB + n - 1)
                if n == 0:
                    pe.wait_ge(s_LTc, NB)
                for h in range(H):
                    if k < 4:
                        mm(bank[2 + t % 2][:, hs(h)], TT[:, t, hs(h)], PM[:, t, hs(h)], start=True, stop=True)
                for h in range(H):
                    last = mm(bank[4 + t % 2][:, hs(h)], PM[:, t, hs(h)], TT[:, t, hs(h)], start=True, stop=True)
                last.then_inc(s_tt, 1)

            for n in range(5 * NB + 1):
                if n < 5 * NB:
                    level_p(n)
                if n >= 1:
                    level_t(n - 1)
            for t in range(NB):
                pe.wait_ge(s_td, 5 * NB + t + 1)
                if t == 0:
                    pe.wait_ge(s_td, 6 * NB)
                    pe.wait_ge(s_vtd, NB)
                if t >= 2:
                    pe.wait_ge(s_uwc, t - 1)
                for h in range(H):
                    mm(bank[2 * (t % 2)][:, hs(h)], TT[:, t, hs(h)], vbeta[:, t, hs(h)], start=True, stop=True)
                for h in range(H):
                    last = mm(bank[2 * (t % 2) + 1][:, hs(h)], kbeg[:, t, hs(h)], TT[:, t, hs(h)],
                              start=True, stop=True)
                last.then_inc(s_uw, 1)
            def gate_row(g):
                for k in range(KD):
                    last = mm(bank[6 + k // 4][:, blk(k % 4)],
                              gcol[:, g, k:k + 1].to_broadcast([P, P]), ident[:], start=True, stop=True)
                last.then_inc(s_gsp, 1)

            pe.wait_ge(s_gcol, 1)
            gate_row(0)
            pe.wait_ge(s_uwc, NB)
            for c in range(NCH):
                t = c // 2
                r = slice(CH * (c % 2), CH * (c % 2) + CH)
                tok = slice(c * CH, (c + 1) * CH)
                pe.wait_ge(s_st, c + 1)
                for h in range(H):
                    off = h * HD + CH * (c % 2)
                    last = mm(bank[0][r, hs(h)], wT[:, t, off:off + CH], state[:, hs(h)], start=True, stop=True)
                last.then_inc(s_wS, 1)
                if c >= 2:
                    pe.wait_ge(s_oc, c - 1)
                for h in range(H):
                    last = mm(bank[2 + c % 2][r, hs(h)], qkvT[:, h, tok], state[:, hs(h)], start=True, stop=True)
                last.then_inc(s_qS, 1)
                pe.wait_ge(s_vn, c + 1)
                for h in range(H):
                    last = mm(bank[1][:, hs(h)], kdec[r, t, hs(h)], vnew[r, hs(h)], start=True, stop=True)
                last.then_inc(s_kv, 1)
                for h in range(H):
                    off = h * HD + CH * (c % 2)
                    last = mm(bank[4 + c % 2][r, hs(h)], QKT[r, t, off:off + CH], vnew[r, hs(h)],
                              start=True, stop=True)
                last.then_inc(s_qkv, 1)
                if c == 0:
                    pe.wait_ge(s_gate, 1)
                    gate_row(1)
            pe.wait_ge(s_gate, 2)
            pe.wait_ge(s_on, 1)
            for k in range(KD):
                if k >= 2:
                    pe.wait_ge(s_olo, k - 1)
                for b in range(NB):
                    last = nc.tensor.transpose(bank[6 + k % 2][:, blk(b)], onat[:, b, blk(k)], ident[:])
                last.then_inc(s_oT, 1)
            pe.wait_ge(s_olo, KD)
            for n in range(T_OUT, T_QUERY):
                split_wait(n)
                natural_tile(n % SPLIT, n % 4, bank[0:4] if n < T_OUT + 4 else bank[4:8])
            pe.wait_ge(s_xs, 2)
            for k in range(KD):
                if k >= 2:
                    pe.wait_ge(s_hf, KD + k - 1)
                for b in range(NB):
                    last = nc.tensor.transpose(bank[k % 2][:, blk(b)], xs2[:, b, blk(k)], ident[:])
                last.then_inc(s_xT, 1)
            pe.wait_ge(s_hlo, 2 * KD)

            def key_scores(n):
                pe.wait_ge(s_qT, n + 1)
                if n == 0:
                    pe.wait_ge(s_key, 16)
                if n >= 2:
                    pe.wait_ge(s_S, n - 1)
                for b in range(NB):
                    last = mm(bank[4 + n % 2][:, blk(b)], qTs[:, n % 2, blk(b)], keys[:, n, :],
                              start=True, stop=True)
                last.then_inc(s_qs, 1)

            for n in range(17):
                if n < 16:
                    split_wait(T_QUERY + n)
                    if n >= 4:
                        pe.wait_ge(s_qT, n - 3)
                    column_tile(n % SPLIT, bank[n % 4])
                if n >= 1:
                    key_scores(n - 1)

            pe.wait_ge(s_qT, 16)
            pe.wait_ge(s_S, 16)

            def gate_group(q, slot):
                pe.wait_ge(s_ohl, q + 1)
                pe.wait_ge(s_gev, q + 1)
                for tk in range(TOK4):
                    c = slice(tk * P, (tk + 1) * P)
                    mm(bank[4 + slot % 4][:, c], ohJ[:, slot % OH, c], ohIh[:, slot % OH, c],
                       start=True, stop=False)
                    last = mm(bank[4 + slot % 4][:, c], ohJ[:, slot % OH, c], ohIl[:, slot % OH, c],
                              start=False, stop=True)
                last.then_inc(s_gp, 1)

            def down_tiles(t0, count, b=None, first=0):
                def one(i, j, free):
                    t = i * 4 + (t0 + j)
                    pe.wait_ge(s_lo, t + (T_DOWN + 1))
                    if free:
                        pe.wait_ge(s_act, t - 3)
                    column_tile(j % SPLIT, bank[j])
                    if b is not None:
                        for r in range(2):
                            gate_group(i * 8 + (32 * b + 2 * j + r), 2 * j + r)
                if first:
                    for j in range(4):
                        one(0, j, False)
                with pe.Fori(first, count // 4) as i:
                    for j in range(4):
                        one(i, j, True)

            down_tiles(0, LEAD, first=1)
            for b in range(NB):
                pe.wait_ge(s_pick, b + 1)
                pe.wait_ge(s_gev, RING + 32 * b)
                for v in range(3):
                    last = nc.tensor.transpose(bank[7][:, v * P:(v + 1) * P], pick[:, v, :], ident[:])
                last.then_inc(s_pkT, 1)
                down_tiles(LEAD + b * (BUILD + REST), BUILD, b)
                down_tiles(LEAD + b * (BUILD + REST) + BUILD, REST)
            down_tiles(LEAD + NB * (BUILD + REST), N_TILES - LEAD - NB * (BUILD + REST))

            def up_tile(t, j, start, stop):
                pe.wait_ge(s_lo, t + (T_UP + 1))
                pe.wait_ge(s_clo, t + 1)
                for b in range(NB):
                    a = blk(b)
                    for half in range(2):
                        w = slice(half * 512, (half + 1) * 512)
                        o = bank[2 * b + half][:]
                        mm(o, chi[:, j % 2, a], whi[:, j % SPLIT, w], start=start, stop=False,
                           skip_group_check=True)
                        mm(o, chi[:, j % 2, a], wlo[:, j % SPLIT, w], start=False, stop=False,
                           skip_group_check=True)
                        last = mm(o, clo[:, j % 2, a], whi[:, j % SPLIT, w], start=False, stop=stop,
                                  skip_group_check=True)
                last.then_inc(s_used, 1)

            pe.wait_ge(s_act, N_TILES)
            pe.wait_ge(s_gev, RING + 32 * NB)
            for t in range(4):
                up_tile(t, t, t == 0, False)
            with pe.Fori(1, N_TILES // 4 - 1) as i:
                for j in range(4):
                    up_tile(i * 4 + j, j, False, False)
            for t in range(N_TILES - 4, N_TILES):
                up_tile(t, t % 4, False, t == N_TILES - 1)

        @block.vector
        def _(dve):
            v = nc.vector
            tt, ts, stt = v.tensor_tensor, v.tensor_scalar, v.scalar_tensor_tensor

            def bc(ap16, t):
                return ap16[:, 4 * t:4 * t + 4].unsqueeze(2).to_broadcast([P, H, P])

            dve.wait_ge(s_pool, 1)
            ge = wk[:, 0, 0:P]
            lt = wk[:, 0, P:2 * P]
            same = wk[:, 0, 2 * P:3 * P]
            xo = wk[:, 1, 0:P].bitcast(I32)
            xk = wk[:, 1, P:2 * P].bitcast(I32)
            tt(ge, xij[:, 0, :], xij[:, 1, :], ALU.is_ge)
            tt(lt, xij[:, 0, :], xij[:, 1, :], ALU.is_lt)
            tt(masks[:, M_STRICT, :], xij[:, 0, :], xij[:, 1, :], ALU.is_gt)
            tt(xo, xij[:, 0, :], xij[:, 1, :], ALU.bitwise_xor)
            v.drain()
            ts(same, xo, CH, None, ALU.is_lt)
            v.drain()
            tt(masks[:, M_INCL, :], ge, same, ALU.mult)
            tt(masks[:, M_U, :], lt, same, ALU.mult)
            tt(masks[:, M_STRICT, :], masks[:, M_STRICT, :], same, ALU.mult)
            v.drain()
            tt(masks[:, M_U, :], masks[:, M_U, :], ident[:], ALU.add)
            for k in range(6):
                v.drain()
                ts(xk, xo, k, None, ALU.logical_shift_right)
                v.drain()
                ts(masks[:, MT + k, :], xk, 1, None, ALU.is_equal)
                if k == 0:
                    ts(masks[:, M_FIRST, :], xk, 1, None, ALU.is_equal)
                v.drain()
                tt(masks[:, MT + k, :], masks[:, MT + k, :], lt, ALU.mult)
            tt(masks[:, M_FIRST, :], masks[:, M_FIRST, :], masks[:, M_STRICT, :], ALU.mult)
            v.drain()
            ts(negm[:], rel[:], 0.0, NEG, ALU.is_lt, ALU.mult).then_inc(s_xij, 1)
            dve.wait_ge(s_ssq, NB)

            def inverse_root(wait_root):
                dve.wait_ge(s_rt, wait_root)
                v.reciprocal(rstd, rstd)
                v.drain()

            ts(rstd, ssq, 1.0 / D, EPS, ALU.mult, ALU.add).then_inc(s_msq, 1)
            inverse_root(1)
            for b in range(NB):
                last = ts(xn[:, b, :], xn[:, b, :], rstd[:, b:b + 1], None, ALU.mult)
            last.then_inc(s_xs, 1)

            def mod_tile(m):
                if m == 0:
                    dve.wait_ge(s_cc, 1)
                part, k = mod_order(m)
                t = (modr if m < 16 else modx)[:, m % 4, :]
                dve.wait_ge(s_modl[m % 4], 16 * (m // 4 + 1))
                v.tensor_tensor_reduce(out=t, in0=t, in1=c_row[:], scale=1.0, scalar=0.0, op0=ALU.mult,
                                       op1=ALU.add, accum_out=modcol[:, part, k:k + 1]).then_inc(s_modu, 1)

            def mod_columns(half, k0, k1):
                v.drain()
                w = slice(k0, k1)
                tt(bcol[:, half, w], modcol[:, 3 * half, w], modbcol[:, 3 * half, w], ALU.add)
                tt(acol[:, half, w], modcol[:, 3 * half + 1, w], modbcol[:, 3 * half + 1, w], ALU.add)
                v.drain()
                stt(out=acol[:, half, w], in0=acol[:, half, w], scalar=1.0, in1=gaincol[:, half, w],
                    op0=ALU.add, op1=ALU.mult).then_inc(s_cols, 1)

            def gate_columns():
                v.drain()
                gates = modcol[:].rearrange("p (a c) k -> p a c k", a=2)[:, :, 2, :]
                biases = modbcol[:].rearrange("p (a c) k -> p a c k", a=2)[:, :, 2, :]
                tt(gcol[:], gates, biases, ALU.add)
                v.drain()
                tt(gcol[:], gcol[:], gaincol[:, 2:4, :], ALU.mult).then_inc(s_gcol, 1)

            def low(half, k, buf):
                dve.wait_ge(s_hhi, KD * half + k + 1)
                tt(act_lo[:, k, :], buf[:, k % 2, :], act_hi[:, k, :].bitcast(F32),
                   ALU.subtract).then_inc(s_hlo, 1)

            dve.wait_ge(s_c, 16 * 3)
            for r in range(4):
                for m in range(4 * r, 4 * r + 4):
                    mod_tile(m)
                mod_columns(0, 2 * r, 2 * r + 2)
                if r >= 1:
                    low(0, 2 * r - 2, wk)
                    low(0, 2 * r - 1, wk)
            low(0, KD - 2, wk)
            low(0, KD - 1, wk)
            dve.wait_ge(s_bas, 1)
            tt(baw_lo[:], baw[:], baw_hi[:].bitcast(F32), ALU.subtract).then_inc(s_bas, 1)
            for m in range(16, 28):
                mod_tile(m)

            def conv(n):
                dve.wait_ge(s_used, T_GDN + n + 1)
                o = qkvT[:, n, :]
                ps = bank[n % 2]
                ts(o, ps[:], conv_w[:, n, 3:4], None, ALU.mult)
                for j in (2, 1, 0):
                    s = 3 - j
                    v.drain()
                    last = stt(out=o[:, s:], in0=ps[:, 0:SEQ - s], scalar=conv_w[:, n, j:j + 1],
                               in1=o[:, s:], op0=ALU.mult, op1=ALU.add)
                last.then_inc(s_conv, 1)

            dve.wait_ge(s_hc, 16 * 5)
            l64 = lam_in.rearrange("p (a n) -> p a n", a=4)
            for m in range(2):
                tt(l64[:, m, :], l64[:, m, :], l64[:, 2 + m, :], ALU.mult)
            v.drain()
            v.tensor_reduce(lam[:, 0:2], l64[:, 0:2, :], AX_X, ALU.add).then_inc(s_lam, 1)
            ts(again, again, 1.0 - LAMBDA_INIT, None, ALU.mult)
            dve.wait_ge(s_baT, 1)
            v.tensor_copy(baT[:], bank[2][0:8, :]).then_inc(s_bac, 1)
            for m in range(28, 36):
                mod_tile(m)
            dve.wait_ge(s_lame, 1)
            tt(lam[:, 2:3], lam[:, 0:1], lam[:, 1:2], ALU.subtract)
            v.drain()
            ts(lam[:, 2:3], lam[:, 2:3], LAMBDA_INIT, -1.0, ALU.add, ALU.mult)

            dve.wait_ge(s_ba, 1)
            ba = bank[3][:, 0:32].rearrange("p (t c) -> p t c", t=NB)
            def th(ap):
                return ap.rearrange("p (t h) -> p t h", t=NB)
            v.tensor_copy(th(g16(G_BETA)), ba[:, :, 0:4])
            tt(th(g16(G_Y)), ba[:, :, 4:8], dt4.unsqueeze(1).to_broadcast([P, NB, H]), ALU.add)
            v.drain()
            stt(out=g16(G_AY), in0=g16(G_Y), scalar=-1.0, in1=g16(G_Y), op0=ALU.mult,
                op1=ALU.max).then_inc(s_g1, 1)
            dve.wait_ge(s_g1e, 1)
            ts(g16(G_BETA), g16(G_BETA), 1.0, None, ALU.add)
            stt(out=g16(G_SP), in0=g16(G_Y), scalar=0.0, in1=g16(G_SP), op0=ALU.max, op1=ALU.add)
            v.drain()
            v.reciprocal(g16(G_BETA), g16(G_BETA))
            stt(out=th(g16(G_LOG)), in0=th(g16(G_SP)), scalar=-1.0,
                in1=alog4.unsqueeze(1).to_broadcast([P, NB, H]), op0=ALU.mult, op1=ALU.mult)

            def biased(i):
                h, b = divmod(i, NB)
                n = (b + 1) * P
                if b == 0:
                    stt(out=bias[:, h % 2, :], in0=rel[:], scalar=-(2.0 ** (-8.0 * (h + 1) / H)),
                        in1=negm[:], op0=ALU.mult, op1=ALU.add)
                    v.drain()
                dve.wait_ge(s_sc, i + 1)
                if i >= 2:
                    dve.wait_ge(s_pt, i - 1)
                for m in range(2):
                    v.tensor_tensor_reduce(out=pr[:, i % 2, m, 0:n], in0=bank[2 + 2 * (i % 2) + m][:, 0:n],
                                           in1=bias[:, h % 2, 512 - n:512], scale=1.0, scalar=-3e38,
                                           op0=ALU.add, op1=ALU.max, accum_out=asm[:, i % 2, m:m + 1])
                v.drain()
                ts(asm[:, i % 2, 2:4], asm[:, i % 2, 0:2], -1.0, None, ALU.mult).then_inc(s_mx, 1)

            def difference(i):
                n = (i % NB + 1) * P
                dve.wait_ge(s_ex, i + 1)
                a = asm[:, i % 2, 4:6]
                v.reciprocal(a, a)
                v.drain()
                tt(a[:, 1:2], a[:, 1:2], lam[:, 2:3], ALU.mult)
                ts(pr[:, i % 2, 0, 0:n], pr[:, i % 2, 0, 0:n], a[:, 0:1], None, ALU.mult)
                v.drain()
                stt(out=pr[:, i % 2, 0, 0:n], in0=pr[:, i % 2, 1, 0:n], scalar=a[:, 1:2],
                    in1=pr[:, i % 2, 0, 0:n], op0=ALU.mult, op1=ALU.add).then_inc(s_pd, 1)

            def attn_out(i):
                h, b = divmod(i, NB)
                dve.wait_ge(s_av, i + 1)
                v.tensor_copy(onat[:, b, h * HD:(h + 1) * HD],
                              bank[7][:, 0:HD]).then_inc(s_oa, 1)

            v.drain()
            for s in range(T_OUT - SLOT0 + 1):
                if 3 <= s <= H * NB + 2:
                    attn_out(s - 3)
                if s < H * NB:
                    biased(s)
                if T_GDN <= SLOT0 + s < T_OUT:
                    conv(SLOT0 + s - T_GDN)
                if s < H * NB:
                    difference(s)
                for m in range(2 * s + 36, min(2 * s + 38, N_MOD)):
                    mod_tile(m)
                if s == 6:
                    mod_columns(1, 0, KD)
                    gate_columns()

            v.tensor_copy(gB[:], g16(G_LOG).unsqueeze(2).to_broadcast([P, 16, P])).then_inc(s_gB, 1)

            dve.wait_ge(s_gc, 1)
            v.tensor_copy(g16(G_CUM), bank[7][:, 0:16]).then_inc(s_gcc, 1)
            v.memset(state[:], 0.0).then_inc(s_st, 1)
            v.drain()
            for t in range(NB):
                dve.wait_ge(s_row, t + 1)
                row = by_head(bank[t][:])
                tt(by_head(QKT[:, t, :]), row, bc(g16(G_CUM), t), ALU.subtract)
                for s in range(2):
                    r = slice(CH * s, CH * (s + 1))
                    tt(g16(G_DEC)[r, 4 * t:4 * t + 4], row[r, :, CH * s + CH - 1],
                       g16(G_CUM)[r, 4 * t:4 * t + 4], ALU.subtract)
                    c = 2 * t + s
                    v.tensor_copy(g_last[:, 4 * c:4 * c + 4], row[:, :, CH * s + CH - 1])
                v.drain()
                tt(by_head(LM[:, t, :]), by_head(QKT[:, t, :]), mask4(M_INCL), ALU.mult)
                v.drain()
                tt(by_head(QKT[:, t, :]), by_head(QKT[:, t, :]), mask4(M_U), ALU.mult).then_inc(s_du, 1)
            for n in range(8):
                dve.wait_ge(s_l2e, n + 1)
                stt(out=qkvT[:, n, :], in0=qkvT[:, n, :], scalar=HD ** -0.5 if n < 4 else 1.0,
                    in1=l2r[:, n, :], op0=ALU.mult, op1=ALU.mult).then_inc(s_l2n, 1)
            for t in range(NB):
                dve.wait_ge(s_de, t + 1)
                tt(by_head(LM[:, t, :]), by_head(LM[:, t, :]), mask4(M_STRICT), ALU.mult)
                tt(by_head(QKT[:, t, :]), by_head(QKT[:, t, :]), mask4(M_U), ALU.mult)
                v.drain()
                dve.wait_ge(s_kg, t + 1)
                tt(LM[:, t, :], LM[:, t, :], bank[4 + t % 2][:], ALU.mult)
                tt(QKT[:, t, :], QKT[:, t, :], bank[6 + t % 2][:], ALU.mult)
                v.drain()
                tt(by_head(LM[:, t, :]), by_head(LM[:, t, :]), bc(g16(G_BETA), t),
                   ALU.mult).then_inc(s_L, 1)
                v.drain()
                tt(by_head(PM[:, t, :]), by_head(LM[:, t, :]), mask4(M_FIRST), ALU.mult)
                v.drain()
                tt(by_head(Tm[:, t, :]), ident[:].unsqueeze(1).to_broadcast([P, H, P]),
                   by_head(PM[:, t, :]), ALU.subtract)
            tt(g16(G_BEXP), g16(G_BETA), g16(G_EXP), ALU.mult)
            v.drain()
            for t in range(NB):
                dve.wait_ge(s_LTc, t + 1)
                tt(by_head(PM[:, t, :]), by_head(LT[:, t, :]), mask4(MT), ALU.mult)
                v.drain()
                tt(by_head(TT[:, t, :]), ident[:].unsqueeze(1).to_broadcast([P, H, P]),
                   by_head(PM[:, t, :]), ALU.subtract).then_inc(s_td, 1)
            def scaled_vk(t):
                dve.wait_ge(s_vt, t + 1)
                tt(by_head(vbeta[:, t, :]), by_head(bank[6][:]), bc(g16(G_BETA), t), ALU.mult)
                tt(by_head(kbeg[:, t, :]), by_head(bank[7][:]), bc(g16(G_BEXP), t), ALU.mult)
                tt(by_head(kdec[:, t, :]), by_head(bank[7][:]), bc(g16(G_DEC), t),
                   ALU.mult).then_inc(s_vtd, 1)

            def masked(n):
                k, t = divmod(n, NB)
                if k >= 1:
                    dve.wait_ge(s_pp, n - NB + 1)
                tt(by_head(LM[:, t, :]), by_head(LT[:, t, :]), mask4(MT + 1 + k), ALU.mult).then_inc(s_lm, 1)

            def updated(n):
                k, t = divmod(n, NB)
                dve.wait_ge(s_tt, n + 1)
                if k < 4:
                    tt(Tm[:, t, :], Tm[:, t, :], bank[2 + t % 2][:], ALU.subtract)
                tt(TT[:, t, :], TT[:, t, :], bank[4 + t % 2][:], ALU.subtract).then_inc(s_td, 1)

            for n in range(NB):
                masked(n)
            for t in range(NB):
                scaled_vk(t)
            for n in range(5 * NB):
                updated(n)
                if n + NB < 5 * NB:
                    v.drain()
                    masked(n + NB)

            def chunk_out(c):
                t = c // 2
                r = slice(CH * (c % 2), CH * (c % 2) + CH)
                o = onat[r, t, 512:1024]
                dve.wait_ge(s_qkv, c + 1)
                tt(by_head(o), by_head(bank[2 + c % 2][r, :]),
                   g16(G_EXP)[r, 4 * t:4 * t + 4].unsqueeze(2).to_broadcast([CH, H, P]), ALU.mult)
                v.drain()
                tt(o, o, bank[4 + c % 2][r, :], ALU.add).then_inc(s_oc, 1)

            dve.wait_ge(s_uwc, NB)
            for c in range(NCH):
                t = c // 2
                r = slice(CH * (c % 2), CH * (c % 2) + CH)
                dve.wait_ge(s_wS, c + 1)
                tt(vnew[r, :], u[r, t, :], bank[0][r, :], ALU.subtract).then_inc(s_vn, 1)
                dve.wait_ge(s_qS, c + 1)
                tt(by_head(state[:]), by_head(state[:]),
                   g_last[:, 4 * c:4 * c + 4].unsqueeze(2).to_broadcast([P, H, P]), ALU.mult)
                v.drain()
                dve.wait_ge(s_kv, c + 1)
                tt(state[:], state[:], bank[1][:], ALU.add).then_inc(s_st, 1)
                chunk_out(c)
            v.drain()
            of = onat[:].rearrange("p b n -> p (b n)")
            o32 = of.rearrange("p (m n) -> p m n", n=HD)
            tt(osq[:], of, of, ALU.mult)
            v.drain()
            v.tensor_reduce(o_ms, osq[:].rearrange("p (m n) -> p m n", n=HD), AX_X, ALU.add)
            v.drain()
            ts(o_ms, o_ms, 1.0 / HD, EPS, ALU.mult, ALU.add).then_inc(s_oms, 1)
            dve.wait_ge(s_omr, 1)
            v.reciprocal(o_ms, o_ms)
            v.drain()
            tt(o32, o32, o_ms.unsqueeze(2).to_broadcast([P, 32, HD]), ALU.mult)
            v.drain()
            o4 = onat[:].rearrange("p b (m n) -> p b m n", n=HD)
            for b in range(NB):
                tt(o4[:, b, 0:4, :], o4[:, b, 0:4, :], again.unsqueeze(1).to_broadcast([P, 4, HD]), ALU.mult)
                tt(o4[:, b, 4:8, :], o4[:, b, 4:8, :], ggain.unsqueeze(1).to_broadcast([P, 4, HD]), ALU.mult)
            v.drain()
            tt(onat[:, :, 512:1024], onat[:, :, 512:1024], zs[:], ALU.mult).then_inc(s_on, 1)
            for k in range(KD):
                dve.wait_ge(s_ohi, k + 1)
                tt(act_lo[:, k, :], bank[6 + k % 2][:], act_hi[:, k, :].bitcast(F32),
                   ALU.subtract).then_inc(s_olo, 1)
            dve.wait_ge(s_ssq, NB + 1)
            v.tensor_reduce(rstd, ssq2.rearrange("p (b a) -> p b a", a=2), AX_X, ALU.add)
            v.drain()
            ts(rstd, rstd, 1.0 / D, EPS, ALU.mult, ALU.add).then_inc(s_msq, 1)
            inverse_root(2)
            dve.wait_ge(s_xr, 16 * NB)
            for b in range(NB):
                for half in range(2):
                    w = slice(half * 512, (half + 1) * 512)
                    stt(out=xs2[:, b, w], in0=bank[4 * half + b][:], scalar=rstd[:, b:b + 1],
                        in1=gate_m[:, w], op0=ALU.mult, op1=ALU.mult)
                v.drain()
                tt(xn[:, b, :], xn[:, b, :], xs2[:, b, :], ALU.add).then_inc(s_x1, 1)
            dve.wait_ge(s_ssq, NB + 2)
            ts(rstd, ssq, 1.0 / D, EPS, ALU.mult, ALU.add).then_inc(s_msq, 1)
            inverse_root(3)
            for b in range(NB):
                last = ts(xs2[:, b, :], xn[:, b, :], rstd[:, b:b + 1], None, ALU.mult)
            last.then_inc(s_xs, 1)
            v.drain()
            for k in range(KD):
                low(1, k, hfl2)
            dve.wait_ge(s_x1o, 16 * NB)
            for n in range(16):
                dve.wait_ge(s_qs, n + 1)
                v.tensor_copy(S[:, :, n, :], bank[4 + n % 2][:].rearrange("p (b n) -> p b n", b=NB)
                              ).then_inc(s_S, 1)

            def top16(lists):
                for vals, _, src in lists:
                    v.max(vals[:, 0:8], src)
                v.drain()
                for vals, idx, src in lists:
                    v.max_index(idx[:, 0:8], vals[:, 0:8], src)
                v.drain()
                for vals, _, src in lists:
                    v.match_replace(out=src, in_to_replace=vals[:, 0:8], in_values=src, imm_value=LOWEST)
                v.drain()
                for vals, _, src in lists:
                    v.max(vals[:, 8:16], src)
                v.drain()
                for vals, idx, src in lists:
                    v.max_index(idx[:, 8:16], vals[:, 8:16], src)

            def retrieve(b):
                top16([(top[:, n, :], topi[:, n, :], S[:, b, n, :]) for n in range(2 * PH)])
                v.drain()
                v.tensor_copy(topf[:], topi[:])
                if b >= 1:
                    dve.wait_ge(s_gp, 32 * b)
                for h in range(PH):
                    tt(cand[:, h, :].rearrange("p (a c) -> p a c", a=TOPK),
                       top[:, 2 * h, :].unsqueeze(2).to_broadcast([P, TOPK, TOPK]),
                       top[:, 2 * h + 1, :].unsqueeze(1).to_broadcast([P, TOPK, TOPK]), ALU.add)
                v.drain()
                if b >= 1:
                    dve.wait_ge(s_gexp, b)
                top16([(best[:, h, :], pos[:, h * TOPK:(h + 1) * TOPK], cand[:, h, :]) for h in range(PH)])
                v.drain()
                v.tensor_copy(gsum[:, 0:PH], best[:, :, 0])
                if b >= 1:
                    dve.wait_ge(s_pkT, b)
                v.drain()
                tt(best[:], best[:], gsum[:, 0:PH].unsqueeze(2).to_broadcast([P, PH, TOPK]),
                   ALU.subtract).then_inc(s_best, 1)
                c3 = cand[:].rearrange("p h (k a) -> p h k a", k=TOPK)
                for m, (op, arg) in enumerate([(ALU.logical_shift_right, 4), (ALU.bitwise_and, 15)]):
                    ts(posi[:], pos[:], arg, None, op)
                    v.drain()
                    v.tensor_copy(posf[:], posi[:])
                    v.drain()
                    flat = cand[:].rearrange("p h (k a) -> p (h k) a", k=TOPK)
                    tt(flat, posf[:].unsqueeze(2).to_broadcast([P, P, TOPK]),
                       iota16[:].unsqueeze(1).to_broadcast([P, P, TOPK]), ALU.is_equal)
                    v.drain()
                    half = topf[:].rearrange("p (h c) k -> p h c k", c=2)[:, :, m, :]
                    tt(c3, c3, half.unsqueeze(2).to_broadcast([P, PH, TOPK, TOPK]), ALU.mult)
                    v.drain()
                    v.tensor_reduce(pick[:, m, :], flat, AX_X, ALU.add)
                dve.wait_ge(s_gexp, b + 1)
                g3 = pick[:, 2, :].rearrange("p (h k) -> p h k", h=PH)
                v.tensor_reduce(gsum[:, PH:2 * PH], g3, AX_X, ALU.add)
                v.drain()
                v.reciprocal(gsum[:, PH:2 * PH], gsum[:, PH:2 * PH])
                v.drain()
                tt(g3, g3, gsum[:, PH:2 * PH].unsqueeze(2).to_broadcast([P, PH, TOPK]),
                   ALU.mult).then_inc(s_pick, 1)
                dve.wait_ge(s_pkT, b + 1)
                v.tensor_copy(pickT[:, 0:2, :], bank[7][:, 0:2 * P].rearrange("p (a n) -> p a n", a=2))
                v.tensor_copy(gTh[:], bank[7][:, 2 * P:3 * P])
                v.drain()
                tt(pickT[:, 3, :], bank[7][:, 2 * P:3 * P], gTh[:].bitcast(F32), ALU.subtract)
                v.tensor_copy(pickT[:, 2, :], gTh[:].bitcast(F32)).then_inc(s_pkc, 1)
                v.drain()

            def onehots(b):
                def one(i, r, free):
                    q = i * OH + (32 * b + r)
                    if free:
                        dve.wait_ge(s_gp, q + (2 - OH))

                    def spread(row, s):
                        tok = bass.ds(i * (OH * TOK4) + (r + s) * TOK4, TOK4)
                        return pickT[:, row, tok].unsqueeze(2).to_broadcast([P, TOK4, P])
                    lane = iotaN[:].unsqueeze(1).to_broadcast([P, TOK4, P])

                    def by_tok(ap):
                        return ap.rearrange("p (t n) -> p t n", t=TOK4)
                    for s in range(2):
                        tt(ohE(b, r + s), lane, spread(0, s), ALU.is_equal)
                    for s in range(2):
                        tt(by_tok(ohJ[:, r + s, :]), lane, spread(1, s), ALU.is_equal)
                    v.drain()
                    for s in range(2):
                        tt(by_tok(ohIh[:, r + s, :]), ohE(b, r + s), spread(2, s),
                           ALU.mult).then_inc(s_oh, 1)
                v.drain()
                if b == 0:
                    for r in range(0, OH, 2):
                        one(0, r, False)
                with dve.Fori(1 if b == 0 else 0, 32 // OH) as i:
                    for r in range(0, OH, 2):
                        one(i, r, True)

            v.drain()
            for b in range(NB):
                retrieve(b)
                onehots(b)

            def up_tile(t, j, free):
                def low():
                    dve.wait_ge(s_chi, t + 1)
                    tt(clo[:, j % 2, :], coef[:, j % 2, :], chi[:, j % 2, :].bitcast(F32),
                       ALU.subtract).then_inc(s_clo, 1)
                dve.wait_ge(s_ain[j], (t - j) * 4 + 16)
                dve.wait_ge(s_gin[j], (t - j) * 4 + 16)
                tt(coef[:, j % 2, :], a_in[:, j, :], g_in[:, j, :], ALU.mult).then_inc(s_cf, 1)
                v.drain()
                low()

            for t in range(4):
                up_tile(t, t, t >= 2)
            with dve.Fori(1, N_TILES // 4) as i:
                for j in range(4):
                    up_tile(i * 4 + j, j, True)
            dve.wait_ge(s_yq, 1)
            v.tensor_reduce(rstd, ssq2.rearrange("p (b a) -> p b a", a=2), AX_X, ALU.add)
            v.drain()
            ts(rstd, rstd, 1.0 / D, EPS, ALU.mult, ALU.add).then_inc(s_ym, 1)
            dve.wait_ge(s_yr, 1)
            v.reciprocal(rstd, rstd)
            v.drain()
            dve.wait_ge(s_x1l, 16 * NB)
            for b in range(NB):
                for half in range(2):
                    w = slice(half * 512, (half + 1) * 512)
                    stt(out=yo[:, b, w], in0=bank[2 * b + half][:], scalar=rstd[:, b:b + 1],
                        in1=gate_f[:, w], op0=ALU.mult, op1=ALU.mult)
                v.drain()
                tt(yo[:, b, :], yo[:, b, :], x1[:, b, :], ALU.add).then_inc(s_yo, 1)


def kernel(**inputs):
    import numpy as np
    import concourse.bacc as bacc
    from concourse import mybir as mb
    from concourse.bass_utils import run_bass_kernel_spmd

    a = {k: np.asarray(v) for k, v in inputs.items()}
    w_mod = a["w_mod"][0].reshape(D, 6, KD, P).transpose(1, 2, 3, 0)
    b_mod = a["b_mod"][0].reshape(6, KD, P)

    def column_tiles(w):
        n = w.shape[1] // P
        return w.reshape(KD, P, n, P).transpose(2, 1, 0, 3).reshape(n, P, D)

    def natural_tiles(w):
        n = w.shape[1] // 512
        return w.reshape(4, 2, P, n, 512).transpose(3, 0, 2, 1, 4).reshape(4 * n, P, D)

    w_in = a["w_in"][0]
    A = 512
    qa, ka, va = w_in[:, 0:A], w_in[:, A:2 * A], w_in[:, 2 * A:3 * A]
    qkv, z = w_in[:, 3 * A:6 * A], w_in[:, 6 * A:7 * A]
    ba = w_in[:, 7 * A:7 * A + 2 * H]
    down = a["expert_down"][0].reshape(N_TILES, P, KD, P).transpose(0, 3, 2, 1).reshape(N_TILES, P, D)
    up = a["expert_up"][0].reshape(N_TILES, P, D)
    arrays = {
        "x": a["x"].reshape(NB, P, D),
        "c": a["c"].reshape(D),
        "mod_tiles": np.stack([w_mod[mod_order(m)] for m in range(N_MOD)]),
        "mod_bias_col": b_mod.transpose(2, 0, 1),
        "gain_cols": np.concatenate([a["pre_mix_gain"], a["pre_ffn_gain"], a["post_mix_gain"],
                                     a["post_ffn_gain"]]).reshape(4, KD, P).transpose(2, 0, 1),
        "in_tiles": np.concatenate([natural_tiles(va), natural_tiles(z),
                                    np.stack([column_tiles(ka), column_tiles(qa)], 1).reshape(8, P, D),
                                    column_tiles(qkv)]),
        "ba_w": ba.reshape(KD, P, 2 * H).transpose(1, 0, 2),
        "conv_col": a["conv_w"][0].reshape(4, 12, P).transpose(2, 1, 0).reshape(P, 48),
        "a_log": a["a_log"][0],
        "dt_bias": a["dt_bias"][0],
        "lambdas": np.concatenate([a[f"lambda_{n}"][0] for n in ("q1", "q2", "k1", "k2")]),
        "head_gains": np.concatenate([a["attn_norm_gain"][0], a["gdn_norm_gain"][0]]),
        "out_tiles": natural_tiles(a["w_out"][0]),
        "query_tiles": column_tiles(a["w_query"][0]),
        "keys_t": a["sub_keys"][0].reshape(2 * PH, P, P).transpose(2, 0, 1),
        "expert_tiles": np.concatenate([down, up]),
    }
    nc = bacc.Bacc("TRN2", target_bir_lowering=False, num_devices=1)
    feed, args = {}, []
    for name, v in arrays.items():
        v = np.ascontiguousarray(v)
        feed[f"in_{name}"] = v
        args.append(nc.dram_tensor(f"in_{name}", v.shape, mb.dt.from_np(v.dtype), kind="ExternalInput").ap())
    out = nc.dram_tensor("out", (NB, P, D), mb.dt.from_np(np.dtype("float32")), kind="ExternalOutput").ap()
    build(nc, *args, out)
    r = run_bass_kernel_spmd(nc, [feed], core_ids=[0])
    return r.results[0]["out"].reshape(1, SEQ, D)
```

```python
import math
from contextlib import ExitStack

import concourse.bass as bass
from concourse import mybir

F32 = mybir.dt.float32
F32R = mybir.dt.float32r
BF16 = mybir.dt.bfloat16
I32 = mybir.dt.int32
U32 = mybir.dt.uint32
ALU = mybir.AluOpType
ACT = mybir.ActivationFunctionType
AX_X = mybir.AxisListType.X

P = 128
D = 1024
SEQ = 512
KD = D // P
NB = SEQ // P
H = 4
HD = 128
QK = 64
CH = 64
NCH = SEQ // CH
EPS = 1e-6
NEG = -1e30
LOWEST = -3.4e38
LAMBDA_INIT = 0.8 - 0.6 * math.exp(0.0)
PH = 8
TOPK = 16
N_TILES = 128

T_VA, T_Z, T_KQ, T_GDN, T_OUT, T_QUERY = 0, 4, 8, 16, 28, 36
SLOT0 = T_KQ + 2
N_MOD = 48
T_DOWN = 52
T_UP = T_DOWN + N_TILES
T_ALL = T_UP + N_TILES
RAW = 4
SPLIT = 2
AHEAD = RAW + 1

LEAD, BUILD, REST = 12, 16, (16, 12, 12, 12)
START = [LEAD + b * BUILD + sum(REST[:b]) for b in range(NB)]
STORE = 8
RING = 2
OH = 4
TOK4 = 4


def mod_order(m):
    half, r = divmod(m, 24)
    return (3 * half + r % 2, r // 2) if r < 16 else (3 * half + 2, r - 16)


def build(nc, x, c, mod_tiles, mod_bias_col, gain_cols, in_tiles,
          ba_w, conv_col, a_log, dt_bias, lambdas, head_gain_cols, out_tiles, query_tiles, keys_t,
          expert_tiles, out):
    act_dram = nc.dram_tensor("act_scratch", (N_TILES, P, SEQ), F32).ap()
    gate_dram = nc.dram_tensor("gate_scratch", (N_TILES, P, SEQ), F32).ap()
    x1_dram = nc.dram_tensor("x1_scratch", (NB, P, D), F32).ap()
    with ExitStack() as ctx:
        def sem(name):
            return ctx.enter_context(nc.semaphore(name))

        cursor = [17408]

        def at(name, shape, dt, offset=None):
            size = 2 if dt == BF16 else 4
            for n in shape[1:]:
                size *= n
            offset = cursor[0] if offset is None else offset
            cursor[0] = offset + (size + 31) // 32 * 32
            assert cursor[0] <= 229344, (name, cursor[0])
            return nc.alloc_sbuf_tensor_at(name, shape, dt, offset=offset)

        ident = at("ident", [P, P], F32)
        acol = at("acol", [P, 2, KD], F32)
        bcol = at("bcol", [P, 2, KD], F32)
        gaincol = at("gaincol", [P, 4, KD], F32)
        modbcol = at("modbcol", [P, 6, KD], F32)
        small = at("small", [P, 64], F32)
        iota16 = at("iota16", [P, TOPK], BF16)
        iotaN = at("iotaN", [P, P], F32)
        gate_m_at = cursor[0]
        gate_m = at("gate_m", [P, D], F32)
        gate_f = at("gate_f", [P, D], F32)
        raw = at("raw", [P, RAW, D], F32)
        whi = at("whi", [P, SPLIT, D], F32R)
        wlo = at("wlo", [P, SPLIT, D], F32R)
        acts = cursor[0]
        act_hi = at("act_hi", [P, KD, SEQ], F32R)
        act_lo = at("act_lo", [P, KD, SEQ], F32R)
        phase = cursor[0]

        xn = at("xn", [P, NB, D], F32)
        kbeg = at("kbeg", [P, NB, 512], F32, phase)
        kdec = at("kdec", [P, NB, 512], F32)
        modx = at("modx", [P, 4, D], F32, phase)
        l2r = at("l2r", [P, 8, SEQ], F32, phase)
        modr = at("modr", [P, 8, D], F32)
        cursor[0] -= 4 * D * 4
        onat = at("onat", [P, NB, D], F32, cursor[0] - 4 * D * 4)
        xs2 = at("xs2", [P, NB, D], F32, cursor[0] - 4 * D * 4)
        kq = cursor[0]
        kaT = at("kaT", [P, H, SEQ], F32)
        qaT = at("qaT", [P, H, SEQ], F32)
        osq = at("osq", [P, NB * D], F32, kq)
        va = at("va", [P, NB, 512], F32)
        zs = at("zs", [P, NB, 512], F32)
        qkvT = at("qkvT", [P, 12, SEQ], F32)
        u = at("u", [P, NB, 512], F32, cursor[0] - 4 * SEQ * 4)
        t_base = cursor[0]
        Tm = at("Tm", [P, NB, 512], F32)
        TT = at("TT", [P, NB, 512], F32)
        PM = at("PM", [P, NB, 512], F32)
        after_t = cursor[0]
        bias = at("bias", [P, 2, 512], F32, t_base)
        pr = at("pr", [P, 2, 2, 512], F32)
        pT = at("pT", [P, 2, 512], F32)
        rel = at("rel", [P, 512], F32)
        negm = at("negm", [P, 512], F32)
        wk = at("wk", [P, 4, 512], F32, t_base + 2 * 512 * 4)
        vbeta = at("vbeta", [P, NB, 512], F32, after_t)
        c_row = at("c_row", [P, D], F32, after_t + D * 4)
        masks = at("masks", [P, 10, P], F32)
        state = at("state", [P, 512], F32)
        vnew = at("vnew", [P, 512], F32)
        ones = at("ones", [P, P], F32, cursor[0] - 512 * 4)
        mrow = at("mrow", [P, 576], F32, cursor[0] + 3 * P * 4)
        gsm = at("gsm", [P, 288], F32)
        baw = at("baw", [P, KD, 8], F32)
        modcol = at("modcol", [P, 6, KD], F32)
        gcol = at("gcol", [P, 2, KD], F32)
        baT = at("baT", [8, SEQ], F32, kq + 2 * H * SEQ * 4 - SEQ * 4)
        baw_hi = at("baw_hi", [P, KD, 8], F32R, after_t + 2048)
        baw_lo = at("baw_lo", [P, KD, 8], F32R)
        xij = at("xij", [P, 2, P], I32, after_t)
        LT = at("LT", [P, NB, 512], F32, acts)
        LM = at("LM", [P, NB, 512], F32)
        QKT = at("QKT", [P, NB, 512], F32)
        wT = at("wT", [P, NB, 512], F32)
        egT = at("egT", [P, NB, 512], F32, cursor[0] - NB * 512 * 4)
        gB = at("gB", [P, 16, P], F32, cursor[0] - NB * 512 * 4)
        carried = vbeta[:, 0, :]

        M_INCL, M_STRICT, M_U, M_FIRST, MT = 0, 1, 2, 3, 4

        def mask4(m):
            return masks[:, m, :].unsqueeze(1).to_broadcast([P, H, P])

        def by_head(ap):
            return ap.rearrange("p (h n) -> p h n", h=H)

        conv_w = mrow[:, 0:48].rearrange("p (n j) -> p n j", n=12)
        hgain = mrow[:, 48:50]
        lam_in = mrow[:, 304:560]
        lam = mrow[:, 560:564]
        eps_t = small[:, 0:1]
        ssq = small[:, 4:8]
        rstd = small[:, 8:12]
        ssq2 = small[:, 32:40]
        asm = small[:, 40:52].rearrange("p (s v) -> p s v", s=2)
        rx = small[:, 56:60]
        G_BETA, G_Y, G_AY, G_SP, G_CUM, G_EXP, G_DEC, G_BEXP, G_LOG = range(9)

        VK_STEPS = (5, 8, 11, 14)
        ROW_BANK = [0, 2, 3, 1]
        SUM_BANK = [2, 3, 4, 5, 6, 4, 5, 6]

        def g16(i):
            return gsm[:, 16 * i:16 * i + 16]

        g_last = gsm[:, 144:176]
        o_ms = gsm[:, 176:208]

        def heads(g0):
            return o_ms.rearrange("p (b g) -> p b g", b=NB)[:, :, g0:g0 + 4]
        alog4 = gsm[:, 208:212]
        dt4 = gsm[:, 212:216]

        bank = [ctx.enter_context(nc.psum_tensor(f"bank{i}", [P, 512], F32)) for i in range(8)]

        cursor[0] = phase
        S = at("S", [P, NB, 2 * PH, P], F32)
        stage = at("stage", [P, P, P], F32)
        keys = at("keys", [P, 2 * PH, P], F32, cursor[0] - P * P * 4)
        qTs = at("qTs", [P, 2, SEQ], F32)
        hfl2 = at("hfl2", [P, 4, SEQ], F32)
        cursor[0] = phase + (32 + 64) * 1024
        aout = at("aout", [P, 2, SEQ], F32)
        cand_at = cursor[0]
        cand = at("cand", [P, PH, 256], F32)
        cursor[0] = cand_at + OH * TOK4 * 2 * P * 4
        top = at("top", [P, 2 * PH, TOPK], F32)
        topi = at("topi", [P, 2 * PH, TOPK], U32)
        topf = at("topf", [P, 2 * PH, TOPK], BF16)
        best = at("best", [P, PH, TOPK], F32)
        pos = at("pos", [P, P], U32)
        posi = at("posi", [P, P], U32)
        posf = at("posf", [P, P], BF16)
        pick = at("pick", [P, 3, P], F32)
        gsum = at("gsum", [P, 2 * PH], F32)
        pickT = at("pickT", [P, 4, P], F32)
        gTh = at("gTh", [P, P], F32R)
        ohJ = at("ohJ", [P, OH, TOK4 * P], F32R)
        ohI = at("ohI", [P, OH * TOK4, 2, P], F32R, cand_at)

        match = at("match", [P, PH, TOPK, TOPK], BF16, cand_at + PH * 256 * 4)

        def ohE(b, slot):
            return S[:, b, slot * TOK4:(slot + 1) * TOK4, :]
        glo = at("glo", [P, RING * TOK4, P], F32, gate_m_at)
        cursor[0] = phase
        a_in = at("a_in", [P, RAW, SEQ], F32)
        g_in = at("g_in", [P, RAW, SEQ], F32)
        coef = at("coef", [P, 2, SEQ], F32)
        chi = at("chi", [P, 2, SEQ], F32R)
        clo = at("clo", [P, 2, SEQ], F32R)
        x1 = at("x1", [P, NB, D], F32)
        yo = at("yo", [P, NB, D], F32)

        s_raw = [sem(f"raw_landed{i}") for i in range(RAW)]
        s_hi = sem("split_hi_ready")
        s_lo = sem("split_lo_ready")
        s_used = sem("split_used")
        s_x = sem("x_landed")
        s_crow = sem("c_landed")
        s_c = sem("consts_landed")
        s_hc = sem("head_consts_landed")
        s_mod8 = [sem(f"first_mod_landed{i}") for i in range(8)]
        s_modl = [sem(f"mod_landed{i}") for i in range(4)]
        s_modu = sem("mod_used")
        s_pool = sem("pool_consts")
        s_xij = sem("masks_made")
        s_cc = sem("c_silu")
        s_cols = sem("mod_columns_read")
        s_ssq = sem("sum_of_squares")
        s_msq = sem("mean_square")
        s_rt = sem("root")
        s_rst = sem("inverse_root")
        s_xs = sem("x_scaled")
        s_xs1 = sem("odd_x_scaled")
        s_xT = sem("x_transposed")
        s_hf = sem("h_float")
        s_hhi = sem("h_hi")
        s_hlo = sem("h_lo")
        s_conv = sem("conv_done")
        s_silu = sem("silu_done")
        s_kq = sem("attn_kq_copied")
        s_nat = sem("natural_tiles_copied")
        s_ba = sem("ba_done")
        s_gcol = sem("gate_columns")
        s_gsp = sem("gate_rows")
        s_gate = sem("gate_rows_copied")
        s_bas = sem("ba_weights_split")
        s_baT = sem("ba_columns")
        s_bac = sem("ba_columns_copied")
        s_sq = sem("qk_squares")
        s_l2 = sem("qk_norm_sums")
        s_l2r = sem("qk_norm_roots")
        s_l2e = sem("qk_inverse_norms")
        s_l2n = sem("qk_normed")
        s_lam = sem("lambda_sums")
        s_lame = sem("lambda_exp")
        s_sc = sem("attn_scores")
        s_mx = sem("attn_max")
        s_ex = sem("attn_exp")
        s_pd = sem("attn_diff")
        s_pt = sem("attn_transposed")
        s_ptc = sem("attn_transposed_copied")
        s_av = sem("attn_values")
        s_oa = sem("attn_out_copied")
        s_g1 = sem("gdn_rows")
        s_g1e = sem("gdn_rows_exp")
        s_gl = sem("gdn_log_decay")
        s_gB = sem("gdn_decay_spread")
        s_gc = sem("gdn_cumsum")
        s_gcc = sem("gdn_cumsum_copied")
        s_row = sem("gdn_decay_rows")
        s_du = [sem("gdn_decay_args_even"), sem("gdn_decay_args_odd")]
        s_de = sem("gdn_decay_exp")
        s_kg = sem("gdn_grams")
        s_L = sem("gdn_L")
        s_LT = sem("gdn_L_transposed")
        s_LTc = sem("gdn_LT_copied")
        s_t0 = sem("inv_first_T")
        s_vt = sem("gdn_vk_transposed")
        s_vtd = sem("gdn_vk_scaled")
        s_lm = sem("inv_masked")
        s_pp = sem("inv_P")
        s_pc = sem("inv_P_copied")
        s_tt = sem("inv_update")
        s_td = sem("inv_T_ready")
        s_uw = sem("gdn_uw")
        s_uwc = sem("gdn_uw_copied")
        s_arg = sem("gdn_decay_differences")
        s_mk = sem("gdn_decays_masked")
        s_qg = sem("q_decayed")
        s_car = sem("scan_state_decayed")
        s_osq = sem("gdn_head_squares")
        s_asq = sem("attn_head_squares")
        s_ams = sem("attn_mean_squares")
        s_amr = sem("attn_head_roots")
        s_amd = sem("attn_inverse_roots")
        s_ona = sem("attn_heads_normed")
        s_wS = sem("scan_wS")
        s_qS = sem("scan_qS")
        s_vn = sem("scan_vnew")
        s_kv = sem("scan_kv")
        s_qkv = sem("scan_outputs")
        s_st = sem("scan_state")
        s_oc = sem("scan_out_copied")
        s_oms = sem("head_mean_squares")
        s_omr = sem("head_roots")
        s_on = sem("heads_normed")
        s_oT = sem("o_transposed")
        s_ohi = sem("o_hi")
        s_olo = sem("o_lo")
        s_xr = sem("x_again_landed")
        s_rx = sem("x1_inverse_root")
        s_yg = sem("y_gated")
        s_x1 = [sem(f"x1_ready{b}") for b in range(NB)]
        s_x1o = sem("x1_stored")
        s_key = sem("keys_landed")
        s_qT = sem("query_copied")
        s_qs = sem("key_scores")
        s_S = sem("key_scores_copied")
        s_act = sem("gelu_done")
        s_ast = [sem(f"act_stored{i}") for i in range(2)]
        s_best = sem("topk_best")
        s_gexp = sem("topk_exp")
        s_pick = sem("picks_ready")
        s_pkT = sem("picks_transposed")
        s_pkc = sem("picks_copied")
        s_oh = sem("onehots_ready")
        s_ohl = sem("onehots_low_ready")
        s_gp = sem("gate_products")
        s_glo = sem("gate_products_low_copied")
        s_gev = sem("gates_staged")
        s_gst = sem("gates_stored")
        s_ain = [sem(f"act_landed{i}") for i in range(RAW)]
        s_gin = [sem(f"gates_landed{i}") for i in range(RAW)]
        s_cf = sem("coef_ready")
        s_chi = sem("coef_hi")
        s_clo = sem("coef_lo")
        s_x1l = sem("x1_landed")
        s_yq = sem("y_squares")
        s_ym = sem("y_mean_square")
        s_yr = sem("y_root")
        s_yo = sem("out_ready")
        s_out = sem("out_stored")

        def raw_wait(eng, n):
            eng.wait_ge(s_raw[n % RAW], 16 * (n // RAW + 1))

        block = ctx.enter_context(nc.Block())

        @block.sync
        def _(sp):
            dq = sp.dma_start
            dq(c_row[:], c.partition_broadcast(P)).then_inc(s_crow, 16)
            for b in range(NB):
                dq(xn[:, b, :], x[b]).then_inc(s_x, 16)
            for dst, src in [(gaincol[:], gain_cols), (modbcol[:], mod_bias_col), (baw[:], ba_w)]:
                dq(dst, src).then_inc(s_c, 16)

            def load_mod(m):
                if m == 16:
                    sp.wait_ge(s_xT, KD)
                if 8 <= m < 16:
                    sp.wait_ge(s_modu, m - 7)
                if m >= 20:
                    sp.wait_ge(s_modu, m - 3)
                dst, landed = (modr[:, m % 8, :], s_mod8[m % 8]) if m < 16 else \
                    (modx[:, m % 4, :], s_modl[m % 4])
                dq(dst, mod_tiles[m]).then_inc(landed, 16)

            def load_raw(n, src):
                if n >= RAW:
                    sp.wait_ge(s_lo, n - RAW + 1)
                dq(raw[:, n % RAW, :], src).then_inc(s_raw[n % RAW], 16)

            for m in range(16):
                load_mod(m)
                if m in (7, 9, 11, 13):
                    load_raw((m - 7) // 2, in_tiles[(m - 7) // 2])
            for dst, src in [(mrow[:, 0:48], conv_col),
                             (hgain, head_gain_cols),
                             (alog4, a_log.partition_broadcast(P)),
                             (dt4, dt_bias.partition_broadcast(P)),
                             (lam_in, lambdas.partition_broadcast(P))]:
                dq(dst, src).then_inc(s_hc, 16)
            for n in range(4, T_OUT):
                load_raw(n, in_tiles[n])
                for m in range(2 * n + 8, min(2 * n + 10, N_MOD)):
                    load_mod(m)
            for n in range(8):
                load_raw(T_OUT + n, out_tiles[n])
            sp.wait_ge(s_on, NB)
            for b in range(NB):
                dq(xn[:, b, :], x[b]).then_inc(s_xr, 16)
            for n in range(4):
                load_raw(T_QUERY + n, query_tiles[n])
            for b in range(NB):
                sp.wait_ge(s_x1[b], 1)
                dq(x1_dram[b], xn[:, b, :]).then_inc(s_x1o, 16)
            sp.wait_ge(s_hlo, 2 * KD)
            sp.wait_ge(s_x1o, 16 * NB)
            dq(keys[:], keys_t).then_inc(s_key, 16)
            for n in range(4, 16):
                load_raw(T_QUERY + n, query_tiles[n])

            for n in range(AHEAD):
                load_raw(T_DOWN + n, expert_tiles[n])

            def down_tiles(t0, count, gates_of=None):
                with sp.Fori(0, count // 4) as i:
                    for j in range(4):
                        t = i * 4 + (t0 + j)
                        sp.wait_ge(s_act, t + 1)
                        dq(act_dram[t], aout[:, j % 2, :]).then_inc(s_ast[j % 2], 16)
                        sp.wait_ge(s_lo, t + (T_DOWN + AHEAD - RAW + 1))
                        slot = (T_DOWN + AHEAD + j) % RAW
                        dq(raw[:, slot, :], expert_tiles[t + AHEAD]).then_inc(s_raw[slot], 16)
                        if gates_of is not None:
                            e = i * 64 + j * 16
                            dq(gate_dram[bass.ds(e, 16), :, gates_of * P:(gates_of + 1) * P]
                               .rearrange("i j t -> j i t"), stage[:, bass.ds(e, 16), :]).then_inc(s_gst, 16)

            down_tiles(0, LEAD)
            for b in range(NB):
                down_tiles(START[b], BUILD)
                lead = 0 if b == NB - 1 else REST[b] - STORE
                if lead:
                    down_tiles(START[b] + BUILD, lead)
                sp.wait_ge(s_gev, RING + 32 * (b + 1))
                down_tiles(START[b] + BUILD + lead, STORE, b)
            done = START[b] + BUILD + STORE
            sp.wait_ge(s_gst, 16 * STORE * NB)
            for r in range(2):
                sp.wait_ge(s_ast[r], 16 * (done // 2))
            for r in range(RAW):
                dq(a_in[:, r, :], act_dram[r]).then_inc(s_ain[r], 16)
                dq(g_in[:, r, :], gate_dram[r]).then_inc(s_gin[r], 16)
            down_tiles(done, N_TILES - done)

            for r in range(2):
                sp.wait_ge(s_ast[r], 16 * (N_TILES // 2))
            for b in range(NB):
                dq(x1[:, b, :], x1_dram[b]).then_inc(s_x1l, 16)

            def up_tile(t, j, more):
                slot = (T_UP + AHEAD + j) % RAW
                if more:
                    sp.wait_ge(s_lo, t + (T_UP + AHEAD - RAW + 1))
                    dq(raw[:, slot, :], expert_tiles[t + (N_TILES + AHEAD)]).then_inc(s_raw[slot], 16)
                sp.wait_ge(s_cf, t + 1)
                dq(a_in[:, j, :], act_dram[t + RAW]).then_inc(s_ain[j], 16)
                dq(g_in[:, j, :], gate_dram[t + RAW]).then_inc(s_gin[j], 16)

            with sp.Fori(0, N_TILES // 4 - 2) as i:
                for j in range(4):
                    up_tile(i * 4 + j, j, True)
            for t in range(N_TILES - 8, N_TILES - 4):
                up_tile(t, t % 4, t + AHEAD < N_TILES)
            for b in range(NB):
                sp.wait_ge(s_yo, b + 1)
                dq(out[b], yo[:, b, :]).then_inc(s_out, 16)
            sp.wait_ge(s_out, 16 * NB)

        @block.gpsimd
        def _(pool):
            g = nc.gpsimd
            g.memset(ident[:], 0.0)
            g.memset(ones[:], 1.0)
            g.memset(small[:, 0:1], EPS)
            g.iota(xij[:, 0, :], pattern=[[0, P]], base=0, channel_multiplier=1)
            g.iota(xij[:, 1, :], pattern=[[1, P]], base=0, channel_multiplier=0)
            g.iota(rel[:], pattern=[[-1, 512]], base=384, channel_multiplier=1,
                   allow_small_or_imprecise_dtypes=True)
            g.iota(iota16[:], pattern=[[1, TOPK]], base=0, channel_multiplier=0,
                   allow_small_or_imprecise_dtypes=True)
            g.iota(iotaN[:], pattern=[[1, P]], base=0, channel_multiplier=0,
                   allow_small_or_imprecise_dtypes=True)
            g.drain()
            g.affine_select(out=ident[:], in_=ident[:], compare_op=ALU.not_equal, fill=1.0, base=0,
                            pattern=[[-1, P]], channel_multiplier=1).then_inc(s_pool, 1)
            def lo(n, j):
                pool.wait_ge(s_hi, n + 1)
                g.tensor_tensor(wlo[:, j % SPLIT, :], raw[:, j % RAW, :],
                                whi[:, j % SPLIT, :].bitcast(F32), ALU.subtract).then_inc(s_lo, 1)

            def lows(t0, t1):
                with pool.Fori(0, (t1 - t0) // RAW) as i:
                    for j in range(RAW):
                        lo(i * RAW + (t0 + j), t0 + j)

            def lows_and_onehots(t0, b):
                with pool.Fori(0, BUILD // RAW) as i:
                    for j in range(RAW):
                        lo(i * RAW + (t0 + j), t0 + j)
                        for r in range(2):
                            slot = 2 * j + r
                            pool.wait_ge(s_oh, i * 8 + (32 * b + slot + 1))
                            tok = bass.ds(i * 32 + slot * TOK4, TOK4)
                            g.tensor_tensor(ohI[:, slot % OH * TOK4:(slot % OH + 1) * TOK4, 1, :],
                                            ohE(b, slot % OH),
                                            pickT[:, 3, tok].unsqueeze(2).to_broadcast([P, TOK4, P]),
                                            ALU.mult).then_inc(s_ohl, 1)

            def by_head(ap):
                return ap.rearrange("p (h n) -> p h n", h=H)

            lows(0, T_OUT)
            for t in range(0, NB, 2):
                pool.wait_ge(s_arg, t + 1)
                g.tensor_tensor(by_head(LM[:, t, :]), by_head(QKT[:, t, :]), mask4(M_INCL), ALU.mult)
                g.drain()
                g.tensor_tensor(by_head(QKT[:, t, :]), by_head(QKT[:, t, :]), mask4(M_U),
                                ALU.mult).then_inc(s_du[0], 1)
            for t in range(NB):
                pool.wait_ge(s_de, t + 1)
                g.tensor_tensor(by_head(LM[:, t, :]), by_head(LM[:, t, :]), mask4(M_STRICT),
                                ALU.mult).then_inc(s_mk, 1)
                g.tensor_tensor(by_head(QKT[:, t, :]), by_head(QKT[:, t, :]), mask4(M_U),
                                ALU.mult).then_inc(s_mk, 1)
            for t in range(NB):
                pool.wait_ge(s_L, t + 1)
                g.tensor_tensor(by_head(Tm[:, t, :]), by_head(LM[:, t, :]), mask4(M_FIRST), ALU.mult)
                g.drain()
                g.tensor_tensor(by_head(Tm[:, t, :]), ident[:].unsqueeze(1).to_broadcast([P, H, P]),
                                by_head(Tm[:, t, :]), ALU.subtract).then_inc(s_t0, 1)
            pool.wait_ge(s_kg, NB)
            pool.wait_ge(s_de, NB + 1)
            for t in range(NB):
                q = qkvT[:, 0:H, t * P:(t + 1) * P]
                last = g.tensor_tensor(q, q, by_head(egT[:, t, :]), ALU.mult)
            last.then_inc(s_qg, 1)
            pool.wait_ge(s_uw, NB)
            for c in range(NCH - 1):
                pool.wait_ge(s_st, c + 1)
                g.tensor_tensor(by_head(carried), by_head(state[:]),
                                g_last[:, 4 * c:4 * c + 4].unsqueeze(2).to_broadcast([P, H, P]),
                                ALU.mult).then_inc(s_car, 1)
                if c >= 3:
                    b = c - 3
                    if b == 0:
                        pool.wait_ge(s_amd, 1)
                    o = by_head(onat[:, b, 0:512])
                    g.tensor_tensor(o, o, o_ms[:, 8 * b:8 * b + 4].unsqueeze(2).to_broadcast([P, H, P]),
                                    ALU.mult).then_inc(s_ona, 1)

            lows(T_OUT, T_QUERY)
            pool.wait_ge(s_xr, 16 * NB)
            for b in (0, 2):
                pool.wait_ge(s_yg, b // 2 + 1)
                g.tensor_tensor(xn[:, b, :], xn[:, b, :], xs2[:, b, :], ALU.add).then_inc(s_x1[b], 1)
            first = T_DOWN + LEAD
            lows(T_QUERY, first)
            lo(first, first)
            for b in range(NB):
                t = T_DOWN + START[b] + 1
                lows_and_onehots(t, b)
                lows(t + BUILD, t + BUILD + REST[b])
            lows(t + BUILD + REST[b], T_ALL - 3)
            for n in range(T_ALL - 3, T_ALL):
                lo(n, n)

        @block.scalar
        def _(act):
            sc = nc.scalar

            def hi(n):
                raw_wait(act, n)
                if n >= SPLIT:
                    act.wait_ge(s_used, n - SPLIT + 1)
                sc.copy(whi[:, n % SPLIT, :], raw[:, n % RAW, :]).then_inc(s_hi, 1)

            act.wait_ge(s_crow, 16)
            sc.activation(c_row[:], c_row[:], ACT.Silu).then_inc(s_cc, 1)
            act.wait_ge(s_x, 16 * NB)
            for b in range(NB):
                sc.activation(qkvT[:, 0:2, :], xn[:, b, :].rearrange("p (a n) -> p a n", a=2),
                              ACT.Square, accum_out=ssq[:, b:b + 1]).then_inc(s_ssq, 1)
                act.wait_ge(s_ssq, b + 1)
            act.wait_ge(s_msq, 1)
            sc.activation(rstd, rstd, ACT.Sqrt).then_inc(s_rt, 1)
            act.wait_ge(s_rst, 1)
            for b in range(NB):
                last = sc.mul(xn[:, b, :], xn[:, b, :], rstd[:, b:b + 1])
            last.then_inc(s_xs, 1)
            act.wait_ge(s_c, 16 * 3)
            sc.copy(baw_hi[:], baw[:]).then_inc(s_bas, 1)
            act.wait_ge(s_xij, 1)

            def shifted(half, buf):
                for k in range(KD + 1):
                    if k < KD:
                        act.wait_ge(s_xT, KD * half + k + 1)
                        act.wait_ge(s_cols, k // 2 + 1 if half == 0 else 5)
                        if k >= 4:
                            act.wait_ge(s_hlo, KD * half + k - 3)
                        sc.activation(buf[:, k % 4, :], bank[6 + k % 2][:], ACT.Identity,
                                      bias=bcol[:, half, k:k + 1],
                                      scale=acol[:, half, k:k + 1]).then_inc(s_hf, 1)
                    if k >= 1:
                        act.wait_ge(s_hf, KD * half + k)
                        sc.copy(act_hi[:, k - 1, :], buf[:, (k - 1) % 4, :]).then_inc(s_hhi, 1)
                    if half == 0 and k in (1, 3, 5, 7):
                        hi((k - 1) // 2)

            shifted(0, wk)
            for n in range(T_Z - 2, T_Z):
                hi(n + 2)
            act.wait_ge(s_used, T_Z)
            for b in range(NB):
                sc.copy(va[:, b, :], bank[b][:]).then_inc(s_nat, 1)
            for n in range(T_Z, T_KQ):
                hi(n + 2)
            act.wait_ge(s_used, T_KQ)
            for b in range(NB):
                sc.activation(zs[:, b, :], bank[4 + b][:], ACT.Silu).then_inc(s_nat, 1)

            def kq_copy(n):
                act.wait_ge(s_used, n + 1)
                h = (n - T_KQ) // 2
                dst, scale = (qaT, QK ** -0.5) if (n - T_KQ) % 2 else (kaT, 1.0)
                sc.mul(dst[:, h, :], bank[n % 2][:], scale).then_inc(s_kq, 1)

            hi(T_KQ + 2)
            kq_copy(T_KQ)
            hi(T_KQ + 3)
            kq_copy(T_KQ + 1)
            act.wait_ge(s_lam, 1)
            sc.activation(lam[:, 0:2], lam[:, 0:2], ACT.Exp).then_inc(s_lame, 1)
            act.wait_ge(s_g1, 1)
            sc.activation(g16(G_BETA), g16(G_BETA), ACT.Exp, scale=-1.0)
            sc.activation(g16(G_SP), g16(G_AY), ACT.Exp, scale=-1.0)
            sc.activation(alog4, alog4, ACT.Exp)
            sc.drain()
            sc.activation(g16(G_SP), g16(G_SP), ACT.Ln, bias=1.0).then_inc(s_g1e, 1)

            def exps(i):
                act.wait_ge(s_mx, i + 1)
                n = (i % NB + 1) * P
                for m in range(2):
                    last = sc.activation(pr[:, i % 2, m, 0:n], pr[:, i % 2, m, 0:n], ACT.Exp,
                                         bias=asm[:, i % 2, 2 + m:3 + m],
                                         accum_out=asm[:, i % 2, 4 + m:5 + m])
                last.then_inc(s_ex, 1)

            def copy_t(i):
                act.wait_ge(s_pt, i + 1)
                if i >= 2:
                    act.wait_ge(s_av, i - 1)
                n = (i % NB + 1) * P
                sc.copy(pT[:, i % 2, 0:n], bank[6][:, 0:n]).then_inc(s_ptc, 1)

            for s in range(T_OUT - SLOT0):
                hi(SLOT0 + s + 2)
                if SLOT0 + s < T_GDN:
                    kq_copy(SLOT0 + s)
                if s < H * NB:
                    exps(s)
                if 1 <= s <= H * NB:
                    copy_t(s - 1)
                if s in (10, 14):
                    g = (s - 10) // 4
                    act.wait_ge(s_conv, 4 * g + 4)
                    sc.activation(qkvT[:, 4 * g:4 * g + 4, :], qkvT[:, 4 * g:4 * g + 4, :],
                                  ACT.Silu).then_inc(s_silu, 1)
                    if g == 0:
                        act.wait_ge(s_modu, N_MOD)
                    act.wait_ge(s_silu, g + 1)
                    for n in range(4 * g, 4 * g + 4):
                        sc.activation(l2r[:, n, :], qkvT[:, n, :], ACT.Square).then_inc(s_sq, 1)
            for n in range(8):
                act.wait_ge(s_l2, n + 1)
                sc.activation(l2r[:, n, :], bank[SUM_BANK[n]][:], ACT.Ln, bias=eps_t).then_inc(s_l2r, 1)
            for n in range(8):
                act.wait_ge(s_l2r, n + 1)
                sc.activation(l2r[:, n, :], l2r[:, n, :], ACT.Exp, scale=-0.5).then_inc(s_l2e, 1)

            for t in range(NB):
                act.wait_ge(s_du[t % 2], t // 2 + 1)
                sc.activation(QKT[:, t, :], QKT[:, t, :], ACT.Exp)
                last = sc.activation(LM[:, t, :], LM[:, t, :], ACT.Exp, scale=-1.0)
                if t == NB - 1:
                    sc.activation(g16(G_EXP), g16(G_CUM), ACT.Exp)
                    sc.activation(g16(G_DEC), g16(G_DEC), ACT.Exp)
                    last = sc.activation(g_last, g_last, ACT.Exp)
                last.then_inc(s_de, 1)
            act.wait_ge(s_row, NB)
            for t in range(NB):
                last = sc.activation(egT[:, t, :], bank[ROW_BANK[t]][:], ACT.Exp)
            last.then_inc(s_de, 1)
            for t in range(NB):
                act.wait_ge(s_LT, t + 1)
                sc.copy(LT[:, t, :], bank[4 + t % 2][:]).then_inc(s_LTc, 1)
            act.wait_ge(s_conv, 12)
            sc.activation(qkvT[:, 8:12, :], qkvT[:, 8:12, :], ACT.Silu).then_inc(s_silu, 1)
            for k in range(1, 6):
                for t in range(NB):
                    n = (k - 1) * NB + t
                    act.wait_ge(s_pp, n + 1)
                    if k > 1:
                        act.wait_ge(s_tt, n - NB + 1)
                    sc.copy(PM[:, t, :], bank[t % 2][:]).then_inc(s_pc, 1)
            for t in range(NB):
                act.wait_ge(s_uw, t + 1)
                if t == 0:
                    act.wait_ge(s_qg, 1)
                sc.copy(u[:, t, :], bank[2 * (t % 2)][:])
                sc.copy(wT[:, t, :], bank[2 * (t % 2) + 1][:]).then_inc(s_uwc, 1)

            def gate_copy(g):
                act.wait_ge(s_gsp, g + 1)
                for half in range(2):
                    last = sc.copy((gate_m, gate_f)[g][:, half * 512:(half + 1) * 512], bank[6 + half][:])
                last.then_inc(s_gate, 1)

            def head_squares(b, g0):
                for g in range(g0, g0 + H):
                    last = sc.activation(TT[:, b, (g % H) * HD:(g % H + 1) * HD],
                                         onat[:, b, g * HD:(g + 1) * HD], ACT.Square,
                                         accum_out=o_ms[:, 8 * b + g:8 * b + g + 1])
                return last

            gate_copy(0)
            for b in range(NB):
                last = head_squares(b, 0)
            last.then_inc(s_asq, 1)
            sc.drain()
            for c in range(NCH):
                t = c // 2
                r = slice(CH * (c % 2), CH * (c % 2) + CH)
                act.wait_ge(s_qkv, c + 1)
                sc.copy(onat[r, t, 512:1024], bank[2 + c % 2][r, :]).then_inc(s_oc, 1)
                if c == 0:
                    gate_copy(1)
                if c % 2:
                    act.wait_ge(s_oc, c + 1)
                    head_squares(t, H).then_inc(s_osq, 1)
                if c == 1:
                    act.wait_ge(s_ams, 1)
                    sc.activation(heads(0), heads(0), ACT.Sqrt).then_inc(s_amr, 1)
                if c >= 2 and c % 2 == 0 or c == NCH - 1:
                    n = t if c == NCH - 1 else t - 1
                    act.wait_ge(s_oms, n + 1)
                    rows = o_ms[:, 8 * n + 4:8 * n + 8]
                    sc.activation(rows, rows, ACT.Sqrt).then_inc(s_omr, 1)
            for k in range(KD):
                if k in (4, 6):
                    hi(T_OUT + k // 2)
                act.wait_ge(s_oT, k + 1)
                g = hgain[:, k // 4:k // 4 + 1]
                sc.activation(act_hi[:, k, :], bank[6 + k % 2][:], ACT.Identity, scale=g).then_inc(s_ohi, 1)
            def y_squares(half):
                for b in range(NB):
                    last = sc.activation(osq[:, (2 * b + half) * 512:(2 * b + half + 1) * 512],
                                         bank[4 * half + b][:], ACT.Square,
                                         accum_out=ssq2[:, 2 * b + half:2 * b + half + 1])
                return last

            for n in range(T_OUT + 4, T_OUT + 6):
                hi(n)
            y_squares(0)
            for n in range(T_OUT + 6, T_QUERY):
                hi(n)
            act.wait_ge(s_used, T_QUERY)
            y_squares(1).then_inc(s_ssq, 1)
            sc.drain()
            act.wait_ge(s_msq, 2)
            sc.activation(rstd, rstd, ACT.Sqrt).then_inc(s_rt, 1)
            hi(T_QUERY)
            hi(T_QUERY + 1)
            def x1_square(b):
                act.wait_ge(s_x1[b], 1)
                sc.activation(osq[:, b * D:(b + 1) * D], xn[:, b, :], ACT.Square,
                              accum_out=ssq[:, b:b + 1]).then_inc(s_ssq, 1)

            def x1_sqrt(pair):
                act.wait_ge(s_msq, 3 + pair)
                r = rx[:, 2 * pair:2 * pair + 2]
                sc.activation(r, r, ACT.Sqrt).then_inc(s_rt, 1)

            def x1_scale(b):
                act.wait_ge(s_rx, b // 2 + 1)
                sc.mul(xs2[:, b, :], xn[:, b, :], rx[:, b:b + 1]).then_inc(s_xs, 1)

            x1_square(0)
            x1_square(1)
            x1_sqrt(0)
            x1_scale(0)
            x1_square(2)
            x1_square(3)
            x1_sqrt(1)
            x1_scale(2)
            shifted(1, hfl2)
            for n in range(16):
                act.wait_ge(s_used, T_QUERY + n + 1)
                if n >= 2:
                    act.wait_ge(s_qs, n - 1)
                sc.copy(qTs[:, n % 2, :], bank[n % 4][:]).then_inc(s_qT, 1)
                hi(T_QUERY + n + 2)


            def down_tiles(t0, count, b=None, first=0):
                def one(i, j, unguarded=False):
                    t = i * 4 + (t0 + j)
                    act.wait_ge(s_used, t + (T_DOWN + 1))
                    slot = (T_DOWN + 2 + j) % RAW
                    act.wait_ge(s_raw[slot], i * 16 + 16 * ((T_DOWN + 2 + t0 + j) // RAW + 1))
                    sc.copy(whi[:, j % SPLIT, :], raw[:, slot, :]).then_inc(s_hi, 1)
                    if j >= 2 or not unguarded:
                        act.wait_ge(s_ast[j % 2], i * 32 + 16 * ((t0 + j) // 2))
                    sc.activation(aout[:, j % 2, :], bank[j][:], ACT.Gelu).then_inc(s_act, 1)
                    if b is not None:
                        for r in range(2):
                            act.wait_ge(s_gp, i * 8 + (32 * b + 2 * j + r + 1))
                            for u2 in range(2):
                                k = r * TOK4 + 2 * u2
                                last = sc.copy(glo[:, k:k + 2, :],
                                               bank[4 + 2 * r + u2][:].rearrange(
                                                   "p (t c i) -> p t c i", t=2, c=2)[:, :, 1, :])
                            last.then_inc(s_glo, 1)
                if first:
                    for j in range(4):
                        one(0, j, True)
                with act.Fori(first, count // 4) as i:
                    for j in range(4):
                        one(i, j)

            def picked_exp(b):
                act.wait_ge(s_best, b + 1)
                sc.activation(pick[:, 2, :], best[:].rearrange("p h k -> p (h k)"),
                              ACT.Exp).then_inc(s_gexp, 1)

            down_tiles(0, LEAD - 4, first=1)
            picked_exp(0)
            down_tiles(LEAD - 4, 4)
            for b in range(NB):
                down_tiles(START[b], BUILD, b)
                if b < NB - 1:
                    down_tiles(START[b] + BUILD, REST[b] - 4)
                    picked_exp(b + 1)
                    down_tiles(START[b + 1] - 4, 4)
                else:
                    down_tiles(START[b] + BUILD, REST[b])

            def round_coef(t, j, reused):
                act.wait_ge(s_cf, t + 1)
                if reused:
                    act.wait_ge(s_used, t + (T_UP - 1))
                sc.copy(chi[:, j % 2, :], coef[:, j % 2, :]).then_inc(s_chi, 1)

            def up_tile(t, j, more):
                if more:
                    slot = (T_UP + 2 + j) % RAW
                    act.wait_ge(s_raw[slot], (t - j) * 4 + 16 * ((T_UP + 2 + j) // RAW + 1))
                    act.wait_ge(s_used, t + (T_UP + 1))
                    sc.copy(whi[:, j % SPLIT, :], raw[:, slot, :]).then_inc(s_hi, 1)

            round_coef(0, 0, False)
            round_coef(1, 1, False)
            up_tile(0, 0, True)
            for t in range(1, 4):
                round_coef(t + 1, t + 1, True)
                up_tile(t, t, True)
            with act.Fori(1, N_TILES // 4 - 1) as i:
                for j in range(4):
                    round_coef(i * 4 + (j + 1), j + 1, True)
                    up_tile(i * 4 + j, j, True)
            for t in range(N_TILES - 4, N_TILES):
                if t + 1 < N_TILES:
                    round_coef(t + 1, t + 1, True)
                up_tile(t, t % 4, t + 2 < N_TILES)
            act.wait_ge(s_used, T_ALL)
            for b in range(NB):
                for half in range(2):
                    last = sc.activation(yo[:, b, half * 512:(half + 1) * 512], bank[2 * b + half][:],
                                         ACT.Square, accum_out=ssq2[:, 2 * b + half:2 * b + half + 1])
            last.then_inc(s_yq, 1)
            act.wait_ge(s_ym, 1)
            sc.activation(rstd, rstd, ACT.Sqrt).then_inc(s_yr, 1)

        @block.tensor
        def _(pe):
            mm = nc.tensor.matmul

            def split_wait(n):
                pe.wait_ge(s_lo, n + 1)

            def column_tile(slot, out_bank, h_low=None):
                for k in range(KD):
                    if h_low is not None:
                        pe.wait_ge(s_hlo, h_low + k + 1)
                    w = slice(k * P, (k + 1) * P)
                    mm(out_bank[:], whi[:, slot, w], act_hi[:, k, :], start=(k == 0), stop=False)
                    mm(out_bank[:], whi[:, slot, w], act_lo[:, k, :], start=False, stop=False)
                    last = mm(out_bank[:], wlo[:, slot, w], act_hi[:, k, :], start=False,
                              stop=(k == KD - 1))
                last.then_inc(s_used, 1)

            def natural_tile(slot, q, banks):
                for b in range(NB):
                    for kk in range(2):
                        k = 2 * q + kk
                        w = slice(kk * 512, (kk + 1) * 512)
                        a = slice(b * P, (b + 1) * P)
                        mm(banks[b][:], act_hi[:, k, a], whi[:, slot, w], start=(k == 0), stop=False)
                        mm(banks[b][:], act_hi[:, k, a], wlo[:, slot, w], start=False, stop=False)
                        last = mm(banks[b][:], act_lo[:, k, a], whi[:, slot, w], start=False,
                                  stop=(k == KD - 1))
                last.then_inc(s_used, 1)

            pe.wait_ge(s_pool, 1)
            pe.wait_ge(s_xs, 1)

            def x_transposes(k):
                if k >= 2:
                    pe.wait_ge(s_hf, k - 1)
                for b in range(NB):
                    last = nc.tensor.transpose(bank[6 + k % 2][:, b * P:(b + 1) * P],
                                               xn[:, b, k * P:(k + 1) * P], ident[:])
                last.then_inc(s_xT, 1)

            for k in range(4):
                x_transposes(k)
            for n in range(T_VA, T_KQ):
                split_wait(n)
                if n < T_Z:
                    pe.wait_ge(s_hlo, 2 * n + 2)
                natural_tile(n % SPLIT, n % 4, bank[0:4] if n < T_Z else bank[4:8])
                if n < 2:
                    x_transposes(2 * n + 4)
                    x_transposes(2 * n + 5)
            pe.wait_ge(s_nat, NB)
            pe.wait_ge(s_bas, 2)
            for k in range(KD):
                mm(bank[2][0:8, :], baw_hi[:, k, :], act_hi[:, k, :], start=(k == 0), stop=False)
                mm(bank[2][0:8, :], baw_hi[:, k, :], act_lo[:, k, :], start=False, stop=False)
                last = mm(bank[2][0:8, :], baw_lo[:, k, :], act_hi[:, k, :], start=False,
                          stop=(k == KD - 1))
            last.then_inc(s_baT, 1)
            for n in range(T_KQ, SLOT0):
                split_wait(n)
                column_tile(n % SPLIT, bank[n % 2])
            pe.wait_ge(s_bac, 1)
            for b in range(NB):
                last = nc.tensor.transpose(bank[3][:, b * 8:b * 8 + 8], baT[:, b * P:(b + 1) * P],
                                           ident[0:8, 0:8])
            last.then_inc(s_ba, 1)

            def scores(i):
                h, b = divmod(i, NB)
                if i == 0:
                    pe.wait_ge(s_g1, 1)
                if i == 1:
                    pe.wait_ge(s_nat, 2 * NB)
                if b == 0:
                    pe.wait_ge(s_kq, 2 * h + 2)
                if i >= 2:
                    pe.wait_ge(s_mx, i - 1)
                for m in range(2):
                    r = slice(m * QK, (m + 1) * QK)
                    last = mm(bank[2 + 2 * (i % 2) + m][:, 0:(b + 1) * P], qaT[r, h, b * P:(b + 1) * P],
                              kaT[r, h, 0:(b + 1) * P], start=True, stop=True)
                last.then_inc(s_sc, 1)

            def transposes(i):
                pe.wait_ge(s_pd, i + 1)
                if i >= 1:
                    pe.wait_ge(s_ptc, i)
                for j in range(i % NB + 1):
                    last = nc.tensor.transpose(bank[6][:, j * P:(j + 1) * P],
                                               pr[:, i % 2, 0, j * P:(j + 1) * P], ident[:])
                last.then_inc(s_pt, 1)

            def values(i):
                h, b = divmod(i, NB)
                pe.wait_ge(s_ptc, i + 1)
                if i >= 1:
                    pe.wait_ge(s_oa, i)
                for j in range(b + 1):
                    last = mm(bank[7][:, 0:HD], pT[:, i % 2, j * P:(j + 1) * P],
                              va[:, j, h * HD:(h + 1) * HD], start=(j == 0), stop=(j == b))
                last.then_inc(s_av, 1)

            def norm_sums(n):
                pe.wait_ge(s_sq, n + 1)
                if n < 4:
                    pe.wait_ge(s_mx, 15 + n // 2)
                elif n == 4:
                    pe.wait_ge(s_ptc, H * NB)
                else:
                    pe.wait_ge(s_l2r, n - 2)
                mm(bank[SUM_BANK[n]][:], ones[:], l2r[:, n, :], start=True, stop=True).then_inc(s_l2, 1)

            for s in range(T_OUT - SLOT0):
                n = SLOT0 + s
                split_wait(n)
                if n - 2 < T_GDN:
                    pe.wait_ge(s_kq, n - 2 - T_KQ + 1)
                else:
                    pe.wait_ge(s_conv, n - 2 - T_GDN + 1)
                column_tile(n % SPLIT, bank[n % 2])
                if s < H * NB:
                    scores(s)
                if 1 <= s <= H * NB:
                    transposes(s - 1)
                if 2 <= s <= H * NB + 1:
                    values(s - 2)
                if s == H * NB + 1:
                    for n2 in range(4):
                        norm_sums(n2)

            def blk(t):
                return slice(t * P, (t + 1) * P)

            def hs(h):
                return slice(h * HD, (h + 1) * HD)

            norm_sums(4)
            pe.wait_ge(s_oa, H * NB)
            pe.wait_ge(s_gB, 1)
            mm(bank[7][:, 0:16], masks[:, M_U, :], g16(G_LOG), start=True, stop=True).then_inc(s_gc, 1)
            for t in range(NB):
                if t == 0:
                    pe.wait_ge(s_conv, 11)
                elif t < 3:
                    pe.wait_ge(s_l2r, t)
                else:
                    pe.wait_ge(s_conv, 12)
                for h in range(H):
                    last = mm(bank[ROW_BANK[t]][:, hs(h)], gB[:, 4 * t + h, :], masks[:, M_U, :],
                              start=True, stop=True)
                last.then_inc(s_row, 1)
                for n in {0: (5, 6), 1: (7,)}.get(t, ()):
                    norm_sums(n)
            pe.wait_ge(s_l2n, 8)
            pe.wait_ge(s_gcc, 1)
            for t in range(NB):
                if t >= 2:
                    pe.wait_ge(s_L, t - 1)
                for h in range(H):
                    mm(bank[4 + t % 2][:, hs(h)], qkvT[:, 4 + h, blk(t)], qkvT[:, 4 + h, blk(t)],
                       start=True, stop=True)
                for h in range(H):
                    last = mm(bank[6 + t % 2][:, hs(h)], qkvT[:, 4 + h, blk(t)], qkvT[:, h, blk(t)],
                              start=True, stop=True)
                last.then_inc(s_kg, 1)
            for t in range(NB):
                if t == 0:
                    pe.wait_ge(s_L, NB)
                if t >= 2:
                    pe.wait_ge(s_LTc, t - 1)
                for h in range(H):
                    last = nc.tensor.transpose(bank[4 + t % 2][:, hs(h)], LM[:, t, hs(h)], ident[:])
                last.then_inc(s_LT, 1)
            def vk_transposes(t):
                if t == 0:
                    pe.wait_ge(s_silu, 3)
                if t >= 1:
                    pe.wait_ge(s_vtd, t)
                for h in range(H):
                    nc.tensor.transpose(bank[6][:, hs(h)], qkvT[:, 8 + h, blk(t)], ident[:])
                for h in range(H):
                    last = nc.tensor.transpose(bank[7][:, hs(h)], qkvT[:, 4 + h, blk(t)], ident[:])
                last.then_inc(s_vt, 1)

            def level_p(n):
                t = n % NB
                if n == 0:
                    pe.wait_ge(s_de, NB + 1)
                pe.wait_ge(s_lm, n + 1)
                pe.wait_ge(s_td, n + 1)
                if n >= 2:
                    pe.wait_ge(s_pc, n - 1)
                for h in range(H):
                    last = mm(bank[t % 2][:, hs(h)], LM[:, t, hs(h)], Tm[:, t, hs(h)], start=True, stop=True)
                last.then_inc(s_pp, 1)

            def level_t(n):
                k, t = divmod(n, NB)
                pe.wait_ge(s_pc, n + 1)
                if n >= 2:
                    pe.wait_ge(s_td, NB + n - 1)
                if n == 0:
                    pe.wait_ge(s_LTc, NB)
                for h in range(H):
                    if k < 4:
                        mm(bank[2 + t % 2][:, hs(h)], TT[:, t, hs(h)], PM[:, t, hs(h)], start=True, stop=True)
                for h in range(H):
                    last = mm(bank[4 + t % 2][:, hs(h)], PM[:, t, hs(h)], TT[:, t, hs(h)], start=True, stop=True)
                last.then_inc(s_tt, 1)

            for n in range(5 * NB + 1):
                if n < 5 * NB:
                    level_p(n)
                if n >= 1:
                    level_t(n - 1)
                if n in VK_STEPS:
                    vk_transposes(VK_STEPS.index(n))
            for t in range(NB):
                pe.wait_ge(s_td, 5 * NB + t + 1)
                if t == 0:
                    pe.wait_ge(s_td, 6 * NB)
                    pe.wait_ge(s_vtd, NB)
                if t >= 2:
                    pe.wait_ge(s_uwc, t - 1)
                for h in range(H):
                    mm(bank[2 * (t % 2)][:, hs(h)], TT[:, t, hs(h)], vbeta[:, t, hs(h)], start=True, stop=True)
                for h in range(H):
                    last = mm(bank[2 * (t % 2) + 1][:, hs(h)], kbeg[:, t, hs(h)], TT[:, t, hs(h)],
                              start=True, stop=True)
                last.then_inc(s_uw, 1)
            def gate_row(g):
                for k in range(KD):
                    last = mm(bank[6 + k // 4][:, blk(k % 4)],
                              gcol[:, g, k:k + 1].to_broadcast([P, P]), ident[:], start=True, stop=True)
                last.then_inc(s_gsp, 1)

            pe.wait_ge(s_gcol, 1)
            gate_row(0)
            pe.wait_ge(s_uwc, NB)
            for c in range(NCH):
                t = c // 2
                r = slice(CH * (c % 2), CH * (c % 2) + CH)
                tok = slice(c * CH, (c + 1) * CH)
                pe.wait_ge(s_st, c + 1)
                for h in range(H):
                    off = h * HD + CH * (c % 2)
                    last = mm(bank[0][r, hs(h)], wT[:, t, off:off + CH], state[:, hs(h)], start=True, stop=True)
                last.then_inc(s_wS, 1)
                if c == 0:
                    pe.wait_ge(s_qg, 1)
                if c >= 2:
                    pe.wait_ge(s_oc, c - 1)
                for h in range(H):
                    mm(bank[2 + c % 2][r, hs(h)], qkvT[:, h, tok], state[:, hs(h)], start=(h == 0),
                       stop=False, skip_group_check=True)
                pe.wait_ge(s_vn, c + 1)
                if c < NCH - 1:
                    for h in range(H):
                        last = mm(bank[1][:, hs(h)], kdec[r, t, hs(h)], vnew[r, hs(h)], start=True, stop=True)
                    last.then_inc(s_kv, 1)
                for h in range(H):
                    off = h * HD + CH * (c % 2)
                    last = mm(bank[2 + c % 2][r, hs(h)], QKT[r, t, off:off + CH], vnew[r, hs(h)],
                              start=False, stop=True, skip_group_check=True)
                last.then_inc(s_qkv, 1)
                if c == 0:
                    pe.wait_ge(s_gate, 1)
                    gate_row(1)
            pe.wait_ge(s_gate, 2)
            def head_transposes(k):
                if k == 0:
                    pe.wait_ge(s_ona, NB)
                if k == 4:
                    pe.wait_ge(s_on, NB)
                if k >= 2:
                    pe.wait_ge(s_olo, k - 1)
                for b in range(NB):
                    last = nc.tensor.transpose(bank[6 + k % 2][:, blk(b)], onat[:, b, blk(k)], ident[:])
                last.then_inc(s_oT, 1)

            def out_tile(n):
                split_wait(n)
                pe.wait_ge(s_olo, KD if n >= T_OUT + 4 else 2 * (n - T_OUT) + 2)
                natural_tile(n % SPLIT, n % 4, bank[0:4] if n < T_OUT + 4 else bank[4:8])

            for k in range(4):
                head_transposes(k)
            for n in range(T_OUT, T_OUT + 2):
                out_tile(n)
                for k in range(2 * (n - T_OUT) + 4, 2 * (n - T_OUT) + 6):
                    head_transposes(k)
            for n in range(T_OUT + 2, T_QUERY):
                out_tile(n)
            pe.wait_ge(s_xs, 1 + NB // 2)
            pe.wait_ge(s_xs1, NB // 2)
            for k in range(KD):
                if k >= 2:
                    pe.wait_ge(s_hf, KD + k - 1)
                for b in range(NB):
                    last = nc.tensor.transpose(bank[6 + k % 2][:, blk(b)], xs2[:, b, blk(k)], ident[:])
                last.then_inc(s_xT, 1)

            def key_scores(n):
                pe.wait_ge(s_qT, n + 1)
                if n == 0:
                    pe.wait_ge(s_key, 16)
                if n >= 2:
                    pe.wait_ge(s_S, n - 1)
                for b in range(NB):
                    last = mm(bank[4 + n % 2][:, blk(b)], qTs[:, n % 2, blk(b)], keys[:, n, :],
                              start=True, stop=True)
                last.then_inc(s_qs, 1)

            for n in range(17):
                if n < 16:
                    split_wait(T_QUERY + n)
                    if n >= 4:
                        pe.wait_ge(s_qT, n - 3)
                    column_tile(n % SPLIT, bank[n % 4], KD if n == 0 else None)
                if n >= 1:
                    key_scores(n - 1)

            pe.wait_ge(s_qT, 16)
            pe.wait_ge(s_S, 16)

            def gate_group(q, slot):
                pe.wait_ge(s_ohl, q + 1)
                pe.wait_ge(s_gev, q + 1)
                for tk in range(TOK4):
                    o = bank[4 + 2 * (slot % 2) + tk // 2][:, (tk % 2) * 2 * P:(tk % 2 + 1) * 2 * P]
                    last = mm(o, ohJ[:, slot % OH, tk * P:(tk + 1) * P], ohI[:, slot % OH * TOK4 + tk, :, :],
                              start=True, stop=True)
                last.then_inc(s_gp, 1)

            def down_tiles(t0, count, b=None, first=0):
                def one(i, j, free):
                    t = i * 4 + (t0 + j)
                    pe.wait_ge(s_lo, t + (T_DOWN + 1))
                    if free:
                        pe.wait_ge(s_act, t - 3)
                    column_tile(j % SPLIT, bank[j])
                    if b is not None:
                        for r in range(2):
                            gate_group(i * 8 + (32 * b + 2 * j + r), 2 * j + r)
                if first:
                    for j in range(4):
                        one(0, j, False)
                with pe.Fori(first, count // 4) as i:
                    for j in range(4):
                        one(i, j, True)

            down_tiles(0, LEAD, first=1)
            for b in range(NB):
                pe.wait_ge(s_pick, b + 1)
                pe.wait_ge(s_gev, RING + 32 * b)
                for v in range(3):
                    last = nc.tensor.transpose(bank[7][:, v * P:(v + 1) * P], pick[:, v, :], ident[:])
                last.then_inc(s_pkT, 1)
                down_tiles(START[b], BUILD, b)
                down_tiles(START[b] + BUILD, REST[b])

            def up_tile(t, j, start, stop):
                pe.wait_ge(s_lo, t + (T_UP + 1))
                pe.wait_ge(s_clo, t + 1)
                for b in range(NB):
                    a = blk(b)
                    for half in range(2):
                        w = slice(half * 512, (half + 1) * 512)
                        o = bank[2 * b + half][:]
                        mm(o, chi[:, j % 2, a], whi[:, j % SPLIT, w], start=start, stop=False,
                           skip_group_check=True)
                        mm(o, chi[:, j % 2, a], wlo[:, j % SPLIT, w], start=False, stop=False,
                           skip_group_check=True)
                        last = mm(o, clo[:, j % 2, a], whi[:, j % SPLIT, w], start=False, stop=stop,
                                  skip_group_check=True)
                last.then_inc(s_used, 1)

            pe.wait_ge(s_act, N_TILES)
            pe.wait_ge(s_gev, RING + 32 * NB)
            for t in range(4):
                up_tile(t, t, t == 0, False)
            with pe.Fori(1, N_TILES // 4 - 1) as i:
                for j in range(4):
                    up_tile(i * 4 + j, j, False, False)
            for t in range(N_TILES - 4, N_TILES):
                up_tile(t, t % 4, False, t == N_TILES - 1)

        @block.vector
        def _(dve):
            v = nc.vector
            tt, ts, stt = v.tensor_tensor, v.tensor_scalar, v.scalar_tensor_tensor

            def bc(ap16, t):
                return ap16[:, 4 * t:4 * t + 4].unsqueeze(2).to_broadcast([P, H, P])

            dve.wait_ge(s_pool, 1)
            ge = wk[:, 0, 0:P]
            lt = wk[:, 0, P:2 * P]
            same = wk[:, 0, 2 * P:3 * P]
            xo = wk[:, 1, 0:P].bitcast(I32)
            xk = wk[:, 2:4, :].rearrange("p a n -> p (a n)").bitcast(I32)
            tt(ge, xij[:, 0, :], xij[:, 1, :], ALU.is_ge)
            tt(lt, xij[:, 0, :], xij[:, 1, :], ALU.is_lt)
            tt(masks[:, M_STRICT, :], xij[:, 0, :], xij[:, 1, :], ALU.is_gt)
            tt(xo, xij[:, 0, :], xij[:, 1, :], ALU.bitwise_xor)
            v.drain()
            ts(same, xo, CH, None, ALU.is_lt)
            v.drain()
            tt(masks[:, M_INCL, :], ge, same, ALU.mult)
            tt(masks[:, M_U, :], lt, same, ALU.mult)
            tt(masks[:, M_STRICT, :], masks[:, M_STRICT, :], same, ALU.mult)
            v.drain()
            tt(masks[:, M_U, :], masks[:, M_U, :], ident[:], ALU.add)
            for k in range(6):
                ts(xk[:, k * P:(k + 1) * P], xo, k, None, ALU.logical_shift_right)
            v.drain()
            ts(masks[:, M_FIRST, :], xk[:, 0:P], 1, None, ALU.is_equal)
            ts(masks[:, MT:MT + 6, :], xk[:, 0:6 * P].rearrange("p (k n) -> p k n", k=6), 1, None,
               ALU.is_equal)
            v.drain()
            tt(masks[:, MT:MT + 6, :], masks[:, MT:MT + 6, :],
               lt.unsqueeze(1).to_broadcast([P, 6, P]), ALU.mult)
            tt(masks[:, M_FIRST, :], masks[:, M_FIRST, :], masks[:, M_STRICT, :], ALU.mult)
            v.drain()
            ts(negm[:], rel[:], 0.0, NEG, ALU.is_lt, ALU.mult).then_inc(s_xij, 1)
            def inverse_root(wait_root):
                dve.wait_ge(s_rt, wait_root)
                v.reciprocal(rstd, rstd)
                v.drain()


            def mod_tile(m):
                if m == 0:
                    dve.wait_ge(s_cc, 1)
                part, k = mod_order(m)
                if m < 16:
                    t = modr[:, m % 8, :]
                    dve.wait_ge(s_mod8[m % 8], 16 * (m // 8 + 1))
                else:
                    t = modx[:, m % 4, :]
                    dve.wait_ge(s_modl[m % 4], 16 * (m // 4 - 3))
                v.tensor_tensor_reduce(out=t, in0=t, in1=c_row[:], scale=1.0, scalar=0.0, op0=ALU.mult,
                                       op1=ALU.add, accum_out=modcol[:, part, k:k + 1]).then_inc(s_modu, 1)

            def mod_columns(half, k0, k1):
                v.drain()
                w = slice(k0, k1)
                tt(bcol[:, half, w], modcol[:, 3 * half, w], modbcol[:, 3 * half, w], ALU.add)
                tt(acol[:, half, w], modcol[:, 3 * half + 1, w], modbcol[:, 3 * half + 1, w], ALU.add)
                v.drain()
                stt(out=acol[:, half, w], in0=acol[:, half, w], scalar=1.0, in1=gaincol[:, half, w],
                    op0=ALU.add, op1=ALU.mult).then_inc(s_cols, 1)

            def gate_columns():
                v.drain()
                gates = modcol[:].rearrange("p (a c) k -> p a c k", a=2)[:, :, 2, :]
                biases = modbcol[:].rearrange("p (a c) k -> p a c k", a=2)[:, :, 2, :]
                tt(gcol[:], gates, biases, ALU.add)
                v.drain()
                tt(gcol[:], gcol[:], gaincol[:, 2:4, :], ALU.mult).then_inc(s_gcol, 1)

            def low(half, k, buf):
                dve.wait_ge(s_hhi, KD * half + k + 1)
                tt(act_lo[:, k, :], buf[:, k % 4, :], act_hi[:, k, :].bitcast(F32),
                   ALU.subtract).then_inc(s_hlo, 1)

            dve.wait_ge(s_c, 16 * 3)
            for r in range(4):
                for m in range(4 * r, 4 * r + 4):
                    mod_tile(m)
                    if m == 1:
                        dve.wait_ge(s_ssq, NB)
                        ts(rstd, ssq, 1.0 / D, EPS, ALU.mult, ALU.add).then_inc(s_msq, 1)
                    if m == 2:
                        dve.wait_ge(s_rt, 1)
                        v.reciprocal(rstd, rstd).then_inc(s_rst, 1)
                mod_columns(0, 2 * r, 2 * r + 2)
                if r >= 1:
                    low(0, 2 * r - 2, wk)
                    low(0, 2 * r - 1, wk)
            low(0, KD - 2, wk)
            low(0, KD - 1, wk)
            dve.wait_ge(s_bas, 1)
            tt(baw_lo[:], baw[:], baw_hi[:].bitcast(F32), ALU.subtract).then_inc(s_bas, 1)
            for m in range(16, 28):
                mod_tile(m)

            def conv(n):
                dve.wait_ge(s_used, T_GDN + n + 1)
                o = qkvT[:, n, :]
                ps = bank[n % 2]
                ts(o, ps[:], conv_w[:, n, 3:4], None, ALU.mult)
                for j in (2, 1, 0):
                    s = 3 - j
                    v.drain()
                    last = stt(out=o[:, s:], in0=ps[:, 0:SEQ - s], scalar=conv_w[:, n, j:j + 1],
                               in1=o[:, s:], op0=ALU.mult, op1=ALU.add)
                last.then_inc(s_conv, 1)

            dve.wait_ge(s_hc, 16 * 5)
            l64 = lam_in.rearrange("p (a n) -> p a n", a=4)
            for m in range(2):
                tt(l64[:, m, :], l64[:, m, :], l64[:, 2 + m, :], ALU.mult)
            v.drain()
            v.tensor_reduce(lam[:, 0:2], l64[:, 0:2, :], AX_X, ALU.add).then_inc(s_lam, 1)
            ts(hgain[:, 0:1], hgain[:, 0:1], 1.0 - LAMBDA_INIT, None, ALU.mult)
            dve.wait_ge(s_baT, 1)
            v.tensor_copy(baT[:], bank[2][0:8, :]).then_inc(s_bac, 1)
            for m in range(28, 36):
                mod_tile(m)
            dve.wait_ge(s_lame, 1)
            tt(lam[:, 2:3], lam[:, 0:1], lam[:, 1:2], ALU.subtract)
            v.drain()
            ts(lam[:, 2:3], lam[:, 2:3], LAMBDA_INIT, -1.0, ALU.add, ALU.mult)

            dve.wait_ge(s_ba, 1)
            ba = bank[3][:, 0:32].rearrange("p (t c) -> p t c", t=NB)
            def th(ap):
                return ap.rearrange("p (t h) -> p t h", t=NB)
            v.tensor_copy(th(g16(G_BETA)), ba[:, :, 0:4])
            tt(th(g16(G_Y)), ba[:, :, 4:8], dt4.unsqueeze(1).to_broadcast([P, NB, H]), ALU.add)
            v.drain()
            stt(out=g16(G_AY), in0=g16(G_Y), scalar=-1.0, in1=g16(G_Y), op0=ALU.mult,
                op1=ALU.max).then_inc(s_g1, 1)
            dve.wait_ge(s_g1e, 1)
            ts(g16(G_BETA), g16(G_BETA), 1.0, None, ALU.add)
            stt(out=g16(G_SP), in0=g16(G_Y), scalar=0.0, in1=g16(G_SP), op0=ALU.max, op1=ALU.add)
            v.drain()
            v.reciprocal(g16(G_BETA), g16(G_BETA))
            stt(out=th(g16(G_LOG)), in0=th(g16(G_SP)), scalar=-1.0,
                in1=alog4.unsqueeze(1).to_broadcast([P, NB, H]), op0=ALU.mult, op1=ALU.mult)

            def biased(i):
                h, b = divmod(i, NB)
                n = (b + 1) * P
                if b == 0:
                    stt(out=bias[:, h % 2, :], in0=rel[:], scalar=-(2.0 ** (-8.0 * (h + 1) / H)),
                        in1=negm[:], op0=ALU.mult, op1=ALU.add)
                    v.drain()
                dve.wait_ge(s_sc, i + 1)
                if i >= 2:
                    dve.wait_ge(s_pt, i - 1)
                for m in range(2):
                    v.tensor_tensor_reduce(out=pr[:, i % 2, m, 0:n], in0=bank[2 + 2 * (i % 2) + m][:, 0:n],
                                           in1=bias[:, h % 2, 512 - n:512], scale=1.0, scalar=-3e38,
                                           op0=ALU.add, op1=ALU.max, accum_out=asm[:, i % 2, m:m + 1])
                v.drain()
                ts(asm[:, i % 2, 2:4], asm[:, i % 2, 0:2], -1.0, None, ALU.mult).then_inc(s_mx, 1)

            def difference(i):
                n = (i % NB + 1) * P
                dve.wait_ge(s_ex, i + 1)
                a = asm[:, i % 2, 4:6]
                v.reciprocal(a, a)
                v.drain()
                tt(a[:, 1:2], a[:, 1:2], lam[:, 2:3], ALU.mult)
                ts(pr[:, i % 2, 0, 0:n], pr[:, i % 2, 0, 0:n], a[:, 0:1], None, ALU.mult)
                v.drain()
                stt(out=pr[:, i % 2, 0, 0:n], in0=pr[:, i % 2, 1, 0:n], scalar=a[:, 1:2],
                    in1=pr[:, i % 2, 0, 0:n], op0=ALU.mult, op1=ALU.add).then_inc(s_pd, 1)

            def attn_out(i):
                h, b = divmod(i, NB)
                dve.wait_ge(s_av, i + 1)
                v.tensor_copy(onat[:, b, h * HD:(h + 1) * HD],
                              bank[7][:, 0:HD]).then_inc(s_oa, 1)

            v.drain()
            def decay_spread():
                v.tensor_copy(gB[:], g16(G_LOG).unsqueeze(2).to_broadcast([P, 16, P])).then_inc(s_gB, 1)

            for s in range(T_OUT - SLOT0):
                if 3 <= s <= H * NB + 1:
                    attn_out(s - 3)
                if s < H * NB:
                    biased(s)
                if SLOT0 + s == T_OUT - 1:
                    dve.wait_ge(s_used, T_OUT)
                    decay_spread()
                    attn_out(s - 2)
                if T_GDN <= SLOT0 + s < T_OUT:
                    conv(SLOT0 + s - T_GDN)
                if s < H * NB:
                    difference(s)
                for m in range(2 * s + 36, min(2 * s + 38, N_MOD)):
                    mod_tile(m)
                if s == 6:
                    mod_columns(1, 0, KD)
                    gate_columns()

            dve.wait_ge(s_gc, 1)
            v.tensor_copy(g16(G_CUM), bank[7][:, 0:16]).then_inc(s_gcc, 1)
            v.memset(state[:], 0.0).then_inc(s_st, 1)
            v.drain()
            def masked_args(t):
                v.drain()
                tt(by_head(LM[:, t, :]), by_head(QKT[:, t, :]), mask4(M_INCL), ALU.mult)
                v.drain()
                tt(by_head(QKT[:, t, :]), by_head(QKT[:, t, :]), mask4(M_U), ALU.mult).then_inc(s_du[1], 1)

            for t in range(NB):
                dve.wait_ge(s_row, t + 1)
                row = by_head(bank[ROW_BANK[t]][:])
                for s in range(2):
                    r = slice(CH * s, CH * (s + 1))
                    tt(g16(G_DEC)[r, 4 * t:4 * t + 4], row[r, :, CH * s + CH - 1],
                       g16(G_CUM)[r, 4 * t:4 * t + 4], ALU.subtract)
                    c = 2 * t + s
                    v.tensor_copy(g_last[:, 4 * c:4 * c + 4], row[:, :, CH * s + CH - 1])
                tt(by_head(QKT[:, t, :]), row, bc(g16(G_CUM), t), ALU.subtract).then_inc(s_arg, 1)
                if t == 1:
                    masked_args(1)
            for n in range(8):
                dve.wait_ge(s_l2e, n + 1)
                stt(out=qkvT[:, n, :], in0=qkvT[:, n, :], scalar=HD ** -0.5 if n < 4 else 1.0,
                    in1=l2r[:, n, :], op0=ALU.mult, op1=ALU.mult).then_inc(s_l2n, 1)
                if n == 3:
                    masked_args(3)
            for t in range(NB):
                dve.wait_ge(s_kg, t + 1)
                dve.wait_ge(s_mk, 2 * t + 2)
                tt(LM[:, t, :], LM[:, t, :], bank[4 + t % 2][:], ALU.mult)
                tt(QKT[:, t, :], QKT[:, t, :], bank[6 + t % 2][:], ALU.mult)
                v.drain()
                tt(by_head(LM[:, t, :]), by_head(LM[:, t, :]), bc(g16(G_BETA), t),
                   ALU.mult).then_inc(s_L, 1)
            tt(g16(G_BEXP), g16(G_BETA), g16(G_EXP), ALU.mult)
            v.drain()
            def masked(n):
                k, t = divmod(n, NB)
                if k >= 1:
                    dve.wait_ge(s_pp, n - NB + 1)
                tt(by_head(LM[:, t, :]), by_head(LT[:, t, :]), mask4(MT + 1 + k), ALU.mult).then_inc(s_lm, 1)

            for t in range(NB):
                dve.wait_ge(s_LTc, t + 1)
                tt(by_head(TT[:, t, :]), by_head(LT[:, t, :]), mask4(MT), ALU.mult)
                v.drain()
                tt(by_head(TT[:, t, :]), ident[:].unsqueeze(1).to_broadcast([P, H, P]),
                   by_head(TT[:, t, :]), ALU.subtract).then_inc(s_td, 1)
                dve.wait_ge(s_t0, t + 1)
                masked(t)
            def scaled_vk(t):
                dve.wait_ge(s_vt, t + 1)
                tt(by_head(vbeta[:, t, :]), by_head(bank[6][:]), bc(g16(G_BETA), t), ALU.mult)
                tt(by_head(kbeg[:, t, :]), by_head(bank[7][:]), bc(g16(G_BEXP), t), ALU.mult)
                tt(by_head(kdec[:, t, :]), by_head(bank[7][:]), bc(g16(G_DEC), t),
                   ALU.mult).then_inc(s_vtd, 1)

            def updated(n):
                k, t = divmod(n, NB)
                dve.wait_ge(s_tt, n + 1)
                if k < 4:
                    tt(Tm[:, t, :], Tm[:, t, :], bank[2 + t % 2][:], ALU.subtract)
                tt(TT[:, t, :], TT[:, t, :], bank[4 + t % 2][:], ALU.subtract).then_inc(s_td, 1)

            for n in range(5 * NB):
                updated(n)
                if n in VK_STEPS:
                    scaled_vk(VK_STEPS.index(n))
                if n + NB < 5 * NB:
                    v.drain()
                    masked(n + NB)

            def mean_squares(t):
                dve.wait_ge(s_osq, t + 1)
                rows = o_ms[:, 8 * t + 4:8 * t + 8]
                ts(rows, rows, 1.0 / HD, EPS, ALU.mult, ALU.add).then_inc(s_oms, 1)

            def gated_heads(t):
                dve.wait_ge(s_osq, t + 1)
                o = onat[:, t, 512:1024]
                tt(o, o, zs[:, t, :], ALU.mult)

            def normed_heads(t):
                dve.wait_ge(s_omr, t + 1)
                rows = o_ms[:, 8 * t + 4:8 * t + 8]
                o = onat[:, t, 512:1024]
                v.reciprocal(rows, rows)
                v.drain()
                tt(by_head(o), by_head(o), rows.unsqueeze(2).to_broadcast([P, H, P]),
                   ALU.mult).then_inc(s_on, 1)

            dve.wait_ge(s_uwc, NB)
            for c in range(NCH):
                t = c // 2
                r = slice(CH * (c % 2), CH * (c % 2) + CH)
                dve.wait_ge(s_wS, c + 1)
                tt(vnew[r, :], u[r, t, :], bank[0][r, :], ALU.subtract).then_inc(s_vn, 1)
                if c == 1:
                    dve.wait_ge(s_asq, 1)
                    ts(heads(0), heads(0), 1.0 / HD, EPS, ALU.mult, ALU.add).then_inc(s_ams, 1)
                if c == 2:
                    dve.wait_ge(s_amr, 1)
                    v.reciprocal(heads(0), heads(0)).then_inc(s_amd, 1)
                if c >= 2 and c % 2 == 0:
                    mean_squares(t - 1)
                if c < NCH - 1:
                    dve.wait_ge(s_car, c + 1)
                    dve.wait_ge(s_kv, c + 1)
                    tt(state[:], carried, bank[1][:], ALU.add).then_inc(s_st, 1)
                if c >= 2 and c % 2 == 0:
                    gated_heads(t - 1)
                if c >= 3 and c % 2 == 1:
                    normed_heads(t - 1)
            mean_squares(NB - 1)
            gated_heads(NB - 1)
            normed_heads(NB - 1)
            for k in range(KD):
                dve.wait_ge(s_ohi, k + 1)
                stt(out=act_lo[:, k, :], in0=bank[6 + k % 2][:], scalar=hgain[:, k // 4:k // 4 + 1],
                    in1=act_hi[:, k, :].bitcast(F32), op0=ALU.mult, op1=ALU.subtract).then_inc(s_olo, 1)
            dve.wait_ge(s_ssq, NB + 1)
            v.tensor_reduce(rstd, ssq2.rearrange("p (b a) -> p b a", a=2), AX_X, ALU.add)
            v.drain()
            ts(rstd, rstd, 1.0 / D, EPS, ALU.mult, ALU.add).then_inc(s_msq, 1)
            inverse_root(2)
            dve.wait_ge(s_xr, 16 * NB)
            def y_gated(b):
                for half in range(2):
                    w = slice(half * 512, (half + 1) * 512)
                    last = stt(out=xs2[:, b, w], in0=bank[4 * half + b][:], scalar=rstd[:, b:b + 1],
                               in1=gate_m[:, w], op0=ALU.mult, op1=ALU.mult)
                if b % 2 == 0:
                    last.then_inc(s_yg, 1)

            def x1_added(b):
                v.drain()
                tt(xn[:, b, :], xn[:, b, :], xs2[:, b, :], ALU.add).then_inc(s_x1[b], 1)

            def x1_mean(pair):
                dve.wait_ge(s_ssq, NB + 3 + 2 * pair)
                w = slice(2 * pair, 2 * pair + 2)
                ts(rx[:, w], ssq[:, w], 1.0 / D, EPS, ALU.mult, ALU.add).then_inc(s_msq, 1)

            def x1_root(pair):
                dve.wait_ge(s_rt, 3 + pair)
                w = slice(2 * pair, 2 * pair + 2)
                v.reciprocal(rx[:, w], rx[:, w]).then_inc(s_rx, 1)

            def x1_scaled(b):
                ts(xs2[:, b, :], xn[:, b, :], rx[:, b:b + 1], None, ALU.mult).then_inc(s_xs1, 1)

            y_gated(0)
            y_gated(1)
            x1_added(1)
            y_gated(2)
            x1_mean(0)
            y_gated(3)
            x1_root(0)
            x1_added(3)
            v.drain()
            x1_scaled(1)
            x1_mean(1)
            x1_root(1)
            v.drain()
            x1_scaled(3)
            v.drain()
            for k in range(KD):
                low(1, k, hfl2)
            dve.wait_ge(s_x1o, 16 * NB)
            for n in range(16):
                dve.wait_ge(s_qs, n + 1)
                v.tensor_copy(S[:, :, n, :], bank[4 + n % 2][:].rearrange("p (b n) -> p b n", b=NB)
                              ).then_inc(s_S, 1)

            def top16(lists):
                for vals, _, src in lists:
                    v.max(vals[:, 0:8], src)
                v.drain()
                for vals, idx, src in lists:
                    v.max_index(idx[:, 0:8], vals[:, 0:8], src)
                v.drain()
                for vals, _, src in lists:
                    v.match_replace(out=src, in_to_replace=vals[:, 0:8], in_values=src, imm_value=LOWEST)
                v.drain()
                for vals, _, src in lists:
                    v.max(vals[:, 8:16], src)
                v.drain()
                for vals, idx, src in lists:
                    v.max_index(idx[:, 8:16], vals[:, 8:16], src)

            def staged(q0, tok):
                dve.wait_ge(s_glo, q0 + 2)
                for s in range(2):
                    for u2 in range(2):
                        ps = bank[4 + 2 * s + u2][:].rearrange("p (t c i) -> p t c i", t=2, c=2)
                        first = tok + (s * TOK4 + u2 * 2)
                        last = tt(stage[:, :, bass.ds(first, 2)].rearrange("p i t -> p t i"),
                                  ps[:, :, 0, :],
                                  glo[:, s * TOK4 + 2 * u2:s * TOK4 + 2 * u2 + 2, :], ALU.add)
                    last.then_inc(s_gev, 1)

            def retrieve(b):
                lists = [(top[:, n, :], topi[:, n, :], S[:, b, n, :]) for n in range(2 * PH)]
                top16(lists[0:1])
                if b >= 1:
                    staged(32 * b - 4, 28 * TOK4)
                top16(lists[1:8])
                if b >= 1:
                    staged(32 * b - 2, 30 * TOK4)
                top16(lists[8:])
                v.drain()
                v.tensor_copy(topf[:], topi[:])
                for h in range(PH):
                    tt(cand[:, h, :].rearrange("p (a c) -> p a c", a=TOPK),
                       top[:, 2 * h, :].unsqueeze(2).to_broadcast([P, TOPK, TOPK]),
                       top[:, 2 * h + 1, :].unsqueeze(1).to_broadcast([P, TOPK, TOPK]), ALU.add)
                v.drain()
                if b >= 1:
                    dve.wait_ge(s_gexp, b)
                top16([(best[:, h, :], pos[:, h * TOPK:(h + 1) * TOPK], cand[:, h, :]) for h in range(PH)])
                v.drain()
                v.tensor_copy(gsum[:, 0:PH], best[:, :, 0])
                if b >= 1:
                    dve.wait_ge(s_pkT, b)
                v.drain()
                tt(best[:], best[:], gsum[:, 0:PH].unsqueeze(2).to_broadcast([P, PH, TOPK]),
                   ALU.subtract).then_inc(s_best, 1)
                flat = match[:].rearrange("p h k a -> p (h k) a")
                for m, (op, arg) in enumerate([(ALU.logical_shift_right, 4), (ALU.bitwise_and, 15)]):
                    ts(posi[:], pos[:], arg, None, op)
                    v.drain()
                    v.tensor_copy(posf[:], posi[:])
                    v.drain()
                    tt(flat, posf[:].unsqueeze(2).to_broadcast([P, P, TOPK]),
                       iota16[:].unsqueeze(1).to_broadcast([P, P, TOPK]), ALU.is_equal)
                    v.drain()
                    half = topf[:].rearrange("p (h c) k -> p h c k", c=2)[:, :, m, :]
                    tt(match[:], match[:], half.unsqueeze(2).to_broadcast([P, PH, TOPK, TOPK]), ALU.mult)
                    v.drain()
                    v.tensor_reduce(pick[:, m, :], flat, AX_X, ALU.add)
                dve.wait_ge(s_gexp, b + 1)
                g3 = pick[:, 2, :].rearrange("p (h k) -> p h k", h=PH)
                v.tensor_reduce(gsum[:, PH:2 * PH], g3, AX_X, ALU.add)
                v.drain()
                v.reciprocal(gsum[:, PH:2 * PH], gsum[:, PH:2 * PH])
                v.drain()
                tt(g3, g3, gsum[:, PH:2 * PH].unsqueeze(2).to_broadcast([P, PH, TOPK]),
                   ALU.mult).then_inc(s_pick, 1)
                dve.wait_ge(s_pkT, b + 1)
                v.tensor_copy(pickT[:, 0:2, :], bank[7][:, 0:2 * P].rearrange("p (a n) -> p a n", a=2))
                v.tensor_copy(gTh[:], bank[7][:, 2 * P:3 * P])
                v.drain()
                tt(pickT[:, 3, :], bank[7][:, 2 * P:3 * P], gTh[:].bitcast(F32), ALU.subtract)
                v.tensor_copy(pickT[:, 2, :], gTh[:].bitcast(F32)).then_inc(s_pkc, 1)
                v.drain()

            def onehots(b):
                def one(i, r, free):
                    if free:
                        staged(i * OH + (32 * b + r - OH), i * (OH * TOK4) + (r - OH) * TOK4)

                    def spread(row, s):
                        tok = bass.ds(i * (OH * TOK4) + (r + s) * TOK4, TOK4)
                        return pickT[:, row, tok].unsqueeze(2).to_broadcast([P, TOK4, P])
                    lane = iotaN[:].unsqueeze(1).to_broadcast([P, TOK4, P])

                    def by_tok(ap):
                        return ap.rearrange("p (t n) -> p t n", t=TOK4)
                    for s in range(2):
                        tt(ohE(b, r + s), lane, spread(0, s), ALU.is_equal)
                    for s in range(2):
                        tt(by_tok(ohJ[:, r + s, :]), lane, spread(1, s), ALU.is_equal)
                    v.drain()
                    for s in range(2):
                        tt(ohI[:, (r + s) * TOK4:(r + s + 1) * TOK4, 0, :], ohE(b, r + s), spread(2, s),
                           ALU.mult).then_inc(s_oh, 1)
                v.drain()
                for r in range(0, OH, 2):
                    one(0, r, False)
                if b >= 1:
                    dve.wait_ge(s_gst, 16 * STORE * b)
                with dve.Fori(1, 32 // OH) as i:
                    for r in range(0, OH, 2):
                        one(i, r, True)

            dve.sem_inc(s_gev, RING)
            v.drain()
            for b in range(NB):
                retrieve(b)
                onehots(b)
            for q in (28, 30):
                staged(32 * (NB - 1) + q, q * TOK4)

            def up_tile(t, j, free):
                def low():
                    dve.wait_ge(s_chi, t + 1)
                    tt(clo[:, j % 2, :], coef[:, j % 2, :], chi[:, j % 2, :].bitcast(F32),
                       ALU.subtract).then_inc(s_clo, 1)
                dve.wait_ge(s_ain[j], (t - j) * 4 + 16)
                dve.wait_ge(s_gin[j], (t - j) * 4 + 16)
                tt(coef[:, j % 2, :], a_in[:, j, :], g_in[:, j, :], ALU.mult).then_inc(s_cf, 1)
                v.drain()
                low()

            for t in range(4):
                up_tile(t, t, t >= 2)
            with dve.Fori(1, N_TILES // 4) as i:
                for j in range(4):
                    up_tile(i * 4 + j, j, True)
            dve.wait_ge(s_yq, 1)
            v.tensor_reduce(rstd, ssq2.rearrange("p (b a) -> p b a", a=2), AX_X, ALU.add)
            v.drain()
            ts(rstd, rstd, 1.0 / D, EPS, ALU.mult, ALU.add).then_inc(s_ym, 1)
            dve.wait_ge(s_yr, 1)
            v.reciprocal(rstd, rstd)
            v.drain()
            dve.wait_ge(s_x1l, 16 * NB)
            for b in range(NB):
                for half in range(2):
                    w = slice(half * 512, (half + 1) * 512)
                    stt(out=yo[:, b, w], in0=bank[2 * b + half][:], scalar=rstd[:, b:b + 1],
                        in1=gate_f[:, w], op0=ALU.mult, op1=ALU.mult)
                v.drain()
                tt(yo[:, b, :], yo[:, b, :], x1[:, b, :], ALU.add).then_inc(s_yo, 1)


def kernel(**inputs):
    import numpy as np
    import concourse.bacc as bacc
    from concourse import mybir as mb
    from concourse.bass_utils import run_bass_kernel_spmd

    a = {k: np.asarray(v) for k, v in inputs.items()}
    w_mod = a["w_mod"][0].reshape(D, 6, KD, P).transpose(1, 2, 3, 0)
    b_mod = a["b_mod"][0].reshape(6, KD, P)

    def column_tiles(w):
        n = w.shape[1] // P
        return w.reshape(KD, P, n, P).transpose(2, 1, 0, 3).reshape(n, P, D)

    def natural_tiles(w):
        n = w.shape[1] // 512
        return w.reshape(4, 2, P, n, 512).transpose(3, 0, 2, 1, 4).reshape(4 * n, P, D)

    w_in = a["w_in"][0]
    A = 512
    qa, ka, va = w_in[:, 0:A], w_in[:, A:2 * A], w_in[:, 2 * A:3 * A]
    qkv, z = w_in[:, 3 * A:6 * A], w_in[:, 6 * A:7 * A]
    ba = w_in[:, 7 * A:7 * A + 2 * H]
    down = a["expert_down"][0].reshape(N_TILES, P, KD, P).transpose(0, 3, 2, 1).reshape(N_TILES, P, D)
    up = a["expert_up"][0].reshape(N_TILES, P, D)
    arrays = {
        "x": a["x"].reshape(NB, P, D),
        "c": a["c"].reshape(D),
        "mod_tiles": np.stack([w_mod[mod_order(m)] for m in range(N_MOD)]),
        "mod_bias_col": b_mod.transpose(2, 0, 1),
        "gain_cols": np.concatenate([a["pre_mix_gain"], a["pre_ffn_gain"], a["post_mix_gain"],
                                     a["post_ffn_gain"]]).reshape(4, KD, P).transpose(2, 0, 1),
        "in_tiles": np.concatenate([natural_tiles(va), natural_tiles(z),
                                    np.stack([column_tiles(ka), column_tiles(qa)], 1).reshape(8, P, D),
                                    column_tiles(qkv)]),
        "ba_w": ba.reshape(KD, P, 2 * H).transpose(1, 0, 2),
        "conv_col": a["conv_w"][0].reshape(4, 12, P).transpose(2, 1, 0).reshape(P, 48),
        "a_log": a["a_log"][0],
        "dt_bias": a["dt_bias"][0],
        "lambdas": np.concatenate([a[f"lambda_{n}"][0] for n in ("q1", "q2", "k1", "k2")]),
        "head_gain_cols": np.stack([a["attn_norm_gain"][0], a["gdn_norm_gain"][0]], 1),
        "out_tiles": natural_tiles(a["w_out"][0]),
        "query_tiles": column_tiles(a["w_query"][0]),
        "keys_t": a["sub_keys"][0].reshape(2 * PH, P, P).transpose(2, 0, 1),
        "expert_tiles": np.concatenate([down, up]),
    }
    nc = bacc.Bacc("TRN2", target_bir_lowering=False, num_devices=1)
    feed, args = {}, []
    for name, v in arrays.items():
        v = np.ascontiguousarray(v)
        feed[f"in_{name}"] = v
        args.append(nc.dram_tensor(f"in_{name}", v.shape, mb.dt.from_np(v.dtype), kind="ExternalInput").ap())
    out = nc.dram_tensor("out", (NB, P, D), mb.dt.from_np(np.dtype("float32")), kind="ExternalOutput").ap()
    build(nc, *args, out)
    r = run_bass_kernel_spmd(nc, [feed], core_ids=[0])
    return r.results[0]["out"].reshape(1, SEQ, D)
```
